# Optimizing a Trainium2 kernel written in Bass

```python
import jax, jax.numpy as jnp
from jax import lax
import numpy as np
import math

D_MODEL = 1024
BATCH = 1
SEQ = 256
DEPTH = 2

N_MIXERS = 2
HEAD_DIM = 64
N_HEADS = D_MODEL // HEAD_DIM
N_KV = 4
GQA = N_HEADS // N_KV
ROT_DIM = HEAD_DIM // 4
ROPE_THETA = 500000.0
NORM_EPS = 1e-6
Q_W = N_HEADS * HEAD_DIM
KV_W = N_KV * HEAD_DIM

CMP_LEN = 32
CMP_STRIDE = 16
CMP_HID = 4 * HEAD_DIM
SEL_BLOCK = 64
SEL_COUNT = 8
WINDOW = 256
NSA_Q_BLOCK = 32
NSA_IN = 2 * Q_W + 6 * KV_W + 3 * N_HEADS

MOBA_BLOCK = 256
MOBA_TOPK = 3
MOBA_Q_BLOCK = 8
MOBA_IN = 2 * Q_W + 2 * KV_W

N_A = (DEPTH + 1) // 2
N_B = DEPTH // 2


def rms_norm(x, g):
    xf = x.astype(jnp.float32)
    y = xf * lax.rsqrt(jnp.mean(xf * xf, axis=-1, keepdims=True) + NORM_EPS)
    return (y * g.astype(jnp.float32)).astype(x.dtype)

def rope_tables(pos):
    inv_freq = ROPE_THETA ** (-jnp.arange(0, ROT_DIM, 2, dtype=jnp.float32) / ROT_DIM)
    ang = pos.astype(jnp.float32)[..., None] * inv_freq
    return jnp.cos(ang), jnp.sin(ang)

def partial_rope(x, cos, sin):
    half = ROT_DIM // 2
    c = cos[:, :, None, :].astype(x.dtype)
    s = sin[:, :, None, :].astype(x.dtype)
    x1, x2, rest = x[..., :half], x[..., half:ROT_DIM], x[..., ROT_DIM:]
    return jnp.concatenate([x1 * c - x2 * s, x2 * c + x1 * s, rest], axis=-1)

def masked_softmax(s, mask):
    s = jnp.where(mask, s.astype(jnp.float32), -jnp.inf)
    m = jnp.max(s, axis=-1, keepdims=True)
    e = jnp.exp(s - jnp.where(jnp.isfinite(m), m, 0.0))
    return e / jnp.maximum(jnp.sum(e, axis=-1, keepdims=True), 1e-30)

def split_cols(a, widths):
    return jnp.split(a, np.cumsum(widths)[:-1].tolist(), axis=-1)

def cmp_to_sel_weights(n_cmp, n_sel):
    cs = np.arange(n_cmp)[:, None] * CMP_STRIDE
    ss = np.arange(n_sel)[None, :] * SEL_BLOCK
    shared = np.clip(np.minimum(cs + CMP_LEN, ss + SEL_BLOCK) - np.maximum(cs, ss), 0, None)
    return jnp.asarray(shared / CMP_LEN, dtype=jnp.float32)

def nsa_mixer(h, cos, sin, positions, w_in, w_out, q_g, k_g, cmp_pe, cmp_w1, cmp_b1, cmp_w2, gate_b):
    B, S, _ = h.shape
    q, kc, vc, ks, vs, kw, vw, gl, z = split_cols(h @ w_in, [Q_W] + [KV_W] * 6 + [3 * N_HEADS, Q_W])
    q = partial_rope(rms_norm(q.reshape(B, S, N_HEADS, HEAD_DIM), q_g), cos, sin)
    q = q.reshape(B, S, N_KV, GQA, HEAD_DIM)
    gates = jax.nn.sigmoid(gl + gate_b).reshape(B, S, N_KV, GQA, 3)
    scale = HEAD_DIM ** -0.5

    n_cmp = (S - CMP_LEN) // CMP_STRIDE + 1
    blk_idx = np.arange(n_cmp)[:, None] * CMP_STRIDE + np.arange(CMP_LEN)[None, :]
    cmp_end = blk_idx[:, -1]

    def compress(t, i):
        blocks = t.reshape(B, S, N_KV, HEAD_DIM)[:, blk_idx] + cmp_pe[i][None, None, :, None, :]
        flat = blocks.transpose(0, 1, 3, 2, 4).reshape(B, n_cmp, N_KV, CMP_LEN * HEAD_DIM)
        return jax.nn.gelu(flat @ cmp_w1[i] + cmp_b1[i]) @ cmp_w2[i]

    cos_c, sin_c = rope_tables(positions[:, cmp_end])
    k_cmp = partial_rope(rms_norm(compress(kc, 0), k_g[0]), cos_c, sin_c)
    v_cmp = compress(vc, 1)
    cmp_end_j = jnp.asarray(cmp_end, dtype=jnp.int32)

    n_sel = S // SEL_BLOCK
    k_sel = min(SEL_COUNT, n_sel)
    sel_w = cmp_to_sel_weights(n_cmp, n_sel)
    ks = partial_rope(rms_norm(ks.reshape(B, S, N_KV, HEAD_DIM), k_g[1]), cos, sin)
    ks_blk = ks.reshape(B, n_sel, SEL_BLOCK, N_KV, HEAD_DIM).transpose(0, 3, 1, 2, 4)
    vs_blk = vs.reshape(B, n_sel, SEL_BLOCK, N_KV, HEAD_DIM).transpose(0, 3, 1, 2, 4)

    pad = ((0, 0), (WINDOW, 0), (0, 0), (0, 0))
    kw_pad = jnp.pad(partial_rope(rms_norm(kw.reshape(B, S, N_KV, HEAD_DIM), k_g[2]), cos, sin), pad)
    vw_pad = jnp.pad(vw.reshape(B, S, N_KV, HEAD_DIM), pad)

    b_i = jnp.arange(B)[:, None, None, None]
    g_i = jnp.arange(N_KV)[None, None, :, None]
    sel_blocks = jnp.arange(n_sel)
    C = NSA_Q_BLOCK

    def q_block(ci):
        t0 = ci * C
        t = t0 + jnp.arange(C)
        qc = lax.dynamic_slice_in_dim(q, t0, C, axis=1)
        gc = lax.dynamic_slice_in_dim(gates, t0, C, axis=1)
        m_cmp = (cmp_end_j[None, :] <= t[:, None])[None, :, None, None, :]
        p_cmp = masked_softmax(jnp.einsum('bcgrd,bngd->bcgrn', qc, k_cmp) * scale, m_cmp)
        o_cmp = jnp.einsum('bcgrn,bngd->bcgrd', p_cmp.astype(v_cmp.dtype), v_cmp)
        imp = jnp.einsum('bcgrn,nj->bcgj', p_cmp, sel_w)
        cur = (t // SEL_BLOCK)[:, None]
        valid = sel_blocks[None, :] <= cur
        forced = (sel_blocks[None, :] == 0) | (sel_blocks[None, :] == cur) | (sel_blocks[None, :] == cur - 1)
        score = jnp.where(forced[None, :, None, :], jnp.inf,
                          jnp.where(valid[None, :, None, :], imp, -jnp.inf))
        _, sel = lax.top_k(score, k_sel)
        kg_sel = ks_blk[b_i, g_i, sel].reshape(B, C, N_KV, k_sel * SEL_BLOCK, HEAD_DIM)
        vg_sel = vs_blk[b_i, g_i, sel].reshape(B, C, N_KV, k_sel * SEL_BLOCK, HEAD_DIM)
        kpos = (sel[..., None] * SEL_BLOCK + jnp.arange(SEL_BLOCK)).reshape(B, C, N_KV, 1, k_sel * SEL_BLOCK)
        m_slc = kpos <= t[None, :, None, None, None]
        p_slc = masked_softmax(jnp.einsum('bcgrd,bcgnd->bcgrn', qc, kg_sel) * scale, m_slc)
        o_slc = jnp.einsum('bcgrn,bcgnd->bcgrd', p_slc.astype(vg_sel.dtype), vg_sel)
        kwc = lax.dynamic_slice_in_dim(kw_pad, t0, C + WINDOW, axis=1)
        vwc = lax.dynamic_slice_in_dim(vw_pad, t0, C + WINDOW, axis=1)
        kp = t0 - WINDOW + jnp.arange(C + WINDOW)
        dist = t[:, None] - kp[None, :]
        m_win = ((dist >= 0) & (dist < WINDOW) & (kp[None, :] >= 0))[None, :, None, None, :]
        p_win = masked_softmax(jnp.einsum('bcgrd,bkgd->bcgrk', qc, kwc) * scale, m_win)
        o_win = jnp.einsum('bcgrk,bkgd->bcgrd', p_win.astype(vwc.dtype), vwc)
        return gc[..., 0:1] * o_cmp + gc[..., 1:2] * o_slc + gc[..., 2:3] * o_win

    o = lax.map(q_block, jnp.arange(S // C))
    o = jnp.moveaxis(o, 0, 1).reshape(B, S, Q_W)
    return (o * jax.nn.silu(z)) @ w_out

def moba_mixer(h, cos, sin, w_in, w_out, q_g, k_g):
    B, S, _ = h.shape
    q, k, v, z = split_cols(h @ w_in, [Q_W, KV_W, KV_W, Q_W])
    q = partial_rope(rms_norm(q.reshape(B, S, N_HEADS, HEAD_DIM), q_g), cos, sin)
    q = q.reshape(B, S, N_KV, GQA, HEAD_DIM)
    k = partial_rope(rms_norm(k.reshape(B, S, N_KV, HEAD_DIM), k_g), cos, sin)
    v = v.reshape(B, S, N_KV, HEAD_DIM)
    scale = HEAD_DIM ** -0.5

    n_blk = -(-S // MOBA_BLOCK)
    pad = ((0, 0), (0, n_blk * MOBA_BLOCK - S), (0, 0), (0, 0))
    k_pad = jnp.pad(k, pad)
    v_pad = jnp.pad(v, pad)
    k_blk = k_pad.reshape(B, n_blk, MOBA_BLOCK, N_KV, HEAD_DIM)
    k_mean = jnp.mean(k_blk.astype(jnp.float32), axis=2).astype(k.dtype)
    k_blk_t = k_blk.transpose(0, 3, 1, 2, 4)
    v_blk_t = v_pad.reshape(B, n_blk, MOBA_BLOCK, N_KV, HEAD_DIM).transpose(0, 3, 1, 2, 4)
    k_top = min(MOBA_TOPK, n_blk - 1)
    b_i = jnp.arange(B)[:, None, None, None, None]
    g_i = jnp.arange(N_KV)[None, None, :, None, None]
    blk = jnp.arange(n_blk)
    C = MOBA_Q_BLOCK

    def q_block(ci):
        t0 = ci * C
        t = t0 + jnp.arange(C)
        qc = lax.dynamic_slice_in_dim(q, t0, C, axis=1)
        own = t0 // MOBA_BLOCK
        bstart = own * MOBA_BLOCK
        k_own = lax.dynamic_slice_in_dim(k_pad, bstart, MOBA_BLOCK, axis=1)
        v_own = lax.dynamic_slice_in_dim(v_pad, bstart, MOBA_BLOCK, axis=1)
        kpos = bstart + jnp.arange(MOBA_BLOCK)
        m_own = jnp.broadcast_to((kpos[None, :] <= t[:, None])[None, :, None, None, :],
                                 (B, C, N_KV, GQA, MOBA_BLOCK))
        s_own = jnp.einsum('bcgrd,bkgd->bcgrk', qc, k_own) * scale
        if k_top > 0:
            s_gate = jnp.einsum('bcgrd,bjgd->bcgrj', qc, k_mean).astype(jnp.float32)
            s_gate = jnp.where(blk < own, s_gate, -jnp.inf)
            _, sel = lax.top_k(s_gate, k_top)
            kg = k_blk_t[b_i, g_i, sel]
            vg = v_blk_t[b_i, g_i, sel].reshape(B, C, N_KV, GQA, k_top * MOBA_BLOCK, HEAD_DIM)
            s_past = jnp.einsum('bcgrd,bcgrkld->bcgrkl', qc, kg).reshape(B, C, N_KV, GQA, k_top * MOBA_BLOCK) * scale
            m_past = jnp.broadcast_to((sel < own)[..., None],
                                      (B, C, N_KV, GQA, k_top, MOBA_BLOCK)).reshape(B, C, N_KV, GQA, k_top * MOBA_BLOCK)
            p = masked_softmax(jnp.concatenate([s_past, s_own], axis=-1),
                               jnp.concatenate([m_past, m_own], axis=-1)).astype(v.dtype)
            n_past = k_top * MOBA_BLOCK
            return (jnp.einsum('bcgrn,bcgrnd->bcgrd', p[..., :n_past], vg)
                    + jnp.einsum('bcgrk,bkgd->bcgrd', p[..., n_past:], v_own))
        p = masked_softmax(s_own, m_own).astype(v.dtype)
        return jnp.einsum('bcgrk,bkgd->bcgrd', p, v_own)

    o = lax.map(q_block, jnp.arange(S // C))
    o = jnp.moveaxis(o, 0, 1).reshape(B, S, Q_W)
    return (o * jax.nn.silu(z)) @ w_out

def first_inputs(seed: int = 0) -> dict:
    key = jax.random.key(seed)
    ks = jax.random.split(key, 20)
    D = D_MODEL

    def nrm(k, shape, s):
        return jax.random.normal(k, shape, jnp.float32) * s

    x = nrm(ks[0], (BATCH, SEQ, D), 1.0)
    c = nrm(ks[1], (BATCH, D), 1.0)
    offset = jax.random.randint(ks[2], (BATCH, 1), 0, 4096, dtype=jnp.int32)
    positions = offset + jnp.arange(SEQ, dtype=jnp.int32)[None, :]
    return {
        "x": x,
        "c": c,
        "positions": positions,
        "norm_g": 1.0 + nrm(ks[3], (DEPTH, D), 0.02),
        "ada_w": nrm(ks[4], (DEPTH, D, 3 * D), 0.5 * D ** -0.5),
        "ada_b": nrm(ks[5], (DEPTH, 3 * D), 0.02),
        "nsa_w_in": nrm(ks[6], (N_A, D, NSA_IN), D ** -0.5),
        "nsa_w_out": nrm(ks[7], (N_A, Q_W, D), Q_W ** -0.5),
        "nsa_q_norm": 1.0 + nrm(ks[8], (N_A, HEAD_DIM), 0.02),
        "nsa_k_norm": 1.0 + nrm(ks[9], (N_A, 3, HEAD_DIM), 0.02),
        "nsa_cmp_pe": nrm(ks[10], (N_A, 2, CMP_LEN, HEAD_DIM), 0.1),
        "nsa_cmp_w1": nrm(ks[11], (N_A, 2, CMP_LEN * HEAD_DIM, CMP_HID), (CMP_LEN * HEAD_DIM) ** -0.5),
        "nsa_cmp_b1": nrm(ks[12], (N_A, 2, CMP_HID), 0.02),
        "nsa_cmp_w2": nrm(ks[13], (N_A, 2, CMP_HID, HEAD_DIM), CMP_HID ** -0.5),
        "nsa_gate_b": nrm(ks[14], (N_A, 3 * N_HEADS), 0.1),
        "moba_w_in": nrm(ks[15], (N_B, D, MOBA_IN), D ** -0.5),
        "moba_w_out": nrm(ks[16], (N_B, Q_W, D), Q_W ** -0.5),
        "moba_q_norm": 1.0 + nrm(ks[17], (N_B, HEAD_DIM), 0.02),
        "moba_k_norm": 1.0 + nrm(ks[18], (N_B, HEAD_DIM), 0.02),
    }

def first_block(x, c, positions, norm_g, ada_w, ada_b, nsa_w_in, nsa_w_out, nsa_q_norm, nsa_k_norm,
              nsa_cmp_pe, nsa_cmp_w1, nsa_cmp_b1, nsa_cmp_w2, nsa_gate_b,
              moba_w_in, moba_w_out, moba_q_norm, moba_k_norm):
    cos, sin = rope_tables(positions)
    cond = jax.nn.silu(c)
    for i in range(DEPTH):
        shift, scale, gate = jnp.split(cond @ ada_w[i] + ada_b[i], 3, axis=-1)
        h = rms_norm(x, norm_g[i]) * (1 + scale[:, None, :]) + shift[:, None, :]
        j = i // N_MIXERS
        if i % N_MIXERS == 0:
            y = nsa_mixer(h, cos, sin, positions, nsa_w_in[j], nsa_w_out[j], nsa_q_norm[j], nsa_k_norm[j],
                          nsa_cmp_pe[j], nsa_cmp_w1[j], nsa_cmp_b1[j], nsa_cmp_w2[j], nsa_gate_b[j])
        else:
            y = moba_mixer(h, cos, sin, moba_w_in[j], moba_w_out[j], moba_q_norm[j], moba_k_norm[j])
        x = x + gate[:, None, :] * y
    return x


DEPTH_2 = 1

N_HEADS_A = 8
N_KV_A = 2
GROUP_A = N_HEADS_A // N_KV_A
N_HEADS_B = 8
WINDOW_2 = 128
WIN_BLOCK = 128
T5_BUCKETS = 32
T5_MAX_DIST = 128
GRID_W = 64
NA_ROWS = 8
NA_COLS = 16
PEER_HEADS = 8
PEER_KEYS = 128
N_EXPERTS = PEER_KEYS * PEER_KEYS
PEER_QDIM = 256
PEER_HALF = PEER_QDIM // 2
PEER_TOPK = 16
PEER_CHUNK = 128
EPS = 1e-6
NEG = -1e30

W_QA = N_HEADS_A * HEAD_DIM
W_KVA = N_KV_A * HEAD_DIM
W_B = N_HEADS_B * HEAD_DIM
D_MIX = W_QA + W_B
D_IN = W_QA + 2 * W_KVA + 3 * W_B
IN_SPLITS = [W_QA, W_QA + W_KVA, W_QA + 2 * W_KVA, W_QA + 2 * W_KVA + W_B, W_QA + 2 * W_KVA + 2 * W_B]


def rms_norm_2(x, g):
    xf = x.astype(jnp.float32)
    y = xf * lax.rsqrt(jnp.mean(xf * xf, axis=-1, keepdims=True) + EPS)
    return (y * g.astype(jnp.float32)).astype(x.dtype)

def modulate(h, shift, scale):
    return h * (1.0 + scale[:, None, :]) + shift[:, None, :]

def t5_bucket(rel):
    half = T5_BUCKETS // 2
    max_exact = half // 2
    ret = jnp.where(rel > 0, half, 0)
    n = jnp.abs(rel)
    nf = jnp.maximum(n, 1).astype(jnp.float32)
    large = max_exact + (jnp.log(nf / max_exact) / math.log(T5_MAX_DIST / max_exact)
                         * (half - max_exact)).astype(jnp.int32)
    large = jnp.minimum(large, half - 1)
    return ret + jnp.where(n < max_exact, n, large)

def windowed_gqa(q, k, v, sink, t5_table):
    B, S = q.shape[0], q.shape[1]
    nb = S // WIN_BLOCK
    span = WIN_BLOCK + 2 * WINDOW_2
    pad = ((0, 0), (WINDOW_2, WINDOW_2), (0, 0), (0, 0))
    k_pad = jnp.pad(k, pad)
    v_pad = jnp.pad(v, pad)
    i = jnp.arange(WIN_BLOCK)[:, None]
    j = jnp.arange(span)[None, :]
    rel = j - WINDOW_2 - i
    band = jnp.abs(rel) <= WINDOW_2
    bias = t5_table[t5_bucket(rel)].transpose(2, 0, 1).astype(jnp.float32)
    scale = HEAD_DIM ** -0.5
    sink_f = sink.astype(jnp.float32)

    def block(b):
        qb = lax.dynamic_slice_in_dim(q, b * WIN_BLOCK, WIN_BLOCK, axis=1)
        qb = qb.reshape(B, WIN_BLOCK, N_KV_A, GROUP_A, HEAD_DIM)
        kb = lax.dynamic_slice_in_dim(k_pad, b * WIN_BLOCK, span, axis=1)
        vb = lax.dynamic_slice_in_dim(v_pad, b * WIN_BLOCK, span, axis=1)
        s = jnp.einsum('bqgrd,bkgd->bgrqk', qb, kb).astype(jnp.float32)
        s = s.reshape(B, N_HEADS_A, WIN_BLOCK, span) * scale + bias
        kpos = b * WIN_BLOCK - WINDOW_2 + jnp.arange(span)
        valid = band & ((kpos >= 0) & (kpos < S))[None, :]
        s = jnp.where(valid, s, NEG)
        sink_col = jnp.broadcast_to(sink_f[None, :, None, None], (B, N_HEADS_A, WIN_BLOCK, 1))
        p = jax.nn.softmax(jnp.concatenate([s, sink_col], axis=-1), axis=-1)[..., :span]
        p = p.astype(v.dtype).reshape(B, N_KV_A, GROUP_A, WIN_BLOCK, span)
        o = jnp.einsum('bgrqk,bkgd->bqgrd', p, vb)
        return o.reshape(B, WIN_BLOCK, N_HEADS_A * HEAD_DIM)

    out = lax.map(block, jnp.arange(nb))
    return out.transpose(1, 0, 2, 3).reshape(B, S, N_HEADS_A * HEAD_DIM)

def neighbourhood_attention(q, k, v, rpb):
    B, S = q.shape[0], q.shape[1]
    rows = S // GRID_W
    kr = min(NA_ROWS, rows)
    q_g = q.reshape(B, rows, GRID_W, N_HEADS_B, HEAD_DIM)
    k_g = k.reshape(B, rows, GRID_W, N_HEADS_B, HEAD_DIM)
    v_g = v.reshape(B, rows, GRID_W, N_HEADS_B, HEAD_DIM)
    cols = jnp.arange(GRID_W)
    col_start = jnp.clip(cols - NA_COLS // 2, 0, GRID_W - NA_COLS)
    col_idx = col_start[:, None] + jnp.arange(NA_COLS)[None, :]
    col_off = col_idx - cols[:, None] + (NA_COLS - 1)
    scale = HEAD_DIM ** -0.5
    rpb_f = rpb.astype(jnp.float32)

    def row_block(r):
        rs = jnp.clip(r - kr // 2, 0, rows - kr)
        q_r = lax.dynamic_index_in_dim(q_g, r, axis=1, keepdims=False)
        k_band = lax.dynamic_slice_in_dim(k_g, rs, kr, axis=1)
        v_band = lax.dynamic_slice_in_dim(v_g, rs, kr, axis=1)
        k_win = k_band[:, :, col_idx]
        v_win = v_band[:, :, col_idx]
        s = jnp.einsum('bchd,bkcwhd->bhckw', q_r, k_win).astype(jnp.float32) * scale
        row_off = rs + jnp.arange(kr) - r + (NA_ROWS - 1)
        bias = rpb_f[:, row_off[None, :, None], col_off[:, None, :]]
        s = (s + bias[None]).reshape(B, N_HEADS_B, GRID_W, kr * NA_COLS)
        p = jax.nn.softmax(s, axis=-1).reshape(B, N_HEADS_B, GRID_W, kr, NA_COLS).astype(v.dtype)
        return jnp.einsum('bhckw,bkcwhd->bchd', p, v_win)

    out = lax.map(row_block, jnp.arange(rows))
    return out.transpose(1, 0, 2, 3, 4).reshape(B, S, N_HEADS_B * HEAD_DIM)

def peer(h, w_query, sub_keys, u_experts, v_experts):
    B, S, D = h.shape
    tokens = h.reshape(B * S // PEER_CHUNK, PEER_CHUNK, D)

    def chunk(xc):
        qh = (xc @ w_query).reshape(PEER_CHUNK, PEER_HEADS, PEER_QDIM)
        s1 = jnp.einsum('thd,hnd->thn', qh[..., :PEER_HALF], sub_keys[:, 0]).astype(jnp.float32)
        s2 = jnp.einsum('thd,hnd->thn', qh[..., PEER_HALF:], sub_keys[:, 1]).astype(jnp.float32)
        v1, i1 = lax.top_k(s1, PEER_TOPK)
        v2, i2 = lax.top_k(s2, PEER_TOPK)
        cand = (v1[..., :, None] + v2[..., None, :]).reshape(PEER_CHUNK, PEER_HEADS, PEER_TOPK * PEER_TOPK)
        vs, ci = lax.top_k(cand, PEER_TOPK)
        e1 = jnp.take_along_axis(i1, ci // PEER_TOPK, axis=-1)
        e2 = jnp.take_along_axis(i2, ci % PEER_TOPK, axis=-1)
        idx = e1 * PEER_KEYS + e2
        g = jax.nn.softmax(vs, axis=-1)
        u_sel = u_experts[idx]
        v_sel = v_experts[idx]
        z = jnp.einsum('td,thkd->thk', xc, u_sel)
        a = (jax.nn.gelu(z.astype(jnp.float32)) * g).astype(xc.dtype)
        return jnp.einsum('thk,thkd->td', a, v_sel)

    out = lax.map(chunk, tokens)
    return out.reshape(B, S, D)

def second_inputs(seed: int = 0) -> dict:
    key = jax.random.key(seed)
    ks = jax.random.split(key, 20)
    f32 = jnp.float32
    D = D_MODEL
    nrm = lambda k, shape, s: jax.random.normal(k, shape, f32) * s
    return {
        "x": nrm(ks[0], (BATCH, SEQ, D), 1.0),
        "c": nrm(ks[1], (BATCH, D), 1.0),
        "w_ada": nrm(ks[2], (DEPTH_2, D, 6 * D), 0.5 * D ** -0.5),
        "b_ada": nrm(ks[3], (DEPTH_2, 6 * D), 0.02),
        "norm1_g": 1.0 + nrm(ks[4], (DEPTH_2, D), 0.02),
        "w_in": nrm(ks[5], (DEPTH_2, D, D_IN), D ** -0.5),
        "sink_a": nrm(ks[6], (DEPTH_2, N_HEADS_A), 0.5),
        "t5_table": nrm(ks[7], (T5_BUCKETS, N_HEADS_A), 0.3),
        "rpb_b": nrm(ks[8], (DEPTH_2, N_HEADS_B, 2 * NA_ROWS - 1, 2 * NA_COLS - 1), 0.3),
        "out_norm_a": 1.0 + nrm(ks[9], (DEPTH_2, W_QA), 0.02),
        "out_norm_b": 1.0 + nrm(ks[10], (DEPTH_2, W_B), 0.02),
        "w_out": nrm(ks[11], (DEPTH_2, D_MIX, D), D_MIX ** -0.5),
        "norm2_g": 1.0 + nrm(ks[12], (DEPTH_2, D), 0.02),
        "w_query": nrm(ks[13], (DEPTH_2, D, PEER_HEADS * PEER_QDIM), D ** -0.5),
        "sub_keys": nrm(ks[14], (DEPTH_2, PEER_HEADS, 2, PEER_KEYS, PEER_HALF), PEER_HALF ** -0.5),
        "u_experts": nrm(ks[15], (DEPTH_2, N_EXPERTS, D), D ** -0.5),
        "v_experts": nrm(ks[16], (DEPTH_2, N_EXPERTS, D), 1.0),
        "final_g": 1.0 + nrm(ks[17], (D,), 0.02),
    }

def second_block(x, c, w_ada, b_ada, norm1_g, w_in, sink_a, t5_table, rpb_b, out_norm_a, out_norm_b,
              w_out, norm2_g, w_query, sub_keys, u_experts, v_experts, final_g):
    B, S, D = x.shape
    c_act = jax.nn.silu(c)
    for layer in range(DEPTH_2):
        ada = c_act @ w_ada[layer] + b_ada[layer]
        shift1, scale1, gate1, shift2, scale2, gate2 = jnp.split(ada, 6, axis=-1)

        h = modulate(rms_norm_2(x, norm1_g[layer]), shift1, scale1)
        proj = h @ w_in[layer]
        qa, ka, va, qb, kb, vb = jnp.split(proj, IN_SPLITS, axis=-1)
        o_a = windowed_gqa(qa.reshape(B, S, N_HEADS_A, HEAD_DIM),
                           ka.reshape(B, S, N_KV_A, HEAD_DIM),
                           va.reshape(B, S, N_KV_A, HEAD_DIM),
                           sink_a[layer], t5_table)
        o_b = neighbourhood_attention(qb.reshape(B, S, N_HEADS_B, HEAD_DIM),
                                      kb.reshape(B, S, N_HEADS_B, HEAD_DIM),
                                      vb.reshape(B, S, N_HEADS_B, HEAD_DIM),
                                      rpb_b[layer])
        mixed = jnp.concatenate([rms_norm_2(o_a, out_norm_a[layer]),
                                 rms_norm_2(o_b, out_norm_b[layer])], axis=-1)
        x = x + gate1[:, None, :] * (mixed @ w_out[layer])

        h2 = modulate(rms_norm_2(x, norm2_g[layer]), shift2, scale2)
        x = x + gate2[:, None, :] * peer(h2, w_query[layer], sub_keys[layer],
                                          u_experts[layer], v_experts[layer])
    return rms_norm_2(x, final_g)


def setup_inputs(seed=0):
    out = dict(first_inputs(seed))
    for name, value in second_inputs(seed + 1).items():
        if name != "x":
            out[name + "_2"] = value
    return out


def reference(
    x, c, positions, norm_g, ada_w, ada_b, nsa_w_in, nsa_w_out, nsa_q_norm, nsa_k_norm,
    nsa_cmp_pe, nsa_cmp_w1, nsa_cmp_b1, nsa_cmp_w2, nsa_gate_b, moba_w_in, moba_w_out,
    moba_q_norm, moba_k_norm, c_2, w_ada_2, b_ada_2, norm1_g_2, w_in_2, sink_a_2, t5_table_2,
    rpb_b_2, out_norm_a_2, out_norm_b_2, w_out_2, norm2_g_2, w_query_2, sub_keys_2, u_experts_2,
    v_experts_2, final_g_2,
):
    x = first_block(
        x, c, positions, norm_g, ada_w, ada_b, nsa_w_in, nsa_w_out, nsa_q_norm, nsa_k_norm,
        nsa_cmp_pe, nsa_cmp_w1, nsa_cmp_b1, nsa_cmp_w2, nsa_gate_b, moba_w_in, moba_w_out,
        moba_q_norm, moba_k_norm,
    )
    return second_block(
        x, c_2, w_ada_2, b_ada_2, norm1_g_2, w_in_2, sink_a_2, t5_table_2, rpb_b_2,
        out_norm_a_2, out_norm_b_2, w_out_2, norm2_g_2, w_query_2, sub_keys_2, u_experts_2,
        v_experts_2, final_g_2,
    )


_drawn_inputs = setup_inputs


def setup_inputs(seed=0):
    import zlib

    import numpy as np

    out = dict(_drawn_inputs(seed))
    spreads = {}
    factors = {'norm_g': 6.432,
     'ada_b': 2.982,
     'nsa_q_norm': 8.0,
     'nsa_k_norm': 8.0,
     'nsa_cmp_pe': 3.628,
     'nsa_cmp_b1': 8.0,
     'nsa_gate_b': 5.795,
     'moba_q_norm': 8.0,
     'moba_k_norm': 8.0,
     'norm1_g_2': 21.429,
     'sink_a_2': 8.0,
     'out_norm_a_2': 44.288,
     'out_norm_b_2': 36.448,
     'final_g_2': 8.618,
     'b_ada_2': 4.033,
     't5_table_2': 8.0,
     'rpb_b_2': 8.0,
     'norm2_g_2': 8.0,
     'w_query_2': 4.751,
     'sub_keys_2': 4.713,
     'u_experts_2': 5.243,
     'v_experts_2': 4.731}
    for name, (base, spread) in spreads.items():
        noise = np.random.default_rng([zlib.crc32(name.encode()), seed]).standard_normal(out[name].shape)
        drawn = base * np.exp(spread * noise) if base else spread * noise
        out[name] = __import__('jax').numpy.asarray(drawn.astype(out[name].dtype))
    for name, factor in factors.items():
        out[name] = (out[name] * factor).astype(out[name].dtype)
    return out
```

```python
from contextlib import ExitStack

import numpy as np
import concourse.bass as bass
from concourse import mybir

F32 = mybir.dt.float32
I32 = mybir.dt.int32
U32 = mybir.dt.uint32
ALU = mybir.AluOpType
ACT = mybir.ActivationFunctionType
AX = mybir.AxisListType.X

P = 128
S = 256
NT = S // P
D = 1024
DC = D // P
HD = 64
NH = 16
NKV = 4
GQA = NH // NKV
ROT = HD // 4
HALF = ROT // 2
THETA = 500000.0
EPS = 1e-6
CMP_LEN, CMP_STRIDE = 32, 16
NCMP = (S - CMP_LEN) // CMP_STRIDE + 1
CPAD = 32
CMP_HID = 4 * HD
NPAIR = CMP_LEN * HD // P
NEG = -1e30
FLOOR = -1e29
WT = 512
RING = 3
HA, HB = 8, 8
KVA = 2
PH, PK, PTOP = 8, 128, 16
BLK = 4

COLS = [("c", 8), ("c_2", 8), ("norm_g", 16), ("ada_b", 48), ("b_ada_2", 48), ("norm1_g_2", 8), ("norm2_g_2", 8),
        ("out_norm_a_2", 4), ("out_norm_b_2", 4), ("nsa_cmp_b1", 4)]
ROWS = [("nsa_q_norm", HD), ("nsa_k_norm", 3 * HD), ("moba_q_norm", HD), ("moba_k_norm", HD), ("nsa_gate_b", 3 * NH),
        ("sink_a_2", HA), ("final_g_2", D)]


def offsets(table):
    at, out = 0, {}
    for name, n in table:
        out[name] = (at, at + n)
        at += n
    return out, at


COL_AT, NCOL = offsets(COLS)
ROW_AT, NROW = offsets(ROWS)


class Line:

    def __init__(self, nc, stack, eng, name):
        self.eng, self.sem, self.count, self.seen = eng, stack.enter_context(nc.semaphore(name)), 0, {}
        self.name = name

    def need(self, *marks):
        for m in marks:
            if m is not None and self.seen.get(m[0].name, 0) < m[1]:
                self.eng.wait_ge(m[0], m[1])
                self.seen[m[0].name] = m[1]

    def did(self, inst):
        self.count += 1
        inst.then_inc(self.sem, 1)
        return (self.sem, self.count)

    def last(self):
        return (self.sem, self.count) if self.count else None


class Load:

    def __init__(self, nc, stack, name):
        self.sem, self.n = stack.enter_context(nc.semaphore(name)), 0

    def did(self, inst):
        self.n += 16
        inst.then_inc(self.sem, 16)
        return (self.sem, self.n)


class Bank:

    def __init__(self, tensor):
        self.t, self.free = tensor, None


def program(nc, a, dbg):
    with ExitStack() as st:
        build(nc, st, a, dbg)


def build(nc, st, a, dbg):
    V, A, G, T, Y = (Line(nc, st, e, n) for e, n in (
        (nc.vector, "vec"), (nc.scalar, "act"), (nc.gpsimd, "pool"), (nc.tensor, "pe"), (nc.sync, "sp")))
    ve, ac, po, pe, sy = nc.vector, nc.scalar, nc.gpsimd, nc.tensor, nc.sync

    scope = [st]

    def sb(name, shape, dt=F32, stack=None):
        return (stack or scope[0]).enter_context(nc.sbuf_tensor(name, shape, dt))

    stores = []

    def load(dst, src, name, eng=None):
        return Load(nc, st, name).did((eng or sy).dma_start(dst, src))

    def meet():
        marks = [e.last() for e in (V, A, G, T)]
        for e in (V, A, G, T, Y):
            e.need(*[m for m in marks if m is not None])

    banks = [Bank(st.enter_context(nc.psum_tensor(f"bank{i}", [P, 512], F32))) for i in range(8)]
    turn = {"proj": 0}

    def proj_bank():
        b = banks[turn["proj"] % 2]
        turn["proj"] += 1
        return b

    x = sb("x_tok", [P, NT, D])
    hT = sb("hT", [P, DC, S])
    ident = sb("ident", [P, P])
    cols = sb("cols", [P, NCOL])
    rows = sb("rows", [P, NROW])
    causal = sb("causal", [P, S])
    cmp_mask = sb("cmp_mask", [P, NT, CPAD])
    iota_k = sb("iota_k", [P, P])
    pos_i = sb("pos_i", [P, NT + 1], I32)
    cosd = sb("cosd", [P, NT + 1, ROT])
    sind = sb("sind", [P, NT + 1, ROT])
    silu_c = sb("silu_c", [P, 2, DC])
    ada = [sb("ada0", [P, 24]), sb("ada1", [P, 24]), sb("ada2", [P, 48])]
    gate_row = sb("gate_row", [P, D])
    mod_a = sb("mod_a", [P, DC])
    stat = sb("stat", [P, 8])
    pow_half = sb("pow_half", [P, NH])
    hkT = sb("hkT", [P, 3, S])
    ring = [sb(f"w_ring{i}", [P, DC * WT]) for i in range(2)]
    layers = ExitStack()
    st.callback(layers.close)
    scope[0] = layers
    ring += [sb(f"w_ring{i}", [P, DC * WT], F32, layers) for i in range(2, RING)]

    def col(name, lo=0, hi=None):
        s, e = COL_AT[name]
        return cols[:, s + lo:(e if hi is None else s + hi)]

    def row(name, lo=0, hi=None):
        s, e = ROW_AT[name]
        return rows[:, s + lo:(e if hi is None else s + hi)]

    m_cols = load(cols[:], a["cols"], "ld_cols")
    m_pos = load(pos_i[:], a["pos"], "ld_pos", ac)
    m_x = load(x[:], a["x"].rearrange("(t p) d -> p t d", p=P), "ld_x", ac)
    m_rows = load(rows[:], a["rows"].broadcast_to([P, NROW]), "ld_rows", ac)

    slot_load = [Load(nc, st, f"ld_ring{i}") for i in range(RING)]
    slot_free = [None] * RING
    streamed = [0]

    def stream(src, chunks, width):
        i = streamed[0] % RING
        streamed[0] += 1
        Y.need(slot_free[i])
        tile = ring[i][:, 0:chunks * width].rearrange("p (c n) -> p c n", c=chunks)
        return tile, slot_load[i].did(sy.dma_start(tile, src.rearrange("(c p) n -> p c n", p=P))), i

    m_z = G.did(po.memset(ident[:], 0.0))
    G.need(m_z)
    m_ident = G.did(po.affine_select(out=ident[:], in_=ident[:], compare_op=ALU.not_equal, fill=1.0, base=0,
                                     pattern=[[-1, P]], channel_multiplier=1))
    m_z = G.did(po.memset(causal[:], 0.0))
    m_p = G.did(po.memset(pow_half[:], -0.5))
    m_c0 = G.did(po.memset(cmp_mask[:], 0.0))
    G.need(m_z)
    m_causal = G.did(po.affine_select(out=causal[:, P:S], in_=causal[:, P:S], compare_op=ALU.is_ge, fill=NEG, base=0,
                                      pattern=[[-1, P]], channel_multiplier=1))
    G.need(m_c0)
    for t in range(NT):
        m = G.did(po.affine_select(out=cmp_mask[:, t, :], in_=cmp_mask[:, t, :], compare_op=ALU.is_ge, fill=NEG,
                                   base=t * P - (CMP_LEN - 1), pattern=[[-CMP_STRIDE, CPAD]], channel_multiplier=1))
    G.need(m)
    m_cmask = G.did(po.memset(cmp_mask[:, :, NCMP:CPAD], NEG))
    m_iota = G.did(po.iota(iota_k[:], [[1, P]], base=0, channel_multiplier=0, allow_small_or_imprecise_dtypes=True))
    m_pow = m_p

    freq = sb("freq", [P, HALF])
    ang = sb("ang", [P, 4, NT + 1, HALF])
    posf = sb("posf", [P, NT + 1])
    for j in range(HALF):
        m_f = G.did(po.memset(freq[:, j:j + 1], float(np.float32(THETA) ** np.float32(-2.0 * j / ROT))))
    V.need(m_pos)
    m = V.did(ve.tensor_copy(posf[:], pos_i[:]))
    V.need(m, m_f)
    for t in range(NT + 1):
        m = V.did(ve.tensor_scalar(ang[:, 0, t, :], freq[:], posf[:, t:t + 1], None, ALU.mult))
    two_pi = 2.0 * np.pi
    parts, rest = [], two_pi
    for bits in (8, 8, 8):
        e = np.floor(np.log2(rest)) + 1 - bits
        p = np.floor(rest / 2.0 ** e) * 2.0 ** e
        parts.append(float(p))
        rest -= p
    parts.append(float(np.float32(rest)))
    magic = float(1.5 * 2 ** 23)
    V.need(m)
    m = V.did(ve.tensor_scalar(ang[:, 1], ang[:, 0], float(1.0 / two_pi), magic, ALU.mult, ALU.add))
    V.need(m)
    m = V.did(ve.tensor_scalar(ang[:, 1], ang[:, 1], -magic, None, ALU.add))
    for p in parts:
        V.need(m)
        m = V.did(ve.scalar_tensor_tensor(out=ang[:, 0], in0=ang[:, 1], scalar=-p, in1=ang[:, 0], op0=ALU.mult,
                                          op1=ALU.add))
    V.need(m)
    pi32 = 3.1415925
    m = V.did(ve.tensor_scalar(ang[:, 0], ang[:, 0], pi32, -pi32, ALU.min, ALU.max))
    V.need(m)
    m = V.did(ve.scalar_tensor_tensor(out=ang[:, 2], in0=ang[:, 0], scalar=-1.0, in1=ang[:, 0], op0=ALU.mult,
                                      op1=ALU.min))
    V.need(m)
    m_r = V.did(ve.tensor_scalar(ang[:, 2], ang[:, 2], float(np.pi / 2), None, ALU.add))
    A.need(m_r)
    m_cos = A.did(ac.activation(ang[:, 3], ang[:, 2], ACT.Sin))
    m_sin = A.did(ac.activation(sind[:, :, HALF:ROT], ang[:, 0], ACT.Sin))
    V.need(m_cos, m_sin)
    V.did(ve.tensor_copy(cosd[:, :, 0:HALF], ang[:, 3]))
    V.did(ve.tensor_copy(cosd[:, :, HALF:ROT], ang[:, 3]))
    m_rope = V.did(ve.tensor_scalar(sind[:, :, 0:HALF], sind[:, :, HALF:ROT], -1.0, None, ALU.mult))

    A.need(m_cols)
    A.did(ac.activation(silu_c[:, 0, :], col("c"), ACT.Silu))
    m_silu = A.did(ac.activation(silu_c[:, 1, :], col("c_2"), ACT.Silu))

    def ada_tile(layer, j):
        src = a["ada_w"][layer] if layer < 2 else a["w_ada_2"]
        w, m_w, slot = stream(src[:, j * WT:(j + 1) * WT], DC, WT)
        b = proj_bank()
        T.need(b.free, m_w, m_silu)
        for i in range(4):
            for c in range(DC):
                last = pe.matmul(b.t[:, i:i + 1], w[:, c, i * P:(i + 1) * P], silu_c[:, layer // 2, c:c + 1],
                                 start=c == 0, stop=c == DC - 1)
        m = T.did(last)
        slot_free[slot] = m
        bias = col("ada_b", 24 * layer, 24 * layer + 24) if layer < 2 else col("b_ada_2")
        V.need(m, m_cols)
        b.free = V.did(ve.tensor_tensor(ada[layer][:, 4 * j:4 * j + 4], b.t[:, 0:4], bias[:, 4 * j:4 * j + 4], ALU.add))
        return b.free

    fillers = [(l, j) for l, n in ((1, 6), (2, 12)) for j in range(n)]
    ada_mark = {}

    def filler(n=1):
        for _ in range(n):
            if fillers:
                l, j = fillers.pop(0)
                ada_mark[l] = ada_tile(l, j)

    for j in range(6):
        ada_mark[0] = ada_tile(0, j)

    def spread_gate(layer, first, stack):
        wide = sb(f"gate_wide{layer}_{first}", [P, P], F32, stack)
        for half in range(2):
            b = proj_bank()
            for i in range(4):
                c = 4 * half + i
                V.need(ada_mark[layer], T.last())
                m = V.did(ve.tensor_copy(wide[:], ada[layer][:, first + c:first + c + 1].broadcast_to([P, P])))
                T.need(m, b.free, m_ident)
                m = T.did(pe.matmul(b.t[:, i * P:(i + 1) * P], wide[:], ident[:], start=True, stop=True))
            V.need(m)
            b.free = V.did(ve.tensor_copy(gate_row[:, half * 512:(half + 1) * 512], b.t[:]))
        return b.free

    def row_rstd(dst, src, width, marks, scratch):
        V.need(*marks)
        m = V.did(ve.tensor_tensor_reduce(out=scratch, in0=src, in1=src, scale=1.0, scalar=0.0, op0=ALU.mult,
                                          op1=ALU.add, accum_out=dst))
        V.need(m)
        m = V.did(ve.tensor_scalar(dst, dst, 1.0 / width, EPS, ALU.mult, ALU.add))
        G.need(m, m_pow)
        return G.did(po.tensor_tensor(dst, dst, pow_half[:, 0:1], ALU.pow))

    def to_columns(src, marks, put):
        for half in range(2):
            b = proj_bank()
            T.need(b.free, m_ident, *marks)
            for i in range(4):
                c = 4 * half + i
                last = pe.transpose(b.t[:, i * P:(i + 1) * P], src[:, c * P:(c + 1) * P], ident[:])
            m = T.did(last)
            b.free = put(half, b.t, m)

    def modulated(layer, norm, shift, scale, stack, m_in):
        xn = sb(f"xn{layer}_{shift}", [P, D], F32, stack)
        V.need(ada_mark[layer])
        m_mod = V.did(ve.scalar_tensor_tensor(out=mod_a[:], in0=ada[layer][:, scale:scale + DC], scalar=1.0, in1=norm,
                                              op0=ALU.add, op1=ALU.mult))
        m_h = None
        for t in range(NT):
            V.need(T.last())
            m = row_rstd(stat[:, t:t + 1], x[:, t, :], D, m_in, xn[:])
            V.need(m)
            m = V.did(ve.tensor_scalar(xn[:], x[:, t, :], stat[:, t:t + 1], None, ALU.mult))

            def put(half, bank, m_t):
                V.need(m_t, m_mod)
                A.need(m_t, m_mod)
                for i in range(4):
                    c = 4 * half + i
                    dst = hT[:, c, t * P:(t + 1) * P]
                    m = V.did(ve.tensor_scalar(dst, bank[:, i * P:(i + 1) * P], mod_a[:, c:c + 1],
                                               ada[layer][:, shift + c:shift + c + 1], ALU.mult, ALU.add))
                return m

            to_columns(xn, [m], put)
        return V.last()

    def project(src, width, m_h, use):
        w, m_w, slot = stream(src, DC, width)
        for t in range(NT):
            b = proj_bank()
            T.need(b.free, m_w, m_h)
            for c in range(DC):
                last = pe.matmul(b.t[:, 0:width], hT[:, c, t * P:(t + 1) * P], w[:, c, :], start=c == 0,
                                 stop=c == DC - 1)
            m = T.did(last)
            slot_free[slot] = m
            b.free = use(t, b.t[:, 0:width], m)

    def project_cols(src, width, m_h, use):
        w, m_w, slot = stream(src, DC, width)
        for i in range(width // P):
            b = proj_bank()
            T.need(b.free, m_w, m_h)
            for c in range(DC):
                last = pe.matmul(b.t[:, 0:S], w[:, c, i * P:(i + 1) * P], hT[:, c, :], start=c == 0, stop=c == DC - 1)
            m = T.did(last)
            slot_free[slot] = m
            b.free = use(i, b.t[:, 0:S], m)

    hn = sb("head_ms", [P, NH])

    def head_norm(src, dst, n, g, tab, post, tmp, marks, g_heads=None):
        s3, d3, t3 = (v.rearrange("p (h d) -> p h d", d=HD) for v in (src, dst, tmp))
        np_ = src.shape[0]
        A.need(*marks)
        m = A.did(ac.activation(tmp, src, ACT.Square))
        V.need(m, *marks)
        m = V.did(ve.tensor_reduce(hn[0:np_, 0:n], t3, AX, ALU.add))
        V.need(m)
        m = V.did(ve.tensor_scalar(hn[0:np_, 0:n], hn[0:np_, 0:n], 1.0 / HD, EPS, ALU.mult, ALU.add))
        G.need(m, m_pow)
        m = G.did(po.tensor_tensor(hn[0:np_, 0:n], hn[0:np_, 0:n], pow_half[0:np_, 0:n], ALU.pow))
        V.need(m)
        m_src = V.did(ve.tensor_tensor(d3, s3, hn[0:np_, 0:n].unsqueeze(2).broadcast_to([np_, n, HD]), ALU.mult))
        V.need(m_src, m_rows)
        m = V.did(ve.scalar_tensor_tensor(out=d3, in0=d3, scalar=post, in1=g[0:np_, :].unsqueeze(1).broadcast_to([np_, n, HD]),
                                          op0=ALU.mult, op1=ALU.mult))
        cc = cosd[0:np_, tab, :].unsqueeze(1).broadcast_to([np_, n, ROT])
        G.need(m, m_rope)
        s_lo = sind[0:np_, tab, 0:HALF].unsqueeze(1).broadcast_to([np_, n, HALF])
        s_hi = sind[0:np_, tab, HALF:ROT].unsqueeze(1).broadcast_to([np_, n, HALF])
        G.did(po.tensor_tensor(t3[:, :, ROT:ROT + HALF], d3[:, :, HALF:ROT], s_lo, ALU.mult))
        G.did(po.tensor_tensor(t3[:, :, ROT + HALF:2 * ROT], d3[:, :, 0:HALF], s_hi, ALU.mult))
        m = G.did(po.tensor_tensor(t3[:, :, 0:ROT], d3[:, :, 0:ROT], cc, ALU.mult))
        G.need(m)
        return m_src, G.did(po.tensor_tensor(d3[:, :, 0:ROT], t3[:, :, 0:ROT], t3[:, :, ROT:2 * ROT], ALU.add))

    def q_tile_use(qT, j, tab_g, bufs):
        def use(t, ps, m):
            qn, tmp = bufs[t]
            V.need(T.last())
            m_src, m = head_norm(ps, qn[:], 8, tab_g, t, HD ** -0.5, tmp[:], [m])
            b = proj_bank()
            T.need(b.free, m, m_ident)
            for i in range(4):
                last = pe.transpose(b.t[:, i * P:(i + 1) * P], qn[:, i * P:(i + 1) * P], ident[:])
            m = T.did(last)
            A.need(m)
            b.free = A.did(ac.activation(qT[:, 4 * j:4 * j + 4, t * P:(t + 1) * P],
                                         b.t[:].rearrange("p (i n) -> p i n", i=4), ACT.Copy))
            return m_src
        return use

    def kv_tile_use(kT, v_sb, g, bufs):
        def use(t, ps, m):
            kn, tmp = bufs[t]
            dup = kn[:, 2 * P:4 * P + 2 * P]
            V.need(T.last())
            m_src, mk = head_norm(ps[:, 0:NKV * HD], kn[:, 0:NKV * HD], NKV, g, t, 1.0, tmp[:, 0:NKV * HD], [m])
            A.need(m_src)
            m_v = A.did(ac.activation(v_sb[:, t, :], ps[:, NKV * HD:2 * NKV * HD], ACT.Copy))
            G.need(mk)
            mk = G.did(po.tensor_copy(dup.rearrange("p (g u d) -> p g u d", g=NKV, u=2),
                                      kn[:, 0:NKV * HD].rearrange("p (g d) -> p g d", g=NKV).unsqueeze(2).broadcast_to(
                                          [P, NKV, 2, HD])))
            b = proj_bank()
            T.need(b.free, mk, m_ident)
            for i in range(NKV):
                last = pe.transpose(b.t[:, i * P:(i + 1) * P], dup[:, i * P:(i + 1) * P], ident[:])
            m = T.did(last)
            V.need(m)
            b.free = V.did(ve.tensor_copy(kT[:, :, t * P:(t + 1) * P], b.t[:].rearrange("p (i n) -> p i n", i=NKV)))
            return m_v
        return use

    soft = {k: [sb(f"{k}{i}", [P, 512], F32, layers) for i in range(2)] for k in ("scores", "probs", "probsT")}
    nmax = sb("nmax", [P, NT, NH])
    rsum = sb("rsum", [P, NT, NH])
    soft_read = {"scores": [None, None], "probs": [None, None], "probsT": [None, None]}

    def attend(tag, heads, q_of, k_of, v_of, bias_of, first_of, causal_keys, marks, done, fill):
        units = []
        for t in range(NT):
            w = P if causal_keys and t == 0 else S
            per = 512 // w
            by = [[h for h in heads if h % 2 == par] for par in (0, 1)]
            cut = [[hs[i:i + per] for i in range(0, len(hs), per)] for hs in by]
            for i in range(len(cut[0])):
                for par in (0, 1):
                    units.append((t, w, cut[par][i]))
        n = len(units)
        m_sc, m_ex, m_tr, m_cp = {}, {}, {}, {}

        def scores(u):
            t, w, hs = units[u]
            b = banks[2 + u % 2]
            T.need(b.free, *marks)
            for j, h in enumerate(hs):
                last = pe.matmul(b.t[:, j * w:(j + 1) * w], q_of(h, t), k_of(h, w), start=True, stop=True)
            m_sc[u] = T.did(last)
            V.need(m_sc[u], soft_read["scores"][u % 2])
            for j, h in enumerate(hs):
                m = V.did(ve.tensor_tensor_reduce(
                    out=soft["scores"][u % 2][:, j * w:(j + 1) * w], in0=b.t[:, j * w:(j + 1) * w],
                    in1=bias_of(h, t, w), scale=-1.0, scalar=first_of(h), op0=ALU.add, op1=ALU.min,
                    accum_out=nmax[:, t, h:h + 1]))
            b.free = m
            A.need(m, soft_read["probs"][u % 2])
            for j, h in enumerate(hs):
                m = A.did(ac.activation(soft["probs"][u % 2][:, j * w:(j + 1) * w],
                                        soft["scores"][u % 2][:, j * w:(j + 1) * w], ACT.Exp, scale=-1.0,
                                        bias=nmax[:, t, h:h + 1], accum_out=rsum[:, t, h:h + 1]))
            soft_read["scores"][u % 2] = m
            m_ex[u] = m

        def turned(u):
            t, w, hs = units[u]
            b = banks[4 + u % 2]
            T.need(b.free, m_ex[u])
            for i in range(len(hs) * w // P):
                last = pe.transpose(b.t[:, i * P:(i + 1) * P], soft["probs"][u % 2][:, i * P:(i + 1) * P], ident[:])
            m_tr[u] = T.did(last)
            soft_read["probs"][u % 2] = m_tr[u]
            V.need(m_tr[u], soft_read["probsT"][u % 2])
            b.free = m_cp[u] = V.did(ve.tensor_copy(soft["probsT"][u % 2][:], b.t[:]))

        def outputs(u):
            t, w, hs = units[u]
            T.need(m_cp[u], banks[6].free, banks[7].free)
            for j, h in enumerate(hs):
                o = banks[6 + h // 8].t[:, (h % 8) * HD:(h % 8 + 1) * HD]
                for k in range(w // P):
                    at = (j * (w // P) + k) * P
                    last = pe.matmul(o, soft["probsT"][u % 2][:, at:at + P], v_of(h, k), start=k == 0, stop=k == w // P - 1)
            m = T.did(last)
            soft_read["probsT"][u % 2] = m
            if u + 1 == n or units[u + 1][0] != t:
                banks[6].free = banks[7].free = done(t, m)

        for u in range(n + 2):
            if u < n:
                scores(u)
            if 0 <= u - 1 < n:
                turned(u - 1)
            if 0 <= u - 2 < n:
                outputs(u - 2)
            if fill and u % fill == fill - 1:
                filler()

    def o_heads(t_ap):
        return t_ap.rearrange("p (h d) -> p h d", d=HD)

    def gated_out(tag, o, z, w_src, layer, first, stack, m_o, norm_cols=None):
        ozT = sb(f"ozT{tag}", [P, DC, S], F32, stack)
        m_g = spread_gate(layer, first, stack)
        m_t = None
        for t in range(NT):
            V.need(*m_o)
            m = V.did(ve.tensor_tensor(o[:, t, :], o[:, t, :], z[:, t, :], ALU.mult)) if z is not None else m_o[0]

            def put(half, bank, m_t):
                if norm_cols is None:
                    A.need(m_t)
                    return A.did(ac.activation(ozT[:, 4 * half:4 * half + 4, t * P:(t + 1) * P],
                                               bank[:].rearrange("p (i n) -> p i n", i=4), ACT.Copy))
                V.need(m_t)
                for i in range(4):
                    c = 4 * half + i
                    m = V.did(ve.tensor_scalar(ozT[:, c, t * P:(t + 1) * P], bank[:, i * P:(i + 1) * P],
                                               norm_cols[:, c:c + 1], None, ALU.mult))
                return m

            to_columns(o[:, t, :], [m, *m_o], put)
        m_ready = [A.last(), V.last()]
        tmp = sb(f"gated{tag}", [P, 512], F32, stack)
        for j in range(2):
            w, m_w, slot = stream(w_src[:, j * WT:(j + 1) * WT], DC, WT)
            for t in range(NT):
                b = proj_bank()
                T.need(b.free, m_w, *m_ready)
                for c in range(DC):
                    last = pe.matmul(b.t[:], ozT[:, c, t * P:(t + 1) * P], w[:, c, :], start=c == 0, stop=c == DC - 1)
                m = T.did(last)
                slot_free[slot] = m
                V.need(m, m_g, V.last())
                b.free = V.did(ve.tensor_tensor(tmp[:], b.t[:], gate_row[:, j * 512:(j + 1) * 512], ALU.mult))
                V.need(b.free)
                V.did(ve.tensor_tensor(x[:, t, j * 512:(j + 1) * 512], x[:, t, j * 512:(j + 1) * 512], tmp[:], ALU.add))
        return V.last()

    def simple_done(o, scale, with_gates=None, marks=()):
        def done(t, m):
            V.need(m, A.last(), *marks)
            m = V.did(ve.tensor_scalar(scale[:, t, :], rsum[:, t, :], 1e-30, None, ALU.max))
            V.need(m)
            m = V.did(ve.reciprocal(scale[:, t, :], scale[:, t, :]))
            if with_gates is not None:
                V.need(m)
                m = V.did(ve.tensor_tensor(scale[:, t, :], scale[:, t, :], with_gates[:, t, :], ALU.mult))
            V.need(m)
            for half in range(2):
                sc = scale[:, t, 8 * half:8 * half + 8].unsqueeze(2).broadcast_to([P, 8, HD])
                if with_gates is None:
                    m = V.did(ve.tensor_tensor(o_heads(o[:, t, 512 * half:512 * half + 512]), o_heads(banks[6 + half].t[:]),
                                               sc, ALU.mult))
                else:
                    V.need(G.last())
                    m = V.did(ve.tensor_tensor(o_heads(soft_add[:, half * 512:half * 512 + 512]),
                                               o_heads(banks[6 + half].t[:]), sc, ALU.mult))
                    G.need(m, V.last())
                    G.did(po.tensor_tensor(o[:, t, 512 * half:512 * half + 512], o[:, t, 512 * half:512 * half + 512],
                                           soft_add[:, half * 512:half * 512 + 512], ALU.add))
            return m
        return done

    soft_add = sb("branch_out", [P, D], F32, layers)[:]

    def causal_bias(h, t, w):
        return causal[:, P:S] if w == P else causal[:]

    with ExitStack() as s0:
        w_in = a["nsa_w_in"]
        m_h = modulated(0, col("norm_g", 0, 8), 0, 8, s0, [m_x])
        qT = sb("qT0", [P, NH // 2, S], F32, s0)
        kTs = [sb(f"kT0{i}", [P, NKV, S], F32, s0) for i in range(2)]
        vs = [sb(f"v0{i}", [P, NT, NKV * HD], F32, s0) for i in range(2)]
        bufs = [(sb(f"qn{t}", [P, 6 * P], F32, s0), sb(f"qtmp{t}", [P, 512], F32, s0)) for t in range(NT)]
        qbufs = [(b[0][:, 0:512], b[1]) for b in bufs]
        z = sb("z0", [P, NT, D], F32, s0)
        gates = sb("gates", [P, 3, NT, NH], F32, s0)
        gtmp = sb("gtmp", [P, 3 * NH], F32, s0)
        o = sb("o0", [P, NT, D], F32, s0)
        scale = sb("scale0", [P, NT, NH], F32, s0)
        x2 = sb("x2", [P, NKV, P], F32, s0)
        xpe = sb("xpe", [P, NPAIR, NKV, NCMP], F32, s0)
        hid = sb("hid", [P, 2, NKV, CPAD], F32, s0)
        pe_sb = sb("cmp_pe", [P, 2, NPAIR], F32, s0)
        w2 = sb("cmp_w2", [P, 2, 2, HD], F32, s0)
        kc_n = sb("kc_n", [P, 2 * HD], F32, s0)
        kc_t = sb("kc_t", [P, HD], F32, s0)
        kcT = sb("kcT", [P, P], F32, s0)
        vbd = sb("vbd", [P, NKV, HD], F32, s0)
        m_pe = load(pe_sb[:], a["cmp_pe"], "ld_pe", ac)
        m_w2 = load(w2[:], a["nsa_cmp_w2"].rearrange("i (c p) d -> p i c d", p=P), "ld_w2", ac)
        mz1 = G.did(po.memset(hid[:], 0.0))
        mz2 = G.did(po.memset(vbd[:], 0.0))

        def x2_use(i2):
            def use(blk, ps, m):
                V.need(m, T.last(), G.last())
                for g2 in range(2):
                    src = ps[g2 * HD:(g2 + 1) * HD, :].rearrange("p (m u) -> p u m", u=2)
                    for par in range(2):
                        mm = V.did(ve.tensor_copy(x2[par * HD:(par + 1) * HD, 2 * blk + g2, :], src[:, par, :]))
                return mm
            return use

        for i in range(2):
            lo = NH * HD + i * NKV * HD
            project_cols(w_in[:, lo:lo + NKV * HD], NKV * HD, m_h, x2_use(i))
            V.need(V.last(), m_pe, T.last())
            for g in range(NKV):
                flat = x2[:, g, :]
                for c0 in (0, 8):
                    src = x2[:, g, c0:c0 + 8 * NCMP].rearrange("p (n c) -> p c n", c=8)
                    m = V.did(ve.tensor_tensor(xpe[:, c0:c0 + 8, g, :], src,
                                               pe_sb[:, i, c0:c0 + 8].unsqueeze(2).broadcast_to([P, 8, NCMP]), ALU.add))
            m_xpe = m
            w1, m_w, slot = stream(a["nsa_cmp_w1"][i], NPAIR, CMP_HID)
            b = proj_bank()
            T.need(b.free, m_w, m_xpe)
            for hb in range(2):
                for c in range(NPAIR):
                    last = pe.matmul(b.t[:, hb * 64:hb * 64 + NKV * NCMP], w1[:, c, hb * P:(hb + 1) * P],
                                     xpe[:, c, :, :].rearrange("p g n -> p (g n)"), start=c == 0, stop=c == NPAIR - 1)
            m = T.did(last)
            slot_free[slot] = m
            A.need(m, mz1, T.last(), m_cols)
            for hb in range(2):
                m = A.did(ac.activation(hid[:, hb, :, 0:NCMP],
                                        b.t[:, hb * 64:hb * 64 + NKV * NCMP].rearrange("p (g n) -> p g n", g=NKV),
                                        ACT.Gelu_apprx_tanh, bias=col("nsa_cmp_b1", 2 * i + hb, 2 * i + hb + 1)))
            b.free = m
            b = proj_bank()
            T.need(b.free, m, m_w2)
            for hb in range(2):
                last = pe.matmul(b.t[:, 0:HD], hid[:, hb, :, :].rearrange("p g n -> p (g n)"), w2[:, i, hb, :],
                                 start=hb == 0, stop=hb == 1)
            m = T.did(last)
            if i == 0:
                _, mk = head_norm(b.t[:, 0:HD], kc_n[:, 0:HD], 1, row("nsa_k_norm", 0, HD), NT, 1.0, kc_t[:], [m])
                b.free = mk
                G.need(mk)
                mk = G.did(po.tensor_copy(kc_n[:, HD:2 * HD], kc_n[:, 0:HD]))
                b2 = proj_bank()
                T.need(b2.free, mk, m_ident)
                m = T.did(pe.transpose(b2.t[:, 0:P], kc_n[:], ident[:]))
                V.need(m)
                b2.free = m_kc = V.did(ve.tensor_copy(kcT[:], b2.t[:, 0:P]))
            else:
                V.need(m, mz2)
                for g in range(NKV):
                    m = V.did(ve.tensor_copy(vbd[g * CPAD:(g + 1) * CPAD, g, :], b.t[g * CPAD:(g + 1) * CPAD, 0:HD]))
                b.free = m_vc = m

        for i in range(2):
            lo = NH * HD + (2 + 2 * i) * NKV * HD
            project(w_in[:, lo:lo + WT], WT, m_h,
                    kv_tile_use(kTs[i], vs[i], row("nsa_k_norm", (i + 1) * HD, (i + 2) * HD), bufs))
        for j in range(2):
            project(w_in[:, j * WT:(j + 1) * WT], WT, m_h, q_tile_use(qT, j, row("nsa_q_norm"), qbufs))
        lo = NH * HD + 6 * NKV * HD

        def gate_use(t, ps, m):
            V.need(m, m_rows, A.last())
            m_s = V.did(ve.tensor_tensor(gtmp[:], ps, row("nsa_gate_b"), ALU.add))
            A.need(m_s)
            A.did(ac.activation(gates[:, :, t, :], gtmp[:].rearrange("p (h b) -> p b h", b=3), ACT.Sigmoid))
            return m_s

        project(w_in[:, lo:lo + 3 * NH], 3 * NH, m_h, gate_use)

        def z_use(j, z):
            def use(t, ps, m):
                A.need(m)
                return A.did(ac.activation(z[:, t, j * 512:(j + 1) * 512], ps, ACT.Silu))
            return use

        for j in range(2):
            at = lo + 3 * NH + j * WT
            project(w_in[:, at:at + WT], WT, m_h, z_use(j, z))
        m_ready = [V.last(), A.last(), G.last()]

        smc = sb("smc", [P, 2, 2 * NKV, CPAD], F32, s0)
        red = sb("red", [P, 3, NH], F32, s0)
        for t in range(NT):
            T.need(banks[2].free, banks[3].free, m_kc, *m_ready)
            for par in range(2):
                for g in range(NKV):
                    for r2 in range(2):
                        h = GQA * g + 2 * r2 + par
                        half = slice(HD * par, HD * par + HD)
                        last = pe.matmul(banks[2 + par].t[:, (NKV * r2 + g) * CPAD:(NKV * r2 + g + 1) * CPAD],
                                         qT[half, h // 2, t * P:(t + 1) * P], kcT[half, g * CPAD:(g + 1) * CPAD],
                                         start=True, stop=True)
                m = T.did(last)
            V.need(m, m_cmask, T.last())
            for par in range(2):
                m = V.did(ve.tensor_tensor(smc[:, par], banks[2 + par].t[:, 0:2 * NKV * CPAD].rearrange("p (h n) -> p h n", n=CPAD),
                                           cmp_mask[:, t, :].unsqueeze(1).broadcast_to([P, 2 * NKV, CPAD]), ALU.add))
                banks[2 + par].free = m
            sm3 = smc[:].rearrange("p a h n -> p (a h) n")
            V.need(m)
            m = V.did(ve.tensor_reduce(red[:, 0, :], sm3, AX, ALU.max))
            V.need(m)
            m = V.did(ve.tensor_scalar(red[:, 0, :], red[:, 0, :], FLOOR, None, ALU.max))
            V.need(m)
            m = V.did(ve.tensor_tensor(sm3, sm3, red[:, 0, :].unsqueeze(2).broadcast_to([P, NH, CPAD]), ALU.subtract))
            A.need(m)
            m = A.did(ac.activation(sm3, sm3, ACT.Exp))
            V.need(m)
            m = V.did(ve.tensor_reduce(red[:, 1, :], sm3, AX, ALU.add))
            for r in range(GQA):
                T.need(m, banks[4].free)
                last = pe.transpose(banks[4].t[:, r * P:(r + 1) * P],
                                    smc[:, r % 2, NKV * (r // 2):NKV * (r // 2 + 1)].rearrange("p g n -> p (g n)"), ident[:])
            m_t = T.did(last)
            V.need(m, m_t, T.last())
            m_c = V.did(ve.tensor_copy(soft["probsT"][0][:], banks[4].t[:]))
            banks[4].free = m_c
            m = V.did(ve.tensor_scalar(red[:, 1, :], red[:, 1, :], 1e-30, None, ALU.max))
            V.need(m)
            m = V.did(ve.reciprocal(red[:, 2, :], red[:, 1, :]))
            V.need(m)
            for par in range(2):
                r4 = red[:, 2, :].rearrange("p (a r g) -> p a r g", a=2, r=2)[:, par]
                g4 = gates[:, 0, t, :].rearrange("p (g r a) -> p a r g", a=2, r=2)[:, par]
                m = V.did(ve.tensor_tensor(r4, r4, g4, ALU.mult))
            T.need(m_c, banks[6].free, banks[7].free, m_vc)
            for r in range(GQA):
                last = pe.matmul(banks[6 + r // 2].t[:, (r % 2) * NKV * HD:(r % 2 + 1) * NKV * HD],
                                 soft["probsT"][0][:, r * P:(r + 1) * P], vbd[:].rearrange("p g d -> p (g d)"),
                                 start=True, stop=True)
            m_o = T.did(last)
            V.need(m_o, m)
            for r in range(GQA):
                src = banks[6 + r // 2].t[:, (r % 2) * NKV * HD:(r % 2 + 1) * NKV * HD].rearrange("p (g d) -> p g d", g=NKV)
                dst = o[:, t, :].rearrange("p (g r d) -> p r g d", g=NKV, r=GQA)[:, r]
                sc = red[:, 2, :].rearrange("p (a r g) -> p a r g", a=2, r=2)[:, r % 2, r // 2]
                m = V.did(ve.tensor_tensor(dst, src, sc.unsqueeze(2).broadcast_to([P, NKV, HD]), ALU.mult))
            banks[6].free = banks[7].free = m
            soft_read["probsT"][0] = m_o

        for i in range(2):
            half_of = lambda h: slice(HD * (h % 2), HD * (h % 2) + HD)
            attend(f"nsa{i}", list(range(NH)),
                   lambda h, t: qT[half_of(h), h // 2, t * P:(t + 1) * P],
                   lambda h, w: kTs[i][half_of(h), h // GQA, 0:w],
                   lambda h, k: vs[i][:, k, (h // GQA) * HD:(h // GQA + 1) * HD],
                   causal_bias, lambda h: 3e38, True, [*m_ready, m_causal],
                   simple_done(o, scale, gates[:, i + 1], marks=()), 4)
        m_x = gated_out("0", o, z, a["nsa_w_out"], 0, 16, s0, [V.last(), G.last()])
        if "x1" in dbg:
            Y.need(m_x)
            stores.append(load(dbg["x1"].rearrange("(t p) d -> p t d", p=P), x[:], "st_x1"))
        meet()

    with ExitStack() as s1:
        filler(100)
        w_in = a["moba_w_in"]
        m_h = modulated(1, col("norm_g", 8, 16), 0, 8, s1, [m_x])
        qT = sb("qT1", [P, NH // 2, S], F32, s1)
        kT = sb("kT1", [P, NKV, S], F32, s1)
        v1 = sb("v1", [P, NT, NKV * HD], F32, s1)
        bufs = [(sb(f"qn1{t}", [P, 6 * P], F32, s1), sb(f"qtmp1{t}", [P, 512], F32, s1)) for t in range(NT)]
        qbufs = [(b[0][:, 0:512], b[1]) for b in bufs]
        z = sb("z1", [P, NT, D], F32, s1)
        o = sb("o1", [P, NT, D], F32, s1)
        scale = sb("scale1", [P, NT, NH], F32, s1)
        project(w_in[:, D:D + WT], WT, m_h, kv_tile_use(kT, v1, row("moba_k_norm"), bufs))
        for j in range(2):
            project(w_in[:, j * WT:(j + 1) * WT], WT, m_h, q_tile_use(qT, j, row("moba_q_norm"), qbufs))

        def z_use1(j):
            def use(t, ps, m):
                A.need(m)
                return A.did(ac.activation(z[:, t, j * 512:(j + 1) * 512], ps, ACT.Silu))
            return use

        for j in range(2):
            project(w_in[:, D + WT + j * WT:D + 2 * WT + j * WT], WT, m_h, z_use1(j))
        m_ready = [V.last(), A.last(), G.last()]
        half_of = lambda h: slice(HD * (h % 2), HD * (h % 2) + HD)
        attend("moba", list(range(NH)),
               lambda h, t: qT[half_of(h), h // 2, t * P:(t + 1) * P],
               lambda h, w: kT[half_of(h), h // GQA, 0:w],
               lambda h, k: v1[:, k, (h // GQA) * HD:(h // GQA + 1) * HD],
               causal_bias, lambda h: 3e38, True, m_ready, simple_done(o, scale), 0)
        m_x = gated_out("1", o, z, a["moba_w_out"], 1, 16, s1, [V.last(), G.last()])
        if "x2" in dbg:
            Y.need(m_x)
            stores.append(load(dbg["x2"].rearrange("(t p) d -> p t d", p=P), x[:], "st_x2"))
        meet()

    with ExitStack() as s2:
        w_in = a["w_in_2"]
        bias_a = sb("bias_a", [P, HA, 3 * P], F32, s2)
        bias_b = sb("bias_b", [P, NT, HB, S], F32, s2)
        m_ba = load(bias_a[:], a["bias_a"], "ld_ba", ac)
        m_bb = load(bias_b[:], a["bias_b"], "ld_bb", ac)
        m_h = modulated(2, col("norm1_g_2"), 0, 8, s2, [m_x])
        qT = sb("qT2", [P, NH // 2, S], F32, s2)
        kaT = sb("kaT", [P, KVA, S], F32, s2)
        kbT = sb("kbT", [P, HB // 2, S], F32, s2)
        va = sb("va", [P, NT, KVA * HD], F32, s2)
        vb = sb("vb", [P, NT, HB * HD], F32, s2)
        o = sb("o2", [P, NT, D], F32, s2)
        scale = sb("scale2", [P, NT, NH], F32, s2)
        nsink = sb("nsink", [P, HA], F32, s2)
        esink = sb("esink", [P, NT, HA], F32, s2)
        wa, wk = HA * HD, KVA * HD

        def q_use(first):
            def use(i, ps, m):
                A.need(m)
                return A.did(ac.activation(qT[:, first + i, :], ps, ACT.Copy, scale=HD ** -0.5))
            return use

        project_cols(w_in[:, 0:wa], wa, m_h, q_use(0))

        def ka_use(i, ps, m):
            V.need(m)
            for g in range(KVA):
                for dup in range(2):
                    mm = V.did(ve.tensor_copy(kaT[dup * HD:(dup + 1) * HD, g, :], ps[g * HD:(g + 1) * HD, :]))
            return mm

        project_cols(w_in[:, wa:wa + wk], wk, m_h, ka_use)

        def v_use(dst):
            def use(t, ps, m):
                V.need(m)
                return V.did(ve.tensor_copy(dst[:, t, :], ps))
            return use

        project(w_in[:, wa + wk:wa + 2 * wk], wk, m_h, v_use(va))
        at = wa + 2 * wk
        project_cols(w_in[:, at:at + WT], WT, m_h, q_use(HA // 2))

        def kb_use(i, ps, m):
            V.need(m)
            return V.did(ve.tensor_copy(kbT[:, i, :], ps))

        project_cols(w_in[:, at + WT:at + 2 * WT], WT, m_h, kb_use)
        project(w_in[:, at + 2 * WT:at + 3 * WT], WT, m_h, v_use(vb))
        V.need(m_rows)
        m_ns = V.did(ve.tensor_scalar(nsink[:], row("sink_a_2"), -1.0, None, ALU.mult))
        V.need(m_ns)
        m_ready = [V.last(), A.last(), G.last()]

        def bias_of(h, t, w):
            return bias_a[:, h, P * (1 - t):P * (3 - t)] if h < HA else bias_b[:, t, h - HA, :]

        def done2(t, m):
            V.need(m, A.last())
            m = V.did(ve.tensor_tensor(esink[:, t, :], row("sink_a_2"), nmax[:, t, 0:HA], ALU.add))
            A.need(m)
            m = A.did(ac.activation(esink[:, t, :], esink[:, t, :], ACT.Exp))
            V.need(m)
            m = V.did(ve.tensor_tensor(rsum[:, t, 0:HA], rsum[:, t, 0:HA], esink[:, t, :], ALU.add))
            return simple_done(o, scale)(t, m)

        attend("mix", list(range(NH)),
               lambda h, t: qT[half_of(h), h // 2, t * P:(t + 1) * P],
               lambda h, w: kaT[half_of(h), h // (HA // KVA), 0:w] if h < HA else kbT[half_of(h), (h - HA) // 2, 0:w],
               lambda h, k: va[:, k, (h // 4) * HD:(h // 4 + 1) * HD] if h < HA else vb[:, k, (h - HA) * HD:(h - HA + 1) * HD],
               bias_of, lambda h: nsink[:, h:h + 1] if h < HA else 3e38, False, [*m_ready, m_ba, m_bb], done2, 0)
        V.need(m_ba, m_bb)
        for t in range(NT):
            for half in range(2):
                part = o[:, t, 512 * half:512 * half + 512]
                m = row_rstd(stat[:, 2 + 2 * t + half:3 + 2 * t + half], part, 512, [V.last()], soft_add[:, 0:512])
                V.need(m)
                V.did(ve.tensor_scalar(part, part, stat[:, 2 + 2 * t + half:3 + 2 * t + half], None, ALU.mult))
        norm_cols = cols[:, COL_AT["out_norm_a_2"][0]:COL_AT["out_norm_b_2"][1]]
        m_x = gated_out("2", o, None, a["w_out_2"], 2, 16, s2, [V.last(), G.last()], norm_cols)
        if "x3" in dbg:
            Y.need(m_x)
            stores.append(load(dbg["x3"].rearrange("(t p) d -> p t d", p=P), x[:], "st_x3"))
        meet()

    with ExitStack() as s3:
        qsT = sb("qsT", [P, 2 * PH, S], F32, s3)
        keysT = sb("keysT", [P, 2 * PH, PK], F32, s3)
        m_keys = load(keysT[:], a["keysT"], "ld_keys", ac)
        m_h = modulated(2, col("norm2_g_2"), 24, 32, s3, [m_x])

        for j in range(4):
            def use(i, ps, m, j=j):
                A.need(m)
                return A.did(ac.activation(qsT[:, 4 * j + i, :], ps, ACT.Copy))
            project_cols(a["w_query_2"][:, j * WT:(j + 1) * WT], WT, m_h, use)
        m_q = A.last()
        sc = sb("key_scores", [P, 2 * PH, PK], F32, s3)
        sc2 = sb("key_scores2", [P, 2, PK], F32, s3)
        top = sb("top", [P, PH, 2, PTOP], F32, s3)
        topi = sb("topi", [P, PH, 2, PTOP], U32, s3)
        topf = sb("topf", [P, PH, 2, PTOP], F32, s3)
        cand = sb("cand", [P, PH, PTOP, PTOP], F32, s3)
        cand2 = sb("cand2", [P, 2, PTOP * PTOP], F32, s3)
        best = sb("best", [P, PH, PTOP], F32, s3)
        besti = sb("besti", [P, PH, PTOP], U32, s3)
        rank_u = sb("rank_u", [P, 2, PH, PTOP], U32, s3)
        rank = sb("rank", [P, 2, PH, PTOP], F32, s3)
        eq = sb("eq", [P, PH, PTOP, PTOP], F32, s3)
        hk = sb("hk", [P, 3, PH, PTOP], F32, s3)
        weight = sb("weight", [P, PH, PTOP], F32, s3)
        gsum = sb("gsum", [P, PH], F32, s3)

        def top16(src, work, vals, idx, marks):
            V.need(V.last(), *marks)
            m = V.did(ve.max(vals[:, 0:8], src))
            V.need(m)
            V.did(ve.max_index(idx[:, 0:8], vals[:, 0:8], src))
            m = V.did(ve.match_replace(work, vals[:, 0:8], src, -3.4e38))
            V.need(m)
            m = V.did(ve.max(vals[:, 8:16], work))
            V.need(m)
            return V.did(ve.max_index(idx[:, 8:16], vals[:, 8:16], work))

        for t in range(NT):
            for q in range(4):
                b = banks[2 + q % 2]
                T.need(b.free, m_q, m_keys)
                for i in range(4):
                    hh = 4 * q + i
                    last = pe.matmul(b.t[:, i * PK:(i + 1) * PK], qsT[:, hh, t * P:(t + 1) * P], keysT[:, hh, :],
                                     start=True, stop=True)
                m = T.did(last)
                A.need(m, V.last())
                b.free = A.did(ac.activation(sc[:, 4 * q:4 * q + 4, :], b.t[:].rearrange("p (i n) -> p i n", i=4), ACT.Copy))
                for i in range(4):
                    hh = 4 * q + i
                    m = top16(sc[:, hh, :], sc2[:, i % 2, :], top[:, hh // 2, hh % 2, :], topi[:, hh // 2, hh % 2, :], [b.free])
            V.need(m)
            m = V.did(ve.tensor_copy(topf[:], topi[:]))
            V.need(m)
            m = V.did(ve.tensor_tensor(cand[:], top[:, :, 0, :].unsqueeze(3).broadcast_to([P, PH, PTOP, PTOP]),
                                       top[:, :, 1, :].unsqueeze(2).broadcast_to([P, PH, PTOP, PTOP]), ALU.add))
            for h in range(PH):
                m = top16(cand[:, h].rearrange("p i j -> p (i j)"), cand2[:, h % 2, :], best[:, h, :], besti[:, h, :], [m])
            V.need(m)
            V.did(ve.tensor_scalar(rank_u[:, 0], besti[:], 4, None, ALU.logical_shift_right))
            m = V.did(ve.tensor_scalar(rank_u[:, 1], besti[:], 15, None, ALU.bitwise_and))
            V.need(m)
            m = V.did(ve.tensor_copy(rank[:], rank_u[:]))
            for side in range(2):
                V.need(m, m_iota)
                m = V.did(ve.tensor_tensor(eq[:], rank[:, side].unsqueeze(3).broadcast_to([P, PH, PTOP, PTOP]),
                                           iota_k[:, 0:PTOP].unsqueeze(1).unsqueeze(1).broadcast_to([P, PH, PTOP, PTOP]),
                                           ALU.is_equal))
                V.need(m)
                m = V.did(ve.tensor_tensor(eq[:], eq[:], topf[:, :, side, :].unsqueeze(2).broadcast_to([P, PH, PTOP, PTOP]),
                                           ALU.mult))
                V.need(m, T.last())
                m = V.did(ve.tensor_reduce(hk[:, side], eq[:], AX, ALU.add))
            V.need(m)
            m = V.did(ve.tensor_tensor(weight[:], best[:], best[:, :, 0:1].broadcast_to([P, PH, PTOP]), ALU.subtract))
            A.need(m)
            m = A.did(ac.activation(weight[:], weight[:], ACT.Exp))
            V.need(m)
            m = V.did(ve.tensor_reduce(gsum[:], weight[:], AX, ALU.add))
            V.need(m)
            m = V.did(ve.reciprocal(gsum[:], gsum[:]))
            V.need(m)
            m = V.did(ve.tensor_tensor(hk[:, 2], weight[:], gsum[:].unsqueeze(2).broadcast_to([P, PH, PTOP]), ALU.mult))
            b = banks[4]
            T.need(m, b.free)
            for i in range(3):
                last = pe.transpose(b.t[:, i * P:(i + 1) * P], hk[:, i].rearrange("p h k -> p (h k)"), ident[:])
            m = T.did(last)
            V.need(m)
            b.free = V.did(ve.tensor_copy(hkT[:, :, t * P:(t + 1) * P], b.t[:, 0:3 * P].rearrange("p (i n) -> p i n", i=3)))
        m_hk = V.last()
        if "hk" in dbg:
            Y.need(m_hk)
            stores.append(load(dbg["hk"], hkT[:], "st_hk"))
        meet()

    layers.close()
    scope[0] = st
    if True:
        gmat = sb("gmat", [P, PK, S])
        TOK = 8
        oh = [sb(f"onehot{i}", [P, TOK, P]) for i in range(2)]
        s_oh = st.enter_context(nc.semaphore("s_onehot"))
        s_gm = st.enter_context(nc.semaphore("s_gatemm"))
        s_ge = st.enter_context(nc.semaphore("s_gateout"))
        nh = TOK // 4
        for e, s in ((ve, s_oh), (pe, s_gm), (ac, s_ge)):
            e.sem_inc(s, 1)
        with nc.Fori(0, S // TOK) as i:
            ve.wait_ge(s_gm, i * nh + 1)
            for k in range(TOK):
                ve.tensor_scalar(oh[0][:, k, :], iota_k[:], hkT[:, 0, bass.ds(i * TOK + k, 1)], None, ALU.is_equal)
                last = ve.tensor_scalar(oh[1][:, k, :], iota_k[:], hkT[:, 1, bass.ds(i * TOK + k, 1)],
                                        hkT[:, 2, bass.ds(i * TOK + k, 1)], ALU.is_equal, ALU.mult)
            last.then_inc(s_oh, 1)
            pe.wait_ge(s_oh, i + 2)
            for q in range(nh):
                pe.wait_ge(s_ge, i * nh + 1 + q - nh + nh)
                for k in range(4):
                    last = pe.matmul(banks[q].t[:, k * P:(k + 1) * P], oh[0][:, 4 * q + k, :], oh[1][:, 4 * q + k, :],
                                     start=True, stop=True)
                last.then_inc(s_gm, 1)
            for q in range(nh):
                ac.wait_ge(s_gm, i * nh + 2 + q)
                ac.activation(gmat[:, :, bass.ds(i * TOK + 4 * q, 4)], banks[q].t[:].rearrange("p (k e) -> p e k", k=4),
                              ACT.Copy).then_inc(s_ge, 1)
        for e in (V, A, T, Y):
            e.eng.wait_ge(s_ge, S // 4 + 1)

    uslot = [ring[i // 2][:, (i % 2) * 2048:(i % 2) * 2048 + 2048] for i in range(BLK)]
    s_uv = [st.enter_context(nc.semaphore(f"s_uv{k}")) for k in range(BLK)]
    s_z = st.enter_context(nc.semaphore("s_z"))
    s_gelu = st.enter_context(nc.semaphore("s_gelu"))
    s_a = st.enter_context(nc.semaphore("s_a"))
    s_out = st.enter_context(nc.semaphore("s_peer"))
    zg = [sb(f"zg{k}", [P, S]) for k in range(2)]
    aT = [sb(f"aT{k}", [P, S]) for k in range(2)]
    outb = banks[4:8]
    n_it = PK // BLK
    for e, s in ((pe, s_z), (ac, s_gelu), (ve, s_a), (pe, s_out)):
        e.sem_inc(s, BLK)

    def peer_block(i, k, first=False, last_block=False):
        e2 = i * BLK + k
        u = uslot[k].rearrange("p (a n) -> p a n", a=2)
        uT = u[:, 0, :].rearrange("p (c e) -> p c e", c=DC)
        vv = u[:, 1, :]
        sy.wait_ge(s_out, e2 + 1)
        sy.dma_start(uslot[k].rearrange("p (a n) -> p a n", a=2), a["uv"][bass.ds(e2, 1)].rearrange("o a p n -> p (o a) n")
                     ).then_inc(s_uv[k], 16)
        pe.wait_ge(s_uv[k], i * 16 + 16)
        pe.wait_ge(s_gelu, e2 + BLK - 1)
        for c in range(DC):
            last = pe.matmul(banks[k % 2].t[:, 0:S], uT[:, c, :], hT[:, c, :], start=c == 0, stop=c == DC - 1)
        last.then_inc(s_z, 1)
        ac.wait_ge(s_z, e2 + BLK + 1)
        ac.wait_ge(s_a, e2 + BLK - 1)
        ac.activation(zg[k % 2][:], banks[k % 2].t[:, 0:S], ACT.Gelu_apprx_tanh).then_inc(s_gelu, 1)
        ve.wait_ge(s_gelu, e2 + BLK + 1)
        ve.wait_ge(s_out, e2 + BLK - 1)
        ve.tensor_tensor(aT[k % 2][:], zg[k % 2][:], gmat[:, bass.ds(e2, 1), :].rearrange("p o t -> p (o t)"), ALU.mult
                         ).then_inc(s_a, 1)

    def out_block(i, k, kk, start, stop):
        e2 = i * BLK + kk
        pe.wait_ge(s_a, e2 + BLK + 1)
        vv = uslot[k].rearrange("p (a n) -> p a n", a=2)[:, 1, :]
        for t in range(NT):
            for h in range(2):
                last = pe.matmul(outb[2 * t + h].t[:], aT[k % 2][:, t * P:(t + 1) * P], vv[:, h * 512:(h + 1) * 512],
                                 start=start, stop=stop, skip_group_check=True)
        last.then_inc(s_out, 1)

    for k in range(BLK):
        peer_block(0, k)
        if k:
            out_block(0, k - 1, k - 1, k == 1, False)
    with nc.Fori(1, n_it) as i:
        for k in range(BLK):
            peer_block(i, k)
            out_block(i, (k - 1) % BLK, k - 1, False, False)
    out_block(n_it - 1, BLK - 1, BLK - 1, False, True)
    total = PK + BLK

    with ExitStack() as s4:
        for e in (ve, ac, pe):
            e.wait_ge(s_out, total)
        m_g = spread_gate(2, 40, s4)
        soft_add = ring[0][:, 0:D]
        for t in range(NT):
            V.need(m_g, V.last())
            for h in range(2):
                m = V.did(ve.tensor_tensor(soft_add[:, h * 512:(h + 1) * 512], outb[2 * t + h].t[:],
                                           gate_row[:, h * 512:(h + 1) * 512], ALU.mult))
            V.need(m)
            m = V.did(ve.tensor_tensor(x[:, t, :], x[:, t, :], soft_add, ALU.add))
            m = row_rstd(stat[:, t:t + 1], x[:, t, :], D, [m], soft_add)
            V.need(m)
            m = V.did(ve.scalar_tensor_tensor(out=x[:, t, :], in0=x[:, t, :], scalar=stat[:, t:t + 1],
                                              in1=row("final_g_2"), op0=ALU.mult, op1=ALU.mult))
            Y.need(m)
            stores.append(load(a["out"].rearrange("(t p) d -> t p d", p=P)[t], x[:, t, :], f"st_out{t}"))
    for m in stores:
        sy.wait_ge(*m)


def t5_buckets(rel):
    half, exact = 16, 8
    n = np.abs(rel)
    nf = np.maximum(n, 1).astype(np.float32)
    large = exact + (np.log(nf / np.float32(exact)) / np.float32(np.log(128 / exact)) * np.float32(half - exact)).astype(np.int32)
    return np.where(rel > 0, half, 0) + np.where(n < exact, n, np.minimum(large, half - 1))


DEBUG = {}


def kernel(**inputs):
    import numpy as _np
    import concourse.bacc as _bacc
    from concourse import mybir as _mybir
    from concourse.bass_utils import run_bass_kernel_spmd as _run

    f = {k: _np.asarray(v) for k, v in inputs.items()}
    arrays = {}
    arrays["cols"] = _np.concatenate([f[n].reshape(-1, P) for n, _ in COLS]).T
    arrays["rows"] = _np.concatenate([f[n].reshape(-1) for n, _ in ROWS])[None, :]
    pos = f["positions"][0]
    cpos = pos[_np.minimum(_np.arange(CPAD) * CMP_STRIDE + CMP_LEN - 1, S - 1)]
    arrays["pos"] = _np.stack([pos[:P], pos[P:], _np.tile(cpos, NKV)], axis=1)
    arrays["x"] = f["x"][0]
    arrays["ada_w"] = f["ada_w"]
    arrays["w_ada_2"] = f["w_ada_2"][0]
    for n in ("nsa_w_in", "nsa_w_out", "moba_w_in", "moba_w_out", "w_in_2", "w_out_2", "w_query_2", "nsa_cmp_w1", "nsa_cmp_w2"):
        arrays[n] = f[n][0]
    arrays["cmp_pe"] = f["nsa_cmp_pe"][0].reshape(2, NPAIR, P).transpose(2, 0, 1)
    rel = _np.arange(3 * P)[None, :] - P - _np.arange(P)[:, None]
    seen = _np.abs(rel) <= P
    table = f["t5_table_2"][t5_buckets(rel)]
    arrays["bias_a"] = _np.where(seen[:, :, None], table, _np.float32(NEG)).transpose(0, 2, 1)
    tok = _np.arange(S)
    rr, cc = tok // 64, tok % 64
    start = _np.clip(cc - 8, 0, 64 - 16)
    row_off = rr[None, :] - rr[:, None] + 7
    col_off = cc[None, :] - cc[:, None] + 15
    inside = (cc[None, :] >= start[:, None]) & (cc[None, :] < start[:, None] + 16)
    rpb = f["rpb_b_2"][0][:, row_off, _np.clip(col_off, 0, 30)]
    bb = _np.where(inside[None], rpb, _np.float32(NEG))
    arrays["bias_b"] = bb.reshape(HB, NT, P, S).transpose(2, 1, 0, 3)
    arrays["keysT"] = f["sub_keys_2"][0].reshape(2 * PH, PK, P).transpose(2, 0, 1)
    u = f["u_experts_2"][0].reshape(PK, PK, DC, P)
    v = f["v_experts_2"][0].reshape(PK, PK, D)
    uv = _np.empty((PK, 2, P, D), _np.float32)
    uv[:, 0] = u.transpose(1, 3, 2, 0).reshape(PK, P, D)
    uv[:, 1] = v.transpose(1, 0, 2)
    arrays["uv"] = uv
    arrays = {k: _np.ascontiguousarray(v) for k, v in arrays.items()}

    nc = _bacc.Bacc("TRN2", target_bir_lowering=False, num_devices=1)
    aps = {k: nc.dram_tensor(f"in_{k}", v.shape, _mybir.dt.from_np(v.dtype), kind="ExternalInput").ap()
           for k, v in arrays.items()}
    aps["out"] = nc.dram_tensor("out", (S, D), F32, kind="ExternalOutput").ap()
    dbg = {k: nc.dram_tensor(f"dbg_{k}", s, F32, kind="ExternalOutput").ap() for k, s in DEBUG.items()}
    program(nc, aps, dbg)
    r = _run(nc, [{f"in_{k}": v for k, v in arrays.items()}], core_ids=[0])
    return r.results[0]["out"][None]
```

```python
from contextlib import ExitStack

import numpy as np
import concourse.bass as bass
from concourse import mybir

F32 = mybir.dt.float32
F32R = mybir.dt.float32r
I32 = mybir.dt.int32
U32 = mybir.dt.uint32
ALU = mybir.AluOpType
ACT = mybir.ActivationFunctionType
AX = mybir.AxisListType.X

P = 128
S = 256
NT = S // P
D = 1024
DC = D // P
HD = 64
NH = 16
NKV = 4
GQA = NH // NKV
ROT = HD // 4
HALF = ROT // 2
THETA = 500000.0
EPS = 1e-6
CMP_LEN, CMP_STRIDE = 32, 16
NCMP = (S - CMP_LEN) // CMP_STRIDE + 1
CPAD = 32
CMP_HID = 4 * HD
NPAIR = CMP_LEN * HD // P
NEG = -1e30
FLOOR = -1e29
WT = 512
RING = 3
ARENA = 32768
KEEP = 48
TOK = 8
HA, HB = 8, 8
KVA = 2
PH, PK, PTOP = 8, 128, 16
BLK = 4

COLS = [("c", 8), ("c_2", 8), ("norm_g", 16), ("ada_b", 48), ("b_ada_2", 48), ("norm1_g_2", 8), ("norm2_g_2", 8),
        ("out_norm_a_2", 4), ("out_norm_b_2", 4), ("nsa_cmp_b1", 4)]
ROWS = [("nsa_q_norm", HD), ("nsa_k_norm", 3 * HD), ("moba_q_norm", HD), ("moba_k_norm", HD), ("nsa_gate_b", 3 * NH),
        ("sink_a_2", HA)]


def offsets(table):
    at, out = 0, {}
    for name, n in table:
        out[name] = (at, at + n)
        at += n
    return out, at


COL_AT, NCOL = offsets(COLS)
ROW_AT, NROW = offsets(ROWS)


class Line:

    def __init__(self, nc, stack, eng, name):
        self.eng, self.sem, self.count, self.seen = eng, stack.enter_context(nc.semaphore(name)), 0, {}
        self.name = name

    def need(self, *marks):
        for m in marks:
            if m is not None and self.seen.get(m[0].name, 0) < m[1]:
                self.eng.wait_ge(m[0], m[1])
                self.seen[m[0].name] = m[1]

    def did(self, inst):
        self.count += 1
        inst.then_inc(self.sem, 1)
        return (self.sem, self.count)

    def last(self):
        return (self.sem, self.count) if self.count else None


class Load:

    def __init__(self, nc, stack, name):
        self.sem, self.n = stack.enter_context(nc.semaphore(name)), 0

    def did(self, inst):
        self.n += 16
        inst.then_inc(self.sem, 16)
        return (self.sem, self.n)


class Bank:

    def __init__(self, tensor):
        self.t, self.free = tensor, None


def program(nc, a, dbg):
    with ExitStack() as st:
        build(nc, st, a, dbg)


def build(nc, st, a, dbg):
    V, A, G, T, Y = (Line(nc, st, e, n) for e, n in (
        (nc.vector, "vec"), (nc.scalar, "act"), (nc.gpsimd, "pool"), (nc.tensor, "pe"), (nc.sync, "sp")))
    ve, ac, po, pe, sy = nc.vector, nc.scalar, nc.gpsimd, nc.tensor, nc.sync

    def sb(name, shape, dt=F32):
        return st.enter_context(nc.sbuf_tensor(name, shape, dt))

    arena = sb("arena", [P, ARENA])
    top = [0]

    def carve(shape, stack, dt=F32):
        n = int(np.prod(shape[1:]))
        at = top[0]
        top[0] = at + n
        assert top[0] <= ARENA, (top[0], ARENA)
        stack.callback(top.__setitem__, 0, at)
        view = arena[0:shape[0], at:at + n]
        if dt != F32:
            view = view.bitcast(dt)
        names = "abcd"[:len(shape) - 1]
        if len(shape) == 2:
            return view
        return view.rearrange(f"p ({' '.join(names)}) -> p {' '.join(names)}", **dict(zip(names, shape[1:])))

    stores = []

    def load(dst, src, name, eng=None):
        return Load(nc, st, name).did((eng or sy).dma_start(dst, src))

    def meet():
        marks = [e.last() for e in (V, A, G, T)]
        for e in (V, A, G, T, Y):
            e.need(*[m for m in marks if m is not None])

    banks = [Bank(st.enter_context(nc.psum_tensor(f"bank{i}", [P, 512], F32))) for i in range(8)]
    turn = {"proj": 0}

    def proj_bank():
        b = banks[turn["proj"] % 2]
        turn["proj"] += 1
        return b

    x = sb("x_tok", [P, NT, D])
    ident = sb("ident", [P, P])
    cols = sb("cols", [P, NCOL])
    rows = sb("rows", [P, NROW])
    causal = sb("causal", [P, S])
    cmp_mask = sb("cmp_mask", [P, NT, CPAD])
    iota_k = sb("iota_k", [P, P])
    pos_i = sb("pos_i", [P, NT + 1], I32)
    cosd = sb("cosd", [P, NT + 1, ROT])
    sind = sb("sind", [P, NT + 1, ROT])
    silu_c = sb("silu_c", [P, 2, DC])
    ada = [sb("ada0", [P, 24]), sb("ada1", [P, 24]), sb("ada2", [P, 48])]
    gate_row = [sb(f"gate_row{i}", [P, D]) for i in range(2)]
    ones = sb("ones", [P, P])
    mod_a = sb("mod_a", [P, DC])
    stat = sb("stat", [P, 8])
    pow_half = sb("pow_half", [P, NH])
    hkT = sb("hkT", [P, 3, S])
    layers = ExitStack()
    st.callback(layers.close)
    raw_all = sb("raw", [P, 4, D])
    ring = [raw_all[:].rearrange("p a n -> p (a n)")] + [carve([P, DC * WT], layers) for i in range(RING - 1)]
    hT = carve([P, DC, S], layers)

    def col(name, lo=0, hi=None):
        s, e = COL_AT[name]
        return cols[:, s + lo:(e if hi is None else s + hi)]

    def row(name, lo=0, hi=None):
        s, e = ROW_AT[name]
        return rows[:, s + lo:(e if hi is None else s + hi)]

    m_cols = load(cols[:], a["cols"], "ld_cols")
    m_pos = load(pos_i[:], a["pos"], "ld_pos", ac)
    m_x = load(x[:], a["x"].rearrange("(t p) d -> p t d", p=P), "ld_x", ac)
    m_rows = load(rows[:], a["rows"].broadcast_to([P, NROW]), "ld_rows", ac)

    slot_load = [Load(nc, st, f"ld_ring{i}") for i in range(RING)]
    slot_free = [None] * RING
    streamed = [0]

    def stream(src, chunks, width):
        i = streamed[0] % RING
        streamed[0] += 1
        Y.need(slot_free[i])
        tile = ring[i][:, 0:chunks * width].rearrange("p (c n) -> p c n", c=chunks)
        return tile, slot_load[i].did(sy.dma_start(tile, src.rearrange("(c p) n -> p c n", p=P))), i

    m_z = G.did(po.memset(ident[:], 0.0))
    G.need(m_z)
    m_ident = G.did(po.affine_select(out=ident[:], in_=ident[:], compare_op=ALU.not_equal, fill=1.0, base=0,
                                     pattern=[[-1, P]], channel_multiplier=1))
    m_z = G.did(po.memset(causal[:], 0.0))
    m_p = G.did(po.memset(pow_half[:], -0.5))
    m_ones = G.did(po.memset(ones[:], 1.0))
    m_c0 = G.did(po.memset(cmp_mask[:], 0.0))
    G.need(m_z)
    m_causal = G.did(po.affine_select(out=causal[:, P:S], in_=causal[:, P:S], compare_op=ALU.is_ge, fill=NEG, base=0,
                                      pattern=[[-1, P]], channel_multiplier=1))
    G.need(m_c0)
    for t in range(NT):
        m = G.did(po.affine_select(out=cmp_mask[:, t, :], in_=cmp_mask[:, t, :], compare_op=ALU.is_ge, fill=NEG,
                                   base=t * P - (CMP_LEN - 1), pattern=[[-CMP_STRIDE, CPAD]], channel_multiplier=1))
    G.need(m)
    m_cmask = G.did(po.memset(cmp_mask[:, :, NCMP:CPAD], NEG))
    m_iota = G.did(po.iota(iota_k[:], [[1, P]], base=0, channel_multiplier=0, allow_small_or_imprecise_dtypes=True))
    m_pow = m_p

    freq = carve([P, HALF], layers)
    ang = carve([P, 4, NT + 1, HALF], layers)
    posf = carve([P, NT + 1], layers)
    for j in range(HALF):
        m_f = G.did(po.memset(freq[:, j:j + 1], float(np.float32(THETA) ** np.float32(-2.0 * j / ROT))))
    V.need(m_pos)
    m = V.did(ve.tensor_copy(posf[:], pos_i[:]))
    V.need(m, m_f)
    for t in range(NT + 1):
        m = V.did(ve.tensor_scalar(ang[:, 0, t, :], freq[:], posf[:, t:t + 1], None, ALU.mult))
    two_pi = 2.0 * np.pi
    parts, rest = [], two_pi
    for bits in (8, 8, 8):
        e = np.floor(np.log2(rest)) + 1 - bits
        p = np.floor(rest / 2.0 ** e) * 2.0 ** e
        parts.append(float(p))
        rest -= p
    parts.append(float(np.float32(rest)))
    magic = float(1.5 * 2 ** 23)
    V.need(m)
    m = V.did(ve.tensor_scalar(ang[:, 1], ang[:, 0], float(1.0 / two_pi), magic, ALU.mult, ALU.add))
    V.need(m)
    m = V.did(ve.tensor_scalar(ang[:, 1], ang[:, 1], -magic, None, ALU.add))
    for p in parts:
        V.need(m)
        m = V.did(ve.scalar_tensor_tensor(out=ang[:, 0], in0=ang[:, 1], scalar=-p, in1=ang[:, 0], op0=ALU.mult,
                                          op1=ALU.add))
    V.need(m)
    pi32 = 3.1415925
    m = V.did(ve.tensor_scalar(ang[:, 0], ang[:, 0], pi32, -pi32, ALU.min, ALU.max))
    V.need(m)
    m = V.did(ve.scalar_tensor_tensor(out=ang[:, 2], in0=ang[:, 0], scalar=-1.0, in1=ang[:, 0], op0=ALU.mult,
                                      op1=ALU.min))
    V.need(m)
    m_r = V.did(ve.tensor_scalar(ang[:, 2], ang[:, 2], float(np.pi / 2), None, ALU.add))
    A.need(m_r)
    m_cos = A.did(ac.activation(ang[:, 3], ang[:, 2], ACT.Sin))
    m_sin = A.did(ac.activation(sind[:, :, HALF:ROT], ang[:, 0], ACT.Sin))
    V.need(m_cos, m_sin)
    V.did(ve.tensor_copy(cosd[:, :, 0:HALF], ang[:, 3]))
    V.did(ve.tensor_copy(cosd[:, :, HALF:ROT], ang[:, 3]))
    m_rope = V.did(ve.tensor_scalar(sind[:, :, 0:HALF], sind[:, :, HALF:ROT], -1.0, None, ALU.mult))

    A.need(m_cols)
    A.did(ac.activation(silu_c[:, 0, :], col("c"), ACT.Silu))
    m_silu = A.did(ac.activation(silu_c[:, 1, :], col("c_2"), ACT.Silu))

    ada_acc = [carve([P, WT], layers) for _ in range(2)]
    ada_turn = [0]
    acc_read = [None, None]

    def ada_tile(layer, j):
        src = a["ada_w"][layer] if layer < 2 else a["w_ada_2"]
        w, m_w, slot = stream(src[:, j * WT:(j + 1) * WT], DC, WT)
        k = ada_turn[0] % 2
        ada_turn[0] += 1
        acc = ada_acc[k]
        V.need(m_w, m_silu, acc_read[k])
        m = V.did(ve.tensor_scalar(acc, w[:, 0, :], silu_c[:, layer // 2, 0:1], None, ALU.mult))
        for c in range(1, DC):
            V.need(m)
            m = V.did(ve.scalar_tensor_tensor(out=acc, in0=w[:, c, :], scalar=silu_c[:, layer // 2, c:c + 1], in1=acc,
                                              op0=ALU.mult, op1=ALU.add))
        slot_free[slot] = m
        b = proj_bank()
        if j % 6 < 4:
            T.need(b.free, m, m_ones)
            for i in range(4):
                last = pe.matmul(b.t[:, i:i + 1], acc[:, i * P:(i + 1) * P], ones[:, 0:1], start=True, stop=True)
            m = acc_read[k] = T.did(last)
            bias = col("ada_b", 24 * layer, 24 * layer + 24) if layer < 2 else col("b_ada_2")
            V.need(m, m_cols)
            b.free = V.did(ve.tensor_tensor(ada[layer][:, 4 * j:4 * j + 4], b.t[:, 0:4], bias[:, 4 * j:4 * j + 4], ALU.add))
        else:
            half = j % 6 - 4
            bsrc = a["ada_b"][layer:layer + 1] if layer < 2 else a["b_ada_2"]
            Y.need(bias_read[0])
            bias_load[0] = ld_bias.did(sy.dma_start(gate_bias, bsrc[:, j * WT:(j + 1) * WT]))
            T.need(b.free, m, m_ones, bias_load[0])
            pe.matmul(b.t[:], ones[:], acc, start=True, stop=False)
            m = acc_read[k] = bias_read[0] = T.did(pe.matmul(b.t[:], ones[0:1, :], gate_bias, start=False, stop=True))
            A.need(m, gate_read[gate_of(layer, j)])
            b.free = A.did(ac.activation(gate_row[gate_of(layer, j)][:, half * 512:(half + 1) * 512], b.t[:], ACT.Copy))
        return b.free

    def gate_of(layer, j):
        return 1 if layer == 1 or j >= 6 else 0

    gate_bias = carve([P, WT], layers)[0:1, :]
    ld_bias = Load(nc, st, "ld_bias")
    bias_load, bias_read, gate_read = [None], [None], [None, None]

    fillers = [(1, j) for j in range(6)] + [(2, j) for j in (0, 1, 2, 3)] + ["layer 1"] + \
        [(2, j) for j in (4, 5, 6, 7, 8, 9)] + ["layer 2"] + [(2, 10), (2, 11)]
    ada_mark = {}

    def filler(n=1):
        for _ in range(n):
            if fillers and not isinstance(fillers[0], str):
                l, j = fillers.pop(0)
                ada_mark[l, j] = ada_tile(l, j)

    def fillers_up_to(tag):
        while fillers and fillers[0] != tag:
            filler()
        if fillers:
            fillers.pop(0)

    for j in range(6):
        ada_mark[0, j] = ada_tile(0, j)

    def row_rstd(dst, src, width, marks, scratch):
        V.need(*marks)
        m = V.did(ve.tensor_tensor_reduce(out=scratch, in0=src, in1=src, scale=1.0, scalar=0.0, op0=ALU.mult,
                                          op1=ALU.add, accum_out=dst))
        V.need(m)
        m = V.did(ve.tensor_scalar(dst, dst, 1.0 / width, EPS, ALU.mult, ALU.add))
        G.need(m, m_pow)
        return G.did(po.tensor_tensor(dst, dst, pow_half[:, 0:1], ALU.pow))

    def to_columns(src, marks, put):
        for half in range(2):
            b = proj_bank()
            T.need(b.free, m_ident, *marks)
            for i in range(4):
                c = 4 * half + i
                last = pe.transpose(b.t[:, i * P:(i + 1) * P], src[:, c * P:(c + 1) * P], ident[:])
            m = T.did(last)
            b.free = put(half, b.t, m)

    def modulated(layer, norm, shift, scale, stack, m_in):
        xn = carve([P, D], stack)
        V.need(*[ada_mark[layer, j] for j in range(shift // 4, shift // 4 + 4)])
        m_mod = V.did(ve.scalar_tensor_tensor(out=mod_a[:], in0=ada[layer][:, scale:scale + DC], scalar=1.0, in1=norm,
                                              op0=ALU.add, op1=ALU.mult))
        m_h = None
        for t in range(NT):
            V.need(T.last())
            m = row_rstd(stat[:, t:t + 1], x[:, t, :], D, m_in, xn[:])
            V.need(m)
            m = V.did(ve.tensor_scalar(xn[:], x[:, t, :], stat[:, t:t + 1], None, ALU.mult))

            def put(half, bank, m_t):
                V.need(m_t, m_mod)
                A.need(m_t, m_mod)
                for i in range(4):
                    c = 4 * half + i
                    dst = hT[:, c, t * P:(t + 1) * P]
                    m = V.did(ve.tensor_scalar(dst, bank[:, i * P:(i + 1) * P], mod_a[:, c:c + 1],
                                               ada[layer][:, shift + c:shift + c + 1], ALU.mult, ALU.add))
                return m

            to_columns(xn, [m], put)
        return V.last()

    def project(src, width, m_h, use):
        w, m_w, slot = stream(src, DC, width)
        for t in range(NT):
            b = proj_bank()
            T.need(b.free, m_w, m_h)
            for c in range(DC):
                last = pe.matmul(b.t[:, 0:width], hT[:, c, t * P:(t + 1) * P], w[:, c, :], start=c == 0,
                                 stop=c == DC - 1)
            m = T.did(last)
            slot_free[slot] = m
            b.free = use(t, b.t[:, 0:width], m)

    def project_cols(src, width, m_h, use):
        w, m_w, slot = stream(src, DC, width)
        for i in range(width // P):
            b = proj_bank()
            T.need(b.free, m_w, m_h)
            for c in range(DC):
                last = pe.matmul(b.t[:, 0:S], w[:, c, i * P:(i + 1) * P], hT[:, c, :], start=c == 0, stop=c == DC - 1)
            m = T.did(last)
            slot_free[slot] = m
            b.free = use(i, b.t[:, 0:S], m)

    hn = sb("head_ms", [P, NH])

    def head_norm(src, dst, n, g, tab, post, tmp, marks, g_heads=None):
        s3, d3, t3 = (v.rearrange("p (h d) -> p h d", d=HD) for v in (src, dst, tmp))
        np_ = src.shape[0]
        A.need(*marks)
        m = A.did(ac.activation(tmp, src, ACT.Square))
        V.need(m, *marks)
        m = V.did(ve.tensor_reduce(hn[0:np_, 0:n], t3, AX, ALU.add))
        V.need(m)
        m = V.did(ve.tensor_scalar(hn[0:np_, 0:n], hn[0:np_, 0:n], 1.0 / HD, EPS, ALU.mult, ALU.add))
        G.need(m, m_pow)
        m = G.did(po.tensor_tensor(hn[0:np_, 0:n], hn[0:np_, 0:n], pow_half[0:np_, 0:n], ALU.pow))
        V.need(m)
        m_src = V.did(ve.tensor_tensor(d3, s3, hn[0:np_, 0:n].unsqueeze(2).broadcast_to([np_, n, HD]), ALU.mult))
        V.need(m_src, m_rows)
        m = V.did(ve.scalar_tensor_tensor(out=d3, in0=d3, scalar=post, in1=g[0:np_, :].unsqueeze(1).broadcast_to([np_, n, HD]),
                                          op0=ALU.mult, op1=ALU.mult))
        cc = cosd[0:np_, tab, :].unsqueeze(1).broadcast_to([np_, n, ROT])
        G.need(m, m_rope)
        s_lo = sind[0:np_, tab, 0:HALF].unsqueeze(1).broadcast_to([np_, n, HALF])
        s_hi = sind[0:np_, tab, HALF:ROT].unsqueeze(1).broadcast_to([np_, n, HALF])
        G.did(po.tensor_tensor(t3[:, :, ROT:ROT + HALF], d3[:, :, HALF:ROT], s_lo, ALU.mult))
        G.did(po.tensor_tensor(t3[:, :, ROT + HALF:2 * ROT], d3[:, :, 0:HALF], s_hi, ALU.mult))
        m = G.did(po.tensor_tensor(t3[:, :, 0:ROT], d3[:, :, 0:ROT], cc, ALU.mult))
        G.need(m)
        return m_src, G.did(po.tensor_tensor(d3[:, :, 0:ROT], t3[:, :, 0:ROT], t3[:, :, ROT:2 * ROT], ALU.add))

    def q_tile_use(qT, j, tab_g, bufs):
        def use(t, ps, m):
            qn, tmp = bufs[t]
            V.need(T.last())
            m_src, m = head_norm(ps, qn[:], 8, tab_g, t, HD ** -0.5, tmp[:], [m])
            b = proj_bank()
            T.need(b.free, m, m_ident)
            for i in range(4):
                last = pe.transpose(b.t[:, i * P:(i + 1) * P], qn[:, i * P:(i + 1) * P], ident[:])
            m = T.did(last)
            A.need(m)
            b.free = A.did(ac.activation(qT[:, 4 * j:4 * j + 4, t * P:(t + 1) * P],
                                         b.t[:].rearrange("p (i n) -> p i n", i=4), ACT.Copy))
            return m_src
        return use

    def kv_tile_use(kT, v_sb, g, bufs):
        def use(t, ps, m):
            kn, tmp = bufs[t]
            dup = kn[:, 2 * P:4 * P + 2 * P]
            V.need(T.last())
            m_src, mk = head_norm(ps[:, 0:NKV * HD], kn[:, 0:NKV * HD], NKV, g, t, 1.0, tmp[:, 0:NKV * HD], [m])
            A.need(m_src)
            m_v = A.did(ac.activation(v_sb[:, t, :], ps[:, NKV * HD:2 * NKV * HD], ACT.Copy))
            G.need(mk)
            mk = G.did(po.tensor_copy(dup.rearrange("p (g u d) -> p g u d", g=NKV, u=2),
                                      kn[:, 0:NKV * HD].rearrange("p (g d) -> p g d", g=NKV).unsqueeze(2).broadcast_to(
                                          [P, NKV, 2, HD])))
            b = proj_bank()
            T.need(b.free, mk, m_ident)
            for i in range(NKV):
                last = pe.transpose(b.t[:, i * P:(i + 1) * P], dup[:, i * P:(i + 1) * P], ident[:])
            m = T.did(last)
            V.need(m)
            b.free = V.did(ve.tensor_copy(kT[:, :, t * P:(t + 1) * P], b.t[:].rearrange("p (i n) -> p i n", i=NKV)))
            return m_v
        return use

    soft = {k: [carve([P, 512], layers) for i in range(2)] for k in ("scores", "probs", "probsT")}
    nmax = sb("nmax", [P, NT, NH])
    rsum = sb("rsum", [P, NT, NH])
    soft_read = {"scores": [None, None], "probs": [None, None], "probsT": [None, None]}

    def attend(tag, heads, q_of, k_of, v_of, bias_of, first_of, causal_keys, marks, done, fill):
        units = []
        for t in range(NT):
            w = P if causal_keys and t == 0 else S
            per = 512 // w
            by = [[h for h in heads if h % 2 == par] for par in (0, 1)]
            cut = [[hs[i:i + per] for i in range(0, len(hs), per)] for hs in by]
            for i in range(len(cut[0])):
                for par in (0, 1):
                    units.append((t, w, cut[par][i]))
        n = len(units)
        m_sc, m_ex, m_tr, m_cp = {}, {}, {}, {}

        def scores(u):
            t, w, hs = units[u]
            b = banks[2 + u % 2]
            T.need(b.free, *marks)
            for j, h in enumerate(hs):
                last = pe.matmul(b.t[:, j * w:(j + 1) * w], q_of(h, t), k_of(h, w), start=True, stop=True)
            m_sc[u] = T.did(last)
            V.need(m_sc[u], soft_read["scores"][u % 2])
            for j, h in enumerate(hs):
                m = V.did(ve.tensor_tensor_reduce(
                    out=soft["scores"][u % 2][:, j * w:(j + 1) * w], in0=b.t[:, j * w:(j + 1) * w],
                    in1=bias_of(h, t, w), scale=-1.0, scalar=first_of(h), op0=ALU.add, op1=ALU.min,
                    accum_out=nmax[:, t, h:h + 1]))
            b.free = m
            A.need(m, soft_read["probs"][u % 2])
            for j, h in enumerate(hs):
                m = A.did(ac.activation(soft["probs"][u % 2][:, j * w:(j + 1) * w],
                                        soft["scores"][u % 2][:, j * w:(j + 1) * w], ACT.Exp, scale=-1.0,
                                        bias=nmax[:, t, h:h + 1], accum_out=rsum[:, t, h:h + 1]))
            soft_read["scores"][u % 2] = m
            m_ex[u] = m

        def turned(u):
            t, w, hs = units[u]
            b = banks[4 + u % 2]
            T.need(b.free, m_ex[u])
            for i in range(len(hs) * w // P):
                last = pe.transpose(b.t[:, i * P:(i + 1) * P], soft["probs"][u % 2][:, i * P:(i + 1) * P], ident[:])
            m_tr[u] = T.did(last)
            soft_read["probs"][u % 2] = m_tr[u]
            V.need(m_tr[u], soft_read["probsT"][u % 2])
            b.free = m_cp[u] = V.did(ve.tensor_copy(soft["probsT"][u % 2][:], b.t[:]))

        def outputs(u):
            t, w, hs = units[u]
            T.need(m_cp[u], banks[6].free, banks[7].free)
            for j, h in enumerate(hs):
                o = banks[6 + h // 8].t[:, (h % 8) * HD:(h % 8 + 1) * HD]
                for k in range(w // P):
                    at = (j * (w // P) + k) * P
                    last = pe.matmul(o, soft["probsT"][u % 2][:, at:at + P], v_of(h, k), start=k == 0, stop=k == w // P - 1)
            m = T.did(last)
            soft_read["probsT"][u % 2] = m
            if u + 1 == n or units[u + 1][0] != t:
                banks[6].free = banks[7].free = done(t, m)

        for u in range(n + 2):
            if u < n:
                scores(u)
            if 0 <= u - 1 < n:
                turned(u - 1)
            if 0 <= u - 2 < n:
                outputs(u - 2)
            if fill and u % fill == fill - 1:
                filler()

    def o_heads(t_ap):
        return t_ap.rearrange("p (h d) -> p h d", d=HD)

    def gated_out(tag, o, z, w_src, layer, first, stack, m_o, norm_cols=None):
        ozT = hT
        gate = 1 if layer == 1 else 0
        m_g = ada_mark[layer, 5]
        m_t = None
        for t in range(NT):
            V.need(*m_o)
            m = V.did(ve.tensor_tensor(o[:, t, :], o[:, t, :], z[:, t, :], ALU.mult)) if z is not None else m_o[0]

            def put(half, bank, m_t):
                if norm_cols is None:
                    A.need(m_t)
                    return A.did(ac.activation(ozT[:, 4 * half:4 * half + 4, t * P:(t + 1) * P],
                                               bank[:].rearrange("p (i n) -> p i n", i=4), ACT.Copy))
                V.need(m_t)
                for i in range(4):
                    c = 4 * half + i
                    m = V.did(ve.tensor_scalar(ozT[:, c, t * P:(t + 1) * P], bank[:, i * P:(i + 1) * P],
                                               norm_cols[:, c:c + 1], None, ALU.mult))
                return m

            to_columns(o[:, t, :], [m, *m_o], put)
        m_ready = [A.last(), V.last()]
        tmp = carve([P, 512], stack)
        for j in range(2):
            w, m_w, slot = stream(w_src[:, j * WT:(j + 1) * WT], DC, WT)
            for t in range(NT):
                b = proj_bank()
                T.need(b.free, m_w, *m_ready)
                for c in range(DC):
                    last = pe.matmul(b.t[:], ozT[:, c, t * P:(t + 1) * P], w[:, c, :], start=c == 0, stop=c == DC - 1)
                m = T.did(last)
                slot_free[slot] = m
                V.need(m, m_g, V.last())
                b.free = V.did(ve.tensor_tensor(tmp[:], b.t[:], gate_row[gate][:, j * 512:(j + 1) * 512], ALU.mult))
                gate_read[gate] = b.free
                V.need(b.free)
                V.did(ve.tensor_tensor(x[:, t, j * 512:(j + 1) * 512], x[:, t, j * 512:(j + 1) * 512], tmp[:], ALU.add))
        return V.last()

    def simple_done(o, scale, with_gates=None, marks=()):
        def done(t, m):
            V.need(m, A.last(), *marks)
            m = V.did(ve.tensor_scalar(scale[:, t, :], rsum[:, t, :], 1e-30, None, ALU.max))
            V.need(m)
            m = V.did(ve.reciprocal(scale[:, t, :], scale[:, t, :]))
            if with_gates is not None:
                V.need(m)
                m = V.did(ve.tensor_tensor(scale[:, t, :], scale[:, t, :], with_gates[:, t, :], ALU.mult))
            V.need(m)
            for half in range(2):
                sc = scale[:, t, 8 * half:8 * half + 8].unsqueeze(2).broadcast_to([P, 8, HD])
                if with_gates is None:
                    m = V.did(ve.tensor_tensor(o_heads(o[:, t, 512 * half:512 * half + 512]), o_heads(banks[6 + half].t[:]),
                                               sc, ALU.mult))
                else:
                    V.need(G.last())
                    m = V.did(ve.tensor_tensor(o_heads(soft_add[:, half * 512:half * 512 + 512]),
                                               o_heads(banks[6 + half].t[:]), sc, ALU.mult))
                    G.need(m, V.last())
                    G.did(po.tensor_tensor(o[:, t, 512 * half:512 * half + 512], o[:, t, 512 * half:512 * half + 512],
                                           soft_add[:, half * 512:half * 512 + 512], ALU.add))
            return m
        return done

    soft_add = carve([P, D], layers)[:]

    def causal_bias(h, t, w):
        return causal[:, P:S] if w == P else causal[:]

    with ExitStack() as s0:
        w_in = a["nsa_w_in"]
        m_h = modulated(0, col("norm_g", 0, 8), 0, 8, s0, [m_x])
        qT = carve([P, NH // 2, S], s0)
        kTs = [carve([P, NKV, S], s0) for i in range(2)]
        vs = [carve([P, NT, NKV * HD], s0) for i in range(2)]
        bufs = [(carve([P, 6 * P], s0), carve([P, 512], s0)) for t in range(NT)]
        qbufs = [(b[0][:, 0:512], b[1]) for b in bufs]
        z = carve([P, NT, D], s0)
        gates = carve([P, 3, NT, NH], s0)
        gtmp = carve([P, 3 * NH], s0)
        o = carve([P, NT, D], s0)
        scale = carve([P, NT, NH], s0)
        x2 = carve([P, NKV, P], s0)
        xpe = carve([P, NPAIR, NKV, NCMP], s0)
        hid = carve([P, 2, NKV, CPAD], s0)
        pe_sb = carve([P, 2, NPAIR], s0)
        w2 = carve([P, 2, 2, HD], s0)
        kc_n = carve([P, 2 * HD], s0)
        kc_t = carve([P, HD], s0)
        kcT = carve([P, P], s0)
        vbd = carve([P, NKV, HD], s0)
        m_pe = load(pe_sb[:], a["cmp_pe"], "ld_pe", ac)
        m_w2 = load(w2[:], a["nsa_cmp_w2"].rearrange("i (c p) d -> p i c d", p=P), "ld_w2", ac)
        mz1 = G.did(po.memset(hid[:], 0.0))
        mz2 = G.did(po.memset(vbd[:], 0.0))

        def x2_use(i2):
            def use(blk, ps, m):
                V.need(m, T.last(), G.last())
                for g2 in range(2):
                    src = ps[g2 * HD:(g2 + 1) * HD, :].rearrange("p (m u) -> p u m", u=2)
                    for par in range(2):
                        mm = V.did(ve.tensor_copy(x2[par * HD:(par + 1) * HD, 2 * blk + g2, :], src[:, par, :]))
                return mm
            return use

        for i in range(2):
            lo = NH * HD + i * NKV * HD
            project_cols(w_in[:, lo:lo + NKV * HD], NKV * HD, m_h, x2_use(i))
            V.need(V.last(), m_pe, T.last())
            for g in range(NKV):
                flat = x2[:, g, :]
                for c0 in (0, 8):
                    src = x2[:, g, c0:c0 + 8 * NCMP].rearrange("p (n c) -> p c n", c=8)
                    m = V.did(ve.tensor_tensor(xpe[:, c0:c0 + 8, g, :], src,
                                               pe_sb[:, i, c0:c0 + 8].unsqueeze(2).broadcast_to([P, 8, NCMP]), ALU.add))
            m_xpe = m
            w1, m_w, slot = stream(a["nsa_cmp_w1"][i], NPAIR, CMP_HID)
            b = proj_bank()
            T.need(b.free, m_w, m_xpe)
            for hb in range(2):
                for c in range(NPAIR):
                    last = pe.matmul(b.t[:, hb * 64:hb * 64 + NKV * NCMP], w1[:, c, hb * P:(hb + 1) * P],
                                     xpe[:, c, :, :].rearrange("p g n -> p (g n)"), start=c == 0, stop=c == NPAIR - 1)
            m = T.did(last)
            slot_free[slot] = m
            A.need(m, mz1, T.last(), m_cols)
            for hb in range(2):
                m = A.did(ac.activation(hid[:, hb, :, 0:NCMP],
                                        b.t[:, hb * 64:hb * 64 + NKV * NCMP].rearrange("p (g n) -> p g n", g=NKV),
                                        ACT.Gelu_apprx_tanh, bias=col("nsa_cmp_b1", 2 * i + hb, 2 * i + hb + 1)))
            b.free = m
            b = proj_bank()
            T.need(b.free, m, m_w2)
            for hb in range(2):
                last = pe.matmul(b.t[:, 0:HD], hid[:, hb, :, :].rearrange("p g n -> p (g n)"), w2[:, i, hb, :],
                                 start=hb == 0, stop=hb == 1)
            m = T.did(last)
            if i == 0:
                _, mk = head_norm(b.t[:, 0:HD], kc_n[:, 0:HD], 1, row("nsa_k_norm", 0, HD), NT, 1.0, kc_t[:], [m])
                b.free = mk
                G.need(mk)
                mk = G.did(po.tensor_copy(kc_n[:, HD:2 * HD], kc_n[:, 0:HD]))
                b2 = proj_bank()
                T.need(b2.free, mk, m_ident)
                m = T.did(pe.transpose(b2.t[:, 0:P], kc_n[:], ident[:]))
                V.need(m)
                b2.free = m_kc = V.did(ve.tensor_copy(kcT[:], b2.t[:, 0:P]))
            else:
                V.need(m, mz2)
                for g in range(NKV):
                    m = V.did(ve.tensor_copy(vbd[g * CPAD:(g + 1) * CPAD, g, :], b.t[g * CPAD:(g + 1) * CPAD, 0:HD]))
                b.free = m_vc = m

        for i in range(2):
            lo = NH * HD + (2 + 2 * i) * NKV * HD
            project(w_in[:, lo:lo + WT], WT, m_h,
                    kv_tile_use(kTs[i], vs[i], row("nsa_k_norm", (i + 1) * HD, (i + 2) * HD), bufs))
        for j in range(2):
            project(w_in[:, j * WT:(j + 1) * WT], WT, m_h, q_tile_use(qT, j, row("nsa_q_norm"), qbufs))
        lo = NH * HD + 6 * NKV * HD

        def gate_use(t, ps, m):
            V.need(m, m_rows, A.last())
            m_s = V.did(ve.tensor_tensor(gtmp[:], ps, row("nsa_gate_b"), ALU.add))
            A.need(m_s)
            A.did(ac.activation(gates[:, :, t, :], gtmp[:].rearrange("p (h b) -> p b h", b=3), ACT.Sigmoid))
            return m_s

        project(w_in[:, lo:lo + 3 * NH], 3 * NH, m_h, gate_use)

        def z_use(j, z):
            def use(t, ps, m):
                A.need(m)
                return A.did(ac.activation(z[:, t, j * 512:(j + 1) * 512], ps, ACT.Silu))
            return use

        for j in range(2):
            at = lo + 3 * NH + j * WT
            project(w_in[:, at:at + WT], WT, m_h, z_use(j, z))
        m_ready = [V.last(), A.last(), G.last()]

        smc = carve([P, 2, 2 * NKV, CPAD], s0)
        red = carve([P, 3, NH], s0)
        for t in range(NT):
            T.need(banks[2].free, banks[3].free, m_kc, *m_ready)
            for par in range(2):
                for g in range(NKV):
                    for r2 in range(2):
                        h = GQA * g + 2 * r2 + par
                        half = slice(HD * par, HD * par + HD)
                        last = pe.matmul(banks[2 + par].t[:, (NKV * r2 + g) * CPAD:(NKV * r2 + g + 1) * CPAD],
                                         qT[half, h // 2, t * P:(t + 1) * P], kcT[half, g * CPAD:(g + 1) * CPAD],
                                         start=True, stop=True)
                m = T.did(last)
            V.need(m, m_cmask, T.last())
            for par in range(2):
                m = V.did(ve.tensor_tensor(smc[:, par], banks[2 + par].t[:, 0:2 * NKV * CPAD].rearrange("p (h n) -> p h n", n=CPAD),
                                           cmp_mask[:, t, :].unsqueeze(1).broadcast_to([P, 2 * NKV, CPAD]), ALU.add))
                banks[2 + par].free = m
            sm3 = smc[:].rearrange("p a h n -> p (a h) n")
            V.need(m)
            m = V.did(ve.tensor_reduce(red[:, 0, :], sm3, AX, ALU.max))
            V.need(m)
            m = V.did(ve.tensor_scalar(red[:, 0, :], red[:, 0, :], FLOOR, None, ALU.max))
            V.need(m)
            m = V.did(ve.tensor_tensor(sm3, sm3, red[:, 0, :].unsqueeze(2).broadcast_to([P, NH, CPAD]), ALU.subtract))
            A.need(m)
            m = A.did(ac.activation(sm3, sm3, ACT.Exp))
            V.need(m)
            m = V.did(ve.tensor_reduce(red[:, 1, :], sm3, AX, ALU.add))
            for r in range(GQA):
                T.need(m, banks[4].free)
                last = pe.transpose(banks[4].t[:, r * P:(r + 1) * P],
                                    smc[:, r % 2, NKV * (r // 2):NKV * (r // 2 + 1)].rearrange("p g n -> p (g n)"), ident[:])
            m_t = T.did(last)
            V.need(m, m_t, T.last())
            m_c = V.did(ve.tensor_copy(soft["probsT"][0][:], banks[4].t[:]))
            banks[4].free = m_c
            m = V.did(ve.tensor_scalar(red[:, 1, :], red[:, 1, :], 1e-30, None, ALU.max))
            V.need(m)
            m = V.did(ve.reciprocal(red[:, 2, :], red[:, 1, :]))
            V.need(m)
            for par in range(2):
                r4 = red[:, 2, :].rearrange("p (a r g) -> p a r g", a=2, r=2)[:, par]
                g4 = gates[:, 0, t, :].rearrange("p (g r a) -> p a r g", a=2, r=2)[:, par]
                m = V.did(ve.tensor_tensor(r4, r4, g4, ALU.mult))
            T.need(m_c, banks[6].free, banks[7].free, m_vc)
            for r in range(GQA):
                last = pe.matmul(banks[6 + r // 2].t[:, (r % 2) * NKV * HD:(r % 2 + 1) * NKV * HD],
                                 soft["probsT"][0][:, r * P:(r + 1) * P], vbd[:].rearrange("p g d -> p (g d)"),
                                 start=True, stop=True)
            m_o = T.did(last)
            V.need(m_o, m)
            for r in range(GQA):
                src = banks[6 + r // 2].t[:, (r % 2) * NKV * HD:(r % 2 + 1) * NKV * HD].rearrange("p (g d) -> p g d", g=NKV)
                dst = o[:, t, :].rearrange("p (g r d) -> p r g d", g=NKV, r=GQA)[:, r]
                sc = red[:, 2, :].rearrange("p (a r g) -> p a r g", a=2, r=2)[:, r % 2, r // 2]
                m = V.did(ve.tensor_tensor(dst, src, sc.unsqueeze(2).broadcast_to([P, NKV, HD]), ALU.mult))
            banks[6].free = banks[7].free = m
            soft_read["probsT"][0] = m_o

        for i in range(2):
            half_of = lambda h: slice(HD * (h % 2), HD * (h % 2) + HD)
            attend(f"nsa{i}", list(range(NH)),
                   lambda h, t: qT[half_of(h), h // 2, t * P:(t + 1) * P],
                   lambda h, w: kTs[i][half_of(h), h // GQA, 0:w],
                   lambda h, k: vs[i][:, k, (h // GQA) * HD:(h // GQA + 1) * HD],
                   causal_bias, lambda h: 3e38, True, [*m_ready, m_causal],
                   simple_done(o, scale, gates[:, i + 1], marks=()), 4)
        m_x = gated_out("0", o, z, a["nsa_w_out"], 0, 16, s0, [V.last(), G.last()])
        if "x1" in dbg:
            Y.need(m_x)
            stores.append(load(dbg["x1"].rearrange("(t p) d -> p t d", p=P), x[:], "st_x1"))
        meet()

    with ExitStack() as s1:
        fillers_up_to("layer 1")
        w_in = a["moba_w_in"]
        m_h = modulated(1, col("norm_g", 8, 16), 0, 8, s1, [m_x])
        qT = carve([P, NH // 2, S], s1)
        kT = carve([P, NKV, S], s1)
        v1 = carve([P, NT, NKV * HD], s1)
        bufs = [(carve([P, 6 * P], s1), carve([P, 512], s1)) for t in range(NT)]
        qbufs = [(b[0][:, 0:512], b[1]) for b in bufs]
        z = carve([P, NT, D], s1)
        o = carve([P, NT, D], s1)
        scale = carve([P, NT, NH], s1)
        project(w_in[:, D:D + WT], WT, m_h, kv_tile_use(kT, v1, row("moba_k_norm"), bufs))
        for j in range(2):
            project(w_in[:, j * WT:(j + 1) * WT], WT, m_h, q_tile_use(qT, j, row("moba_q_norm"), qbufs))

        def z_use1(j):
            def use(t, ps, m):
                A.need(m)
                return A.did(ac.activation(z[:, t, j * 512:(j + 1) * 512], ps, ACT.Silu))
            return use

        for j in range(2):
            project(w_in[:, D + WT + j * WT:D + 2 * WT + j * WT], WT, m_h, z_use1(j))
        m_ready = [V.last(), A.last(), G.last()]
        half_of = lambda h: slice(HD * (h % 2), HD * (h % 2) + HD)
        attend("moba", list(range(NH)),
               lambda h, t: qT[half_of(h), h // 2, t * P:(t + 1) * P],
               lambda h, w: kT[half_of(h), h // GQA, 0:w],
               lambda h, k: v1[:, k, (h // GQA) * HD:(h // GQA + 1) * HD],
               causal_bias, lambda h: 3e38, True, m_ready, simple_done(o, scale), 3)
        m_x = gated_out("1", o, z, a["moba_w_out"], 1, 16, s1, [V.last(), G.last()])
        if "x2" in dbg:
            Y.need(m_x)
            stores.append(load(dbg["x2"].rearrange("(t p) d -> p t d", p=P), x[:], "st_x2"))
        meet()

    with ExitStack() as s2:
        fillers_up_to("layer 2")
        w_in = a["w_in_2"]
        bias_a = carve([P, HA, 3 * P], s2)
        bias_b = carve([P, NT, HB, S], s2)
        m_ba = load(bias_a[:], a["bias_a"], "ld_ba", ac)
        m_bb = load(bias_b[:], a["bias_b"], "ld_bb", ac)
        m_h = modulated(2, col("norm1_g_2"), 0, 8, s2, [m_x])
        qT = carve([P, NH // 2, S], s2)
        kaT = carve([P, KVA, S], s2)
        kbT = carve([P, HB // 2, S], s2)
        va = carve([P, NT, KVA * HD], s2)
        vb = carve([P, NT, HB * HD], s2)
        o = carve([P, NT, D], s2)
        scale = carve([P, NT, NH], s2)
        nsink = carve([P, HA], s2)
        esink = carve([P, NT, HA], s2)
        wa, wk = HA * HD, KVA * HD

        def q_use(first):
            def use(i, ps, m):
                A.need(m)
                return A.did(ac.activation(qT[:, first + i, :], ps, ACT.Copy, scale=HD ** -0.5))
            return use

        project_cols(w_in[:, 0:wa], wa, m_h, q_use(0))

        def ka_use(i, ps, m):
            V.need(m)
            for g in range(KVA):
                for dup in range(2):
                    mm = V.did(ve.tensor_copy(kaT[dup * HD:(dup + 1) * HD, g, :], ps[g * HD:(g + 1) * HD, :]))
            return mm

        project_cols(w_in[:, wa:wa + wk], wk, m_h, ka_use)

        def v_use(dst):
            def use(t, ps, m):
                V.need(m)
                return V.did(ve.tensor_copy(dst[:, t, :], ps))
            return use

        project(w_in[:, wa + wk:wa + 2 * wk], wk, m_h, v_use(va))
        at = wa + 2 * wk
        project_cols(w_in[:, at:at + WT], WT, m_h, q_use(HA // 2))

        def kb_use(i, ps, m):
            V.need(m)
            return V.did(ve.tensor_copy(kbT[:, i, :], ps))

        project_cols(w_in[:, at + WT:at + 2 * WT], WT, m_h, kb_use)
        project(w_in[:, at + 2 * WT:at + 3 * WT], WT, m_h, v_use(vb))
        V.need(m_rows)
        m_ns = V.did(ve.tensor_scalar(nsink[:], row("sink_a_2"), -1.0, None, ALU.mult))
        V.need(m_ns)
        m_ready = [V.last(), A.last(), G.last()]

        def bias_of(h, t, w):
            return bias_a[:, h, P * (1 - t):P * (3 - t)] if h < HA else bias_b[:, t, h - HA, :]

        def done2(t, m):
            V.need(m, A.last())
            m = V.did(ve.tensor_tensor(esink[:, t, :], row("sink_a_2"), nmax[:, t, 0:HA], ALU.add))
            A.need(m)
            m = A.did(ac.activation(esink[:, t, :], esink[:, t, :], ACT.Exp))
            V.need(m)
            m = V.did(ve.tensor_tensor(rsum[:, t, 0:HA], rsum[:, t, 0:HA], esink[:, t, :], ALU.add))
            return simple_done(o, scale)(t, m)

        attend("mix", list(range(NH)),
               lambda h, t: qT[half_of(h), h // 2, t * P:(t + 1) * P],
               lambda h, w: kaT[half_of(h), h // (HA // KVA), 0:w] if h < HA else kbT[half_of(h), (h - HA) // 2, 0:w],
               lambda h, k: va[:, k, (h // 4) * HD:(h // 4 + 1) * HD] if h < HA else vb[:, k, (h - HA) * HD:(h - HA + 1) * HD],
               bias_of, lambda h: nsink[:, h:h + 1] if h < HA else 3e38, False, [*m_ready, m_ba, m_bb], done2, 8)
        V.need(m_ba, m_bb)
        for t in range(NT):
            for half in range(2):
                part = o[:, t, 512 * half:512 * half + 512]
                m = row_rstd(stat[:, 2 + 2 * t + half:3 + 2 * t + half], part, 512, [V.last()], soft_add[:, 0:512])
                V.need(m)
                V.did(ve.tensor_scalar(part, part, stat[:, 2 + 2 * t + half:3 + 2 * t + half], None, ALU.mult))
        norm_cols = cols[:, COL_AT["out_norm_a_2"][0]:COL_AT["out_norm_b_2"][1]]
        m_x = gated_out("2", o, None, a["w_out_2"], 2, 16, s2, [V.last(), G.last()], norm_cols)
        if "x3" in dbg:
            Y.need(m_x)
            stores.append(load(dbg["x3"].rearrange("(t p) d -> p t d", p=P), x[:], "st_x3"))
        meet()

    split = {}
    for name in ("u", "v"):
        split[name] = [[sb(f"{name}_{part}{k}", [P, D], F32R) for k in range(2)] for part in ("hi", "lo")]
    raw = {name: [raw_all[:, 2 * n + k, :] for k in range(2)] for n, name in enumerate(("u", "v"))}
    h_hi, h_lo = sb("h_hi", [P, DC, S], F32R), sb("h_lo", [P, DC, S], F32R)
    a_hi, a_lo = ([sb(f"a_{part}{k}", [P, S], F32R) for k in range(2)] for part in ("hi", "lo"))

    def new_sem(name):
        return st.enter_context(nc.semaphore(name))

    s_load = {(n, k): new_sem(f"s_load_{n}{k}") for n in ("u", "v") for k in range(2)}
    s_uhi, s_ulo, s_vhi, s_vlo, s_z, s_gelu, s_a, s_out = (
        new_sem(n) for n in ("s_uhi", "s_ulo", "s_vhi", "s_vlo", "s_z", "s_gelu", "s_a", "s_out"))
    for e, s in ((ac, s_uhi), (po, s_ulo), (ac, s_vhi), (ve, s_vlo), (pe, s_z), (ac, s_gelu), (ve, s_a), (pe, s_out)):
        e.sem_inc(s, 2)
    mat = arena[:, 0:PK * S].rearrange("p (e t) -> p e t", e=PK)
    zbank, outb = banks[0:2], banks[4:8]

    def at(i, k):
        return i * 2 + k

    def load_block(name, i, k, s_split):
        sy.wait_ge(s_split, at(i, k) + 1)
        sy.dma_start(raw[name][k], a[name][bass.ds(at(i, k), 1)].rearrange("o p n -> (o p) n")).then_inc(s_load[name, k], 16)

    def split_hi(name, i, k, s_hi, s_used, first):
        ac.wait_ge(s_load[name, k], (i - first) * 16 + 16)
        ac.wait_ge(s_used, at(i, k) + 1)
        ac.activation(split[name][0][k][:], raw[name][k], ACT.Copy).then_inc(s_hi, 1)

    def split_lo(eng, name, i, k, s_hi, s_lo):
        eng.wait_ge(s_hi, at(i, k) + 3)
        eng.tensor_tensor(split[name][1][k][:], raw[name][k], split[name][0][k][:].bitcast(F32), ALU.subtract).then_inc(s_lo, 1)

    def z_product(b, slot):
        pe.wait_ge(s_ulo, b + 3)
        pe.wait_ge(s_gelu, b + 1)
        k = slot % 2
        u_hi, u_lo = (quad[slot][x].rearrange("p (c e) -> p c e", c=DC) for x in range(2))
        n = 0
        for c in range(DC):
            for u, h in ((u_hi, h_hi), (u_hi, h_lo), (u_lo, h_hi)):
                last = pe.matmul(zbank[k].t[:, 0:S], u[:, c, :], h[:, c, :], start=n == 0, stop=n == 3 * DC - 1)
                n += 1
        last.then_inc(s_z, 1)

    def out_product(i, k, start=False, stop=False):
        pe.wait_ge(s_vlo, at(i, k) + 3)
        pe.wait_ge(s_a, at(i, k) + 3)
        for t in range(NT):
            for n, (x, y) in enumerate(((a_hi, 0), (a_hi, 1), (a_lo, 0))):
                for h in range(2):
                    last = pe.matmul(outb[2 * t + h].t[:], x[k][:, t * P:(t + 1) * P],
                                     split["v"][y][k][:, h * 512:(h + 1) * 512], start=start and n == 0,
                                     stop=stop and n == 2, skip_group_check=True)
        last.then_inc(s_out, 1)

    def split_a(i, k, src, link):
        ve.wait_ge(s_out, at(i, k) + 1)
        ve.tensor_copy(a_hi[k][:], src).then_inc(link, 1)
        return lambda n: (ve.wait_ge(link, n), ve.tensor_tensor(a_lo[k][:], src, a_hi[k][:].bitcast(F32), ALU.subtract).then_inc(s_a, 1))

    def block_of(i, k):
        return mat[:, bass.ds(at(i, k), 1), :].rearrange("p o t -> p (o t)")

    quad = [(split[n][0][k][:], split[n][1][k][:]) for n in ("u", "v") for k in range(2)]
    s_quad = [new_sem(f"s_load_quad{k}") for k in range(4)]

    def quad_load(b, slot):
        if not isinstance(b, int):
            sy.wait_ge(s_ulo, b - 1)
        sy.dma_start(raw_all[:, slot, :], a["u"][bass.ds(b, 1)].rearrange("o p n -> (o p) n")).then_inc(s_quad[slot], 16)

    def quad_split(b, turn, slot):
        ac.wait_ge(s_quad[slot], turn * 16 + 16)
        if not isinstance(b, int):
            ac.wait_ge(s_z, b - 1)
        ac.activation(quad[slot][0], raw_all[:, slot, :], ACT.Copy).then_inc(s_uhi, 1)
        po.wait_ge(s_uhi, b + 3)
        po.tensor_tensor(quad[slot][1], raw_all[:, slot, :], quad[slot][0].bitcast(F32), ALU.subtract).then_inc(s_ulo, 1)

    def u_load(i, k):
        load_block("u", i, k, s_ulo)

    def u_split(i, k):
        split_hi("u", i, k, s_uhi, s_z, KEEP // 2 + 1)
        split_lo(po, "u", i, k, s_uhi, s_ulo)

    def v_split(i, k):
        load_block("v", i, k, s_vlo)
        split_hi("v", i, k, s_vhi, s_out, 0)
        split_lo(ve, "v", i, k, s_vhi, s_vlo)

    def after(i, k):
        return (i, 1) if k == 0 else (i + 1, 0)

    with ExitStack() as s3:
        m_h = modulated(2, col("norm2_g_2"), 24, 32, s3, [m_x])
        m_hh = V.did(ve.tensor_copy(h_hi[:], hT[:])) if not V.need(m_h) else None
        V.need(m_hh)
        m_hl = V.did(ve.tensor_tensor(h_lo[:], hT[:], h_hi[:].bitcast(F32), ALU.subtract))
        top[0] = max(top[0], KEEP * S)
        qsT = carve([P, 2 * PH, S], s3)
        keysT = carve([P, 2 * PH, PK], s3)
        Y.need(V.last(), T.last(), A.last(), G.last())
        m_keys = load(keysT, a["keysT"], "ld_keys")

        for j in range(4):
            def use(i, ps, m, j=j):
                A.need(m)
                return A.did(ac.activation(qsT[:, 4 * j + i, :], ps, ACT.Copy))
            project_cols(a["w_query_2"][:, j * WT:(j + 1) * WT], WT, m_h, use)
        m_q = A.last()
        sc = carve([P, NT, 2 * PH, PK], s3)
        sc2 = carve([P, 2, PK], s3)
        top_v = carve([P, PH, 2, PTOP], s3)
        top_i = carve([P, PH, 2, PTOP], s3, U32)
        top_f = carve([P, PH, 2, PTOP], s3)
        cand, eq = (qsT[:, 8 * x:8 * x + 8, :].rearrange("p (h) (i j) -> p h i j", j=PTOP) for x in range(2))
        cand2 = carve([P, 2, PTOP * PTOP], s3)
        best = carve([P, PH, PTOP], s3)
        best_i = carve([P, PH, PTOP], s3, U32)
        rank_u = carve([P, 2, PH, PTOP], s3, U32)
        rank = carve([P, 2, PH, PTOP], s3)
        hk = carve([P, NT, 3, PH, PTOP], s3)
        weight = carve([P, NT, PH, PTOP], s3)
        gsum = carve([P, PH], s3)

        def top16(src, work, vals, idx, marks):
            V.need(V.last(), *marks)
            m = V.did(ve.max(vals[:, 0:8], src))
            V.need(m)
            V.did(ve.max_index(idx[:, 0:8], vals[:, 0:8], src))
            m = V.did(ve.match_replace(work, vals[:, 0:8], src, -3.4e38))
            V.need(m)
            m = V.did(ve.max(vals[:, 8:16], work))
            V.need(m)
            return V.did(ve.max_index(idx[:, 8:16], vals[:, 8:16], work))

        m_sc = {}
        for t in range(NT):
            for q in range(4):
                b = banks[2 + q % 2]
                T.need(b.free, m_q, m_keys)
                for i in range(4):
                    hh = 4 * q + i
                    last = pe.matmul(b.t[:, i * PK:(i + 1) * PK], qsT[:, hh, t * P:(t + 1) * P], keysT[:, hh, :],
                                     start=True, stop=True)
                m = m_scored = T.did(last)
                A.need(m, V.last())
                b.free = m_sc[t, q] = A.did(ac.activation(sc[:, t, 4 * q:4 * q + 4, :],
                                                          b.t[:].rearrange("p (i n) -> p i n", i=4), ACT.Copy))

        for e in (T, Y, A, G):
            e.need(m_hl, T.last(), A.last())
        for k in range(4):
            quad_load(k, k)
            quad_split(k, 0, k)

        def kept_block(i, k, ahead):
            b = i * 4 + k
            z_product(b, k)
            ac.wait_ge(s_z, b + 3)
            ac.activation(mat[:, bass.ds(b, 1), :].rearrange("p o t -> p (o t)"), zbank[k % 2].t[:, 0:S],
                          ACT.Gelu_apprx_tanh).then_inc(s_gelu, 1)
            if ahead:
                if isinstance(b, int):
                    sy.wait_ge(s_ulo, b + 3)
                    ac.wait_ge(s_z, b + 3)
                quad_load(b + 4, k)
                quad_split(b + 4, i + 1, k)

        with nc.Fori(0, KEEP // 4 - 1, engines=(mybir.EngineType.SP, mybir.EngineType.Activation, mybir.EngineType.Pool,
                                                mybir.EngineType.PE)) as i:
            for k in range(4):
                kept_block(i, k, True)
        for k in range(4):
            kept_block(KEEP // 4 - 1, k, k < 2)

        for t in range(NT):
            for hh in range(2 * PH):
                m = top16(sc[:, t, hh, :], sc2[:, hh % 2, :], top_v[:, hh // 2, hh % 2, :], top_i[:, hh // 2, hh % 2, :],
                          [m_sc[t, hh // 4]])
            V.need(m)
            m = V.did(ve.tensor_copy(top_f, top_i))
            V.need(m, m_scored)
            m = V.did(ve.tensor_tensor(cand, top_v[:, :, 0, :].unsqueeze(3).broadcast_to([P, PH, PTOP, PTOP]),
                                       top_v[:, :, 1, :].unsqueeze(2).broadcast_to([P, PH, PTOP, PTOP]), ALU.add))
            for h in range(PH):
                m = top16(cand[:, h].rearrange("p i j -> p (i j)"), cand2[:, h % 2, :], best[:, h, :], best_i[:, h, :], [m])
            V.need(m)
            V.did(ve.tensor_scalar(rank_u[:, 0], best_i, 4, None, ALU.logical_shift_right))
            m = V.did(ve.tensor_scalar(rank_u[:, 1], best_i, 15, None, ALU.bitwise_and))
            V.need(m)
            m = V.did(ve.tensor_copy(rank, rank_u))
            for side in range(2):
                V.need(m, m_iota)
                m = V.did(ve.tensor_tensor(eq, rank[:, side].unsqueeze(3).broadcast_to([P, PH, PTOP, PTOP]),
                                           iota_k[:, 0:PTOP].unsqueeze(1).unsqueeze(1).broadcast_to([P, PH, PTOP, PTOP]),
                                           ALU.is_equal))
                V.need(m)
                m = V.did(ve.tensor_tensor(eq, eq, top_f[:, :, side, :].unsqueeze(2).broadcast_to([P, PH, PTOP, PTOP]),
                                           ALU.mult))
                V.need(m)
                m = V.did(ve.tensor_reduce(hk[:, t, side], eq, AX, ALU.add))
            V.need(m)
            m = V.did(ve.tensor_tensor(weight[:, t], best, best[:, :, 0:1].broadcast_to([P, PH, PTOP]), ALU.subtract))
        A.need(m)
        m = A.did(ac.activation(weight, weight, ACT.Exp))
        for t in range(NT):
            V.need(m, V.last())
            mm = V.did(ve.tensor_reduce(gsum, weight[:, t], AX, ALU.add))
            V.need(mm)
            mm = V.did(ve.reciprocal(gsum, gsum))
            V.need(mm)
            mm = V.did(ve.tensor_tensor(hk[:, t, 2], weight[:, t], gsum.unsqueeze(2).broadcast_to([P, PH, PTOP]), ALU.mult))
            b = banks[2 + t]
            T.need(mm, b.free)
            for i in range(3):
                last = pe.transpose(b.t[:, i * P:(i + 1) * P], hk[:, t, i].rearrange("p h k -> p (h k)"), ident[:])
            mm = T.did(last)
            V.need(mm)
            b.free = V.did(ve.tensor_copy(hkT[:, :, t * P:(t + 1) * P], b.t[:, 0:3 * P].rearrange("p (i n) -> p i n", i=3)))
        if "hk" in dbg:
            Y.need(V.last())
            stores.append(load(dbg["hk"], hkT[:], "st_hk"))
        meet()
    fillers_up_to(None)
    meet()
    layers.close()

    n_quad = S // TOK // 4
    s_oh, s_ohg, s_gm, s_gc, s_gx = (new_sem(n) for n in ("s_onehot", "s_onehot_g", "s_gatemm", "s_gatecopy", "s_gatemul"))
    raw_oh = raw_all[:].rearrange("p (k x) (j n) -> p k x j n", k=2, n=P)
    nq = TOK // 4
    for e, s, n in ((ve, s_oh, 8), (po, s_ohg, 4), (pe, s_gm, 4 * nq), (ac, s_gc, 4 * nq), (ve, s_gx, 4 * nq)):
        e.sem_inc(s, n)
    iota_w = iota_k[:].unsqueeze(1).broadcast_to([P, TOK, P])
    for e in (ve, ac, po):
        e.wait_ge(s_gelu, KEEP + 2)
        e.wait_ge(s_ulo, KEEP + 4)

    def one_hots(i, k):
        g = i * 4 + k

        def tokens(side):
            return hkT[:, side, bass.ds(g * TOK, TOK)].unsqueeze(2).broadcast_to([P, TOK, P])

        ve.wait_ge(s_gm, (g + 3) * nq)
        ve.tensor_tensor(raw_oh[:, k % 2, 1], iota_w, tokens(1), ALU.is_equal).then_inc(s_oh, 1)
        po.wait_ge(s_oh, g * 2 + 9)
        po.tensor_tensor(raw_oh[:, k % 2, 1], raw_oh[:, k % 2, 1], tokens(2), ALU.mult).then_inc(s_ohg, 1)
        ve.tensor_tensor(raw_oh[:, k % 2, 0], iota_w, tokens(0), ALU.is_equal).then_inc(s_oh, 1)

    def gate_group(i, k):
        g = i * 4 + k
        one_hots(i, k)
        pe.wait_ge(s_oh, g * 2 + 10)
        pe.wait_ge(s_ohg, g + 5)
        pe.wait_ge(s_gx, (g + 1) * nq)
        for q in range(nq):
            for j in range(4):
                last = pe.matmul(banks[nq * k + q].t[:, j * P:(j + 1) * P], raw_oh[:, k % 2, 0, 4 * q + j, :],
                                 raw_oh[:, k % 2, 1, 4 * q + j, :], start=True, stop=True)
            last.then_inc(s_gm, 1)
        for q in range(nq):
            ac.wait_ge(s_gm, (g + 4) * nq + q + 1)
            ac.activation(mat[:, KEEP:PK, bass.ds(g * TOK + 4 * q, 4)],
                          banks[nq * k + q].t[:].rearrange("p (k e) -> p e k", k=4)[:, KEEP:PK, :],
                          ACT.Copy).then_inc(s_gc, 1)

    def multiply(i, k):
        g = i * 4 + k
        for q in range(nq):
            ve.wait_ge(s_gc, (g + 4) * nq + q + 1)
            dst = mat[:, 0:KEEP, bass.ds(g * TOK + 4 * q, 4)]
            ve.tensor_tensor(dst, banks[nq * k + q].t[:].rearrange("p (k e) -> p e k", k=4)[:, 0:KEEP, :], dst,
                             ALU.mult).then_inc(s_gx, 1)

    gate_group(0, 0)
    gate_group(0, 1)
    for k in (2, 3):
        gate_group(0, k)
        multiply(0, k - 2)
    with nc.Fori(1, n_quad) as i:
        for k in range(4):
            gate_group(i, k)
            multiply(i if k >= 2 else i - 1, (k - 2) % 4)
    multiply(n_quad - 1, 2)
    multiply(n_quad - 1, 3)
    total = (S // TOK + 4) * nq
    for e in (ve, ac, pe, po, sy):
        e.wait_ge(s_gx, total)

    s_link = new_sem("s_link")
    ve.sem_inc(s_link, 2)

    def kept_a(i, k):
        split_a(i, k, block_of(i, k), s_link)(at(i, k) + 3)

    v_split(0, 0)
    kept_a(0, 0)
    kept_a(0, 1)
    v_split(0, 1)
    out_product(0, 0, start=True)
    with nc.Fori(0, KEEP // 2 - 1) as i:
        kept_a(i + 1, 0)
        v_split(i + 1, 0)
        out_product(i, 1)
        kept_a(i + 1, 1)
        v_split(i + 1, 1)
        out_product(i + 1, 0)
    last_kept = (KEEP // 2 - 1, 1)
    v_split(KEEP // 2, 0)
    z_product(KEEP, 0)
    out_product(*last_kept)

    zg = [hkT[:, k, :] for k in range(2)]
    s_mul = new_sem("s_mul")
    ve.sem_inc(s_mul, 2)

    def rest_block(i, k, ahead=2, stop=False):
        ac.wait_ge(s_z, at(i, k) + 3)
        ac.wait_ge(s_a, at(i, k) + 1)
        ac.activation(zg[k], zbank[k].t[:, 0:S], ACT.Gelu_apprx_tanh).then_inc(s_gelu, 1)
        ve.wait_ge(s_gelu, at(i, k) + 3)
        ve.tensor_tensor(zg[k], zg[k], block_of(i, k), ALU.mult).then_inc(s_mul, 1)
        if ahead >= 2:
            u_load(i + 1, k)
            u_split(i + 1, k)
        ve.wait_ge(s_mul, at(i, k) - KEEP + 3)
        split_a(i, k, zg[k], s_link)(at(i, k) + 3)
        if ahead >= 1:
            v_split(*after(i, k))
            z_product(at(i, k) + 1, 1 - k)
        out_product(i, k, stop=stop)

    with nc.Fori(KEEP // 2, PK // 2 - 1) as i:
        rest_block(i, 0)
        rest_block(i, 1)
    rest_block(PK // 2 - 1, 0, ahead=1)
    rest_block(PK // 2 - 1, 1, ahead=0, stop=True)

    for e in (ve, ac, pe):
        e.wait_ge(s_out, PK + 2)
    tmp = arena[:, 0:D]
    sy.wait_ge(s_ulo, PK + 2)
    final_g = raw_all[:, 0, :]
    m_fg = load(final_g, a["final_g"].broadcast_to([P, D]), "ld_final_g")
    V.need(*[m for m in (A.last(),) if m])
    for t in range(NT):
        V.need(V.last())
        for h in range(2):
            m = V.did(ve.tensor_tensor(tmp[:, h * 512:(h + 1) * 512], outb[2 * t + h].t[:],
                                       gate_row[1][:, h * 512:(h + 1) * 512], ALU.mult))
        V.need(m)
        m = V.did(ve.tensor_tensor(x[:, t, :], x[:, t, :], tmp, ALU.add))
        m = row_rstd(stat[:, t:t + 1], x[:, t, :], D, [m], tmp)
        V.need(m, m_fg)
        m = V.did(ve.scalar_tensor_tensor(out=x[:, t, :], in0=x[:, t, :], scalar=stat[:, t:t + 1],
                                          in1=final_g, op0=ALU.mult, op1=ALU.mult))
        Y.need(m)
        stores.append(load(a["out"].rearrange("(t p) d -> t p d", p=P)[t], x[:, t, :], f"st_out{t}"))
    for m in stores:
        sy.wait_ge(*m)


def t5_buckets(rel):
    half, exact = 16, 8
    n = np.abs(rel)
    nf = np.maximum(n, 1).astype(np.float32)
    large = exact + (np.log(nf / np.float32(exact)) / np.float32(np.log(128 / exact)) * np.float32(half - exact)).astype(np.int32)
    return np.where(rel > 0, half, 0) + np.where(n < exact, n, np.minimum(large, half - 1))


DEBUG = {}


def kernel(**inputs):
    import numpy as _np
    import concourse.bacc as _bacc
    from concourse import mybir as _mybir
    from concourse.bass_utils import run_bass_kernel_spmd as _run

    f = {k: _np.asarray(v) for k, v in inputs.items()}
    arrays = {}
    arrays["cols"] = _np.concatenate([f[n].reshape(-1, P) for n, _ in COLS]).T
    arrays["rows"] = _np.concatenate([f[n].reshape(-1) for n, _ in ROWS])[None, :]
    pos = f["positions"][0]
    cpos = pos[_np.minimum(_np.arange(CPAD) * CMP_STRIDE + CMP_LEN - 1, S - 1)]
    arrays["pos"] = _np.stack([pos[:P], pos[P:], _np.tile(cpos, NKV)], axis=1)
    arrays["x"] = f["x"][0]
    arrays["ada_w"] = f["ada_w"]
    arrays["w_ada_2"] = f["w_ada_2"][0]
    for n in ("nsa_w_in", "nsa_w_out", "moba_w_in", "moba_w_out", "w_in_2", "w_out_2", "w_query_2", "nsa_cmp_w1", "nsa_cmp_w2"):
        arrays[n] = f[n][0]
    arrays["cmp_pe"] = f["nsa_cmp_pe"][0].reshape(2, NPAIR, P).transpose(2, 0, 1)
    rel = _np.arange(3 * P)[None, :] - P - _np.arange(P)[:, None]
    seen = _np.abs(rel) <= P
    table = f["t5_table_2"][t5_buckets(rel)]
    arrays["bias_a"] = _np.where(seen[:, :, None], table, _np.float32(NEG)).transpose(0, 2, 1)
    tok = _np.arange(S)
    rr, cc = tok // 64, tok % 64
    start = _np.clip(cc - 8, 0, 64 - 16)
    row_off = rr[None, :] - rr[:, None] + 7
    col_off = cc[None, :] - cc[:, None] + 15
    inside = (cc[None, :] >= start[:, None]) & (cc[None, :] < start[:, None] + 16)
    rpb = f["rpb_b_2"][0][:, row_off, _np.clip(col_off, 0, 30)]
    bb = _np.where(inside[None], rpb, _np.float32(NEG))
    arrays["bias_b"] = bb.reshape(HB, NT, P, S).transpose(2, 1, 0, 3)
    arrays["keysT"] = f["sub_keys_2"][0].reshape(2 * PH, PK, P).transpose(2, 0, 1)
    arrays["u"] = f["u_experts_2"][0].reshape(PK, PK, DC, P).transpose(1, 3, 2, 0).reshape(PK, P, D)
    arrays["v"] = f["v_experts_2"][0].reshape(PK, PK, D).transpose(1, 0, 2)
    arrays["final_g"] = f["final_g_2"][None, :]
    arrays["ada_b"] = f["ada_b"]
    arrays["b_ada_2"] = f["b_ada_2"]
    arrays = {k: _np.ascontiguousarray(v) for k, v in arrays.items()}

    nc = _bacc.Bacc("TRN2", target_bir_lowering=False, num_devices=1, dynamic_dma_scratch_size=1024)
    aps = {k: nc.dram_tensor(f"in_{k}", v.shape, _mybir.dt.from_np(v.dtype), kind="ExternalInput").ap()
           for k, v in arrays.items()}
    aps["out"] = nc.dram_tensor("out", (S, D), F32, kind="ExternalOutput").ap()
    dbg = {k: nc.dram_tensor(f"dbg_{k}", s, F32, kind="ExternalOutput").ap() for k, s in DEBUG.items()}
    program(nc, aps, dbg)
    r = _run(nc, [{f"in_{k}": v for k, v in arrays.items()}], core_ids=[0])
    return r.results[0]["out"][None]
```

```python
from contextlib import ExitStack

import numpy as np
import concourse.bass as bass
from concourse import mybir

F32 = mybir.dt.float32
F32R = mybir.dt.float32r
I32 = mybir.dt.int32
U32 = mybir.dt.uint32
ALU = mybir.AluOpType
ACT = mybir.ActivationFunctionType
AX = mybir.AxisListType.X

P = 128
S = 256
NT = S // P
D = 1024
DC = D // P
HD = 64
NH = 16
NKV = 4
GQA = NH // NKV
ROT = HD // 4
HALF = ROT // 2
THETA = 500000.0
EPS = 1e-6
CMP_LEN, CMP_STRIDE = 32, 16
NCMP = (S - CMP_LEN) // CMP_STRIDE + 1
CPAD = 32
CMP_HID = 4 * HD
NPAIR = CMP_LEN * HD // P
NEG = -1e30
FLOOR = -1e29
WT = 512
RING = 3
ARENA = 32768
KEEP = 48
TOK = 8
HA, HB = 8, 8
KVA = 2
PH, PK, PTOP = 8, 128, 16
BLK = 4

COLS = [("c", 8), ("c_2", 8), ("norm_g", 16), ("ada_b", 48), ("b_ada_2", 48), ("norm1_g_2", 8), ("norm2_g_2", 8),
        ("out_norm_a_2", 4), ("out_norm_b_2", 4), ("nsa_cmp_b1", 4)]
ROWS = [("nsa_q_norm", HD), ("nsa_k_norm", 3 * HD), ("moba_q_norm", HD), ("moba_k_norm", HD), ("nsa_gate_b", 3 * NH),
        ("sink_a_2", HA)]


def offsets(table):
    at, out = 0, {}
    for name, n in table:
        out[name] = (at, at + n)
        at += n
    return out, at


COL_AT, NCOL = offsets(COLS)
ROW_AT, NROW = offsets(ROWS)


class Line:

    def __init__(self, nc, stack, eng, name):
        self.eng, self.sem, self.count, self.seen = eng, stack.enter_context(nc.semaphore(name)), 0, {}
        self.name = name

    def need(self, *marks):
        for m in marks:
            if m is not None and self.seen.get(m[0].name, 0) < m[1]:
                self.eng.wait_ge(m[0], m[1])
                self.seen[m[0].name] = m[1]

    def did(self, inst):
        self.count += 1
        inst.then_inc(self.sem, 1)
        return (self.sem, self.count)

    def last(self):
        return (self.sem, self.count) if self.count else None


class Load:

    def __init__(self, nc, stack, name):
        self.sem, self.n = stack.enter_context(nc.semaphore(name)), 0

    def did(self, inst):
        self.n += 16
        inst.then_inc(self.sem, 16)
        return (self.sem, self.n)


class Bank:

    def __init__(self, tensor):
        self.t, self.free = tensor, None


def program(nc, a, dbg):
    with ExitStack() as st:
        build(nc, st, a, dbg)


def build(nc, st, a, dbg):
    V, A, G, T, Y = (Line(nc, st, e, n) for e, n in (
        (nc.vector, "vec"), (nc.scalar, "act"), (nc.gpsimd, "pool"), (nc.tensor, "pe"), (nc.sync, "sp")))
    ve, ac, po, pe, sy = nc.vector, nc.scalar, nc.gpsimd, nc.tensor, nc.sync

    def sb(name, shape, dt=F32):
        return st.enter_context(nc.sbuf_tensor(name, shape, dt))

    arena = sb("arena", [P, ARENA])
    top = [0]

    def carve(shape, stack, dt=F32):
        n = int(np.prod(shape[1:]))
        at = top[0]
        top[0] = at + n
        assert top[0] <= ARENA, (top[0], ARENA)
        stack.callback(top.__setitem__, 0, at)
        view = arena[0:shape[0], at:at + n]
        if dt != F32:
            view = view.bitcast(dt)
        names = "abcd"[:len(shape) - 1]
        if len(shape) == 2:
            return view
        return view.rearrange(f"p ({' '.join(names)}) -> p {' '.join(names)}", **dict(zip(names, shape[1:])))

    stores = []

    def load(dst, src, name, eng=None):
        return Load(nc, st, name).did((eng or sy).dma_start(dst, src))

    def meet(with_loads=False):
        marks = [e.last() for e in (V, A, G, T)]
        for e in (V, A, G, T) if not with_loads else (V, A, G, T, Y):
            e.need(*[m for m in marks if m is not None])

    banks = [Bank(st.enter_context(nc.psum_tensor(f"bank{i}", [P, 512], F32))) for i in range(8)]
    turn = {"proj": 0, "spare": 0}
    spare_pair = [2]

    def proj_bank():
        b = banks[turn["proj"] % 2]
        turn["proj"] += 1
        return b

    def spare_bank():
        b = banks[spare_pair[0] + turn["spare"] % 2]
        turn["spare"] += 1
        return b

    later = []

    def run_later():
        due = later[:]
        later.clear()
        for work in due:
            work()

    x = sb("x_tok", [P, NT, D])
    ident = sb("ident", [P, P])
    cols = sb("cols", [P, NCOL])
    rows = sb("rows", [P, NROW])
    causal = sb("causal", [P, S])
    cmp_mask = sb("cmp_mask", [P, NT, CPAD])
    iota_k = sb("iota_k", [P, P])
    pos_i = sb("pos_i", [P, NT + 1], I32)
    cosd = sb("cosd", [P, NT + 1, ROT])
    sind = sb("sind", [P, NT + 1, ROT])
    silu_c = sb("silu_c", [P, 2, DC])
    ada = [sb("ada0", [P, 24]), sb("ada1", [P, 24]), sb("ada2", [P, 48])]
    gate_row = [sb(f"gate_row{i}", [P, D]) for i in range(2)]
    ones = sb("ones", [P, P])
    mod_a = sb("mod_a", [P, DC])
    stat = sb("stat", [P, 8])
    pow_half = sb("pow_half", [P, NH])
    hkT = sb("hkT", [P, 3, S])
    layers = ExitStack()
    st.callback(layers.close)
    raw_all = sb("raw", [P, 4, D])
    ring = [raw_all[:].rearrange("p a n -> p (a n)")] + [carve([P, DC * WT], layers) for i in range(RING - 1)]
    hT = carve([P, DC, S], layers)

    def col(name, lo=0, hi=None):
        s, e = COL_AT[name]
        return cols[:, s + lo:(e if hi is None else s + hi)]

    def row(name, lo=0, hi=None):
        s, e = ROW_AT[name]
        return rows[:, s + lo:(e if hi is None else s + hi)]

    m_cols = load(cols[:], a["cols"], "ld_cols")
    m_pos = load(pos_i[:], a["pos"], "ld_pos", ac)
    m_x = load(x[:], a["x"].rearrange("(t p) d -> p t d", p=P), "ld_x", ac)
    m_rows = load(rows[:], a["rows"].broadcast_to([P, NROW]), "ld_rows", ac)

    slot_load = [Load(nc, st, f"ld_ring{i}") for i in range(RING)]
    slot_free = [None] * RING
    streamed = [0]

    def stream(src, chunks, width):
        i = streamed[0] % RING
        streamed[0] += 1
        Y.need(slot_free[i])
        tile = ring[i][:, 0:chunks * width].rearrange("p (c n) -> p c n", c=chunks)
        return tile, slot_load[i].did(sy.dma_start(tile, src.rearrange("(c p) n -> p c n", p=P))), i

    m_z = G.did(po.memset(ident[:], 0.0))
    G.need(m_z)
    m_ident = G.did(po.affine_select(out=ident[:], in_=ident[:], compare_op=ALU.not_equal, fill=1.0, base=0,
                                     pattern=[[-1, P]], channel_multiplier=1))
    m_z = G.did(po.memset(causal[:], 0.0))
    m_p = G.did(po.memset(pow_half[:], -0.5))
    m_ones = G.did(po.memset(ones[:], 1.0))
    m_c0 = G.did(po.memset(cmp_mask[:], 0.0))
    G.need(m_z)
    m_causal = G.did(po.affine_select(out=causal[:, P:S], in_=causal[:, P:S], compare_op=ALU.is_ge, fill=NEG, base=0,
                                      pattern=[[-1, P]], channel_multiplier=1))
    G.need(m_c0)
    for t in range(NT):
        m = G.did(po.affine_select(out=cmp_mask[:, t, :], in_=cmp_mask[:, t, :], compare_op=ALU.is_ge, fill=NEG,
                                   base=t * P - (CMP_LEN - 1), pattern=[[-CMP_STRIDE, CPAD]], channel_multiplier=1))
    G.need(m)
    m_cmask = G.did(po.memset(cmp_mask[:, :, NCMP:CPAD], NEG))
    m_iota = G.did(po.iota(iota_k[:], [[1, P]], base=0, channel_multiplier=0, allow_small_or_imprecise_dtypes=True))
    m_pow = m_p

    freq = carve([P, HALF], layers)
    ang = carve([P, 4, NT + 1, HALF], layers)
    posf = carve([P, NT + 1], layers)
    for j in range(HALF):
        m_f = G.did(po.memset(freq[:, j:j + 1], float(np.float32(THETA) ** np.float32(-2.0 * j / ROT))))
    V.need(m_pos)
    m = V.did(ve.tensor_copy(posf[:], pos_i[:]))
    V.need(m, m_f)
    for t in range(NT + 1):
        m = V.did(ve.tensor_scalar(ang[:, 0, t, :], freq[:], posf[:, t:t + 1], None, ALU.mult))
    two_pi = 2.0 * np.pi
    parts, rest = [], two_pi
    for bits in (8, 8, 8):
        e = np.floor(np.log2(rest)) + 1 - bits
        p = np.floor(rest / 2.0 ** e) * 2.0 ** e
        parts.append(float(p))
        rest -= p
    parts.append(float(np.float32(rest)))
    magic = float(1.5 * 2 ** 23)
    V.need(m)
    m = V.did(ve.tensor_scalar(ang[:, 1], ang[:, 0], float(1.0 / two_pi), magic, ALU.mult, ALU.add))
    V.need(m)
    m = V.did(ve.tensor_scalar(ang[:, 1], ang[:, 1], -magic, None, ALU.add))
    for p in parts:
        V.need(m)
        m = V.did(ve.scalar_tensor_tensor(out=ang[:, 0], in0=ang[:, 1], scalar=-p, in1=ang[:, 0], op0=ALU.mult,
                                          op1=ALU.add))
    V.need(m)
    pi32 = 3.1415925
    m = V.did(ve.tensor_scalar(ang[:, 0], ang[:, 0], pi32, -pi32, ALU.min, ALU.max))
    V.need(m)
    m = V.did(ve.scalar_tensor_tensor(out=ang[:, 2], in0=ang[:, 0], scalar=-1.0, in1=ang[:, 0], op0=ALU.mult,
                                      op1=ALU.min))
    V.need(m)
    m_r = V.did(ve.tensor_scalar(ang[:, 2], ang[:, 2], float(np.pi / 2), None, ALU.add))
    A.need(m_r)
    m_cos = A.did(ac.activation(ang[:, 3], ang[:, 2], ACT.Sin))
    m_sin = A.did(ac.activation(sind[:, :, HALF:ROT], ang[:, 0], ACT.Sin))
    V.need(m_cos, m_sin)
    V.did(ve.tensor_copy(cosd[:, :, 0:HALF], ang[:, 3]))
    V.did(ve.tensor_copy(cosd[:, :, HALF:ROT], ang[:, 3]))
    m_rope = V.did(ve.tensor_scalar(sind[:, :, 0:HALF], sind[:, :, HALF:ROT], -1.0, None, ALU.mult))

    A.need(m_cols)
    A.did(ac.activation(silu_c[:, 0, :], col("c"), ACT.Silu))
    m_silu = A.did(ac.activation(silu_c[:, 1, :], col("c_2"), ACT.Silu))

    scores_pair = carve([P, 2 * 512], layers)
    probs_three = carve([P, 3 * 512], layers)
    soft = {"scores": [scores_pair[:, 0:512], scores_pair[:, 512:1024]],
            "probs": [probs_three[:, i * 512:(i + 1) * 512] for i in range(3)],
            "probsT": [carve([P, 512], layers) for _ in range(2)]}
    CHUNKS = 4
    chunk_buf = [carve([P, WT], layers) for _ in range(CHUNKS)]
    chunk_load = [Load(nc, st, f"ld_chunk{i}") for i in range(CHUNKS)]
    chunk_free, chunk_mark, chunk_count = [None] * CHUNKS, [None] * CHUNKS, {"asked": 0, "used": 0}
    ada_acc = [carve([P, WT], layers) for _ in range(2)]
    ada_turn = [0]
    acc_read = [None, None]

    def ask_chunks():
        while chunk_count["asked"] < min(len(chunk_order), chunk_count["used"] + CHUNKS):
            i, (l, j, c) = chunk_count["asked"] % CHUNKS, chunk_order[chunk_count["asked"]]
            src = a["ada_w"][l] if l < 2 else a["w_ada_2"]
            A.need(chunk_free[i])
            chunk_mark[i] = chunk_load[i].did(ac.dma_start(chunk_buf[i], src[c * P:(c + 1) * P, j * WT:(j + 1) * WT]))
            chunk_count["asked"] += 1

    def ada_steps(layer, j):
        k = ada_turn[0] % 2
        ada_turn[0] += 1
        if acc_read[k] == "due":
            run_later()
        acc = ada_acc[k]
        if j % 6 >= 4:
            side = j % 2
            if bias_read[side] == "due":
                run_later()
            bsrc = a["ada_b"][layer:layer + 1] if layer < 2 else a["b_ada_2"]
            A.need(bias_read[side])
            bias_row, ones_row = gate_bias[32 * side:32 * side + 1, :], ones[32 * side:32 * side + 1, :]
            m_bias = ld_bias[side].did(ac.dma_start(bias_row, bsrc[:, j * WT:(j + 1) * WT]))
            bias_read[side] = "due"
        whole = (layer, j) in FIRST
        if whole:
            w, m_w, slot = stream(a["ada_w"][layer][:, j * WT:(j + 1) * WT], DC, WT)
        for c in range(DC):
            yield
            if whole:
                V.need(m_w)
                src = w[:, c, :]
            else:
                ask_chunks()
                i = chunk_count["used"] % CHUNKS
                V.need(chunk_mark[i])
                src = chunk_buf[i]
            factor = silu_c[:, layer // 2, c:c + 1]
            if c == 0:
                V.need(m_silu, acc_read[k])
                m = V.did(ve.tensor_scalar(acc, src, factor, None, ALU.mult))
            else:
                V.need(m)
                m = V.did(ve.scalar_tensor_tensor(out=acc, in0=src, scalar=factor, in1=acc, op0=ALU.mult, op1=ALU.add))
            if whole:
                slot_free[slot] = m
            else:
                chunk_free[i] = m
                chunk_count["used"] += 1
                ask_chunks()
        acc_read[k] = "due"

        def sum_partitions():
            b = spare_bank()
            if j % 6 < 4:
                T.need(b.free, m, m_ones)
                for i in range(4):
                    last = pe.matmul(b.t[:, i:i + 1], acc[:, i * P:(i + 1) * P], ones[:, 0:1], start=True, stop=True)
                acc_read[k] = T.did(last)
                bias = col("ada_b", 24 * layer, 24 * layer + 24) if layer < 2 else col("b_ada_2")
                V.need(acc_read[k], m_cols)
                b.free = V.did(ve.tensor_tensor(ada[layer][:, 4 * j:4 * j + 4], b.t[:, 0:4], bias[:, 4 * j:4 * j + 4],
                                                ALU.add))
            else:
                half = j % 6 - 4
                T.need(b.free, m, m_ones, m_bias)
                pe.matmul(b.t[:], ones[:], acc, start=True, stop=False)
                acc_read[k] = bias_read[side] = T.did(pe.matmul(b.t[:], ones_row, bias_row, start=False, stop=True))
                A.need(acc_read[k], gate_read[gate_of(layer, j)])
                b.free = A.did(ac.activation(gate_row[gate_of(layer, j)][:, half * 512:(half + 1) * 512], b.t[:], ACT.Copy))
            ada_mark[layer, j] = b.free

        later.append(sum_partitions)

    def gate_of(layer, j):
        return 1 if layer == 1 or j >= 6 else 0

    gate_bias = carve([P, WT], layers)
    ld_bias = [Load(nc, st, f"ld_bias{i}") for i in range(2)]
    bias_read, gate_read = [None, None], [None, None]

    fillers = [(0, j) for j in range(6)] + [(1, j) for j in range(4)] + [(2, j) for j in range(4)] + [(1, 4), (1, 5)] + \
        ["layer 0"] + [(2, j) for j in range(4, 10)] + ["layer 1"] + [(2, 10), (2, 11)]
    FIRST = fillers[0:4]
    chunk_order = [(*f, c) for f in fillers[4:] if not isinstance(f, str) for c in range(DC)]
    ada_mark = {}

    current = []

    def trickle(n):
        while n > 0:
            if not current:
                if not fillers or isinstance(fillers[0], str):
                    return
                current.append(ada_steps(*fillers.pop(0)))
                next(current[0])
            if next(current[0], "end") == "end":
                current.clear()
            n -= 1

    def ensure(layer, js):
        while any((layer, j) not in ada_mark for j in js):
            trickle(DC)
            run_later()
        return [ada_mark[layer, j] for j in js]

    def row_rstd(dst, src, width, marks, scratch):
        V.need(*marks)
        m = V.did(ve.tensor_tensor_reduce(out=scratch, in0=src, in1=src, scale=1.0, scalar=0.0, op0=ALU.mult,
                                          op1=ALU.add, accum_out=dst))
        V.need(m)
        m = V.did(ve.tensor_scalar(dst, dst, 1.0 / width, EPS, ALU.mult, ALU.add))
        G.need(m, m_pow)
        return G.did(po.tensor_tensor(dst, dst, pow_half[:, 0:1], ALU.pow))

    def to_columns(src, marks, put):
        out = []
        for half in range(2):
            b = spare_bank()
            T.need(b.free, m_ident, *marks)
            for i in range(4):
                c = 4 * half + i
                last = pe.transpose(b.t[:, i * P:(i + 1) * P], src[:, c * P:(c + 1) * P], ident[:])
            b.free = put(half, b.t, T.did(last))
            out.append(b.free)
        return out

    def scaled_columns(t, factor, shift=None):
        def put(half, bank, m_t):
            e = A if half else V
            e.need(m_t)
            for i in range(4):
                c = 4 * half + i
                dst, src = hT[:, c, t * P:(t + 1) * P], bank[:, i * P:(i + 1) * P]
                add = None if shift is None else shift[:, c:c + 1]
                if half:
                    m = A.did(ac.activation(dst, src, ACT.Identity, scale=factor[:, c:c + 1],
                                            bias=0.0 if add is None else add))
                elif add is None:
                    m = V.did(ve.tensor_scalar(dst, src, factor[:, c:c + 1], None, ALU.mult))
                else:
                    m = V.did(ve.tensor_scalar(dst, src, factor[:, c:c + 1], add, ALU.mult, ALU.add))
            return m
        return put

    x_mark = [m_x] * NT
    h_mark = [None] * NT

    def modulated(layer, norm, shift, scale):
        xn, m_xn = (probs_three[:, 0:D], scores_pair), [None] * NT

        def normalised(t):
            V.need(row_rstd(stat[:, t:t + 1], x[:, t, :], D, [x_mark[t]], xn[t]))
            m_xn[t] = V.did(ve.tensor_scalar(xn[t], x[:, t, :], stat[:, t:t + 1], None, ALU.mult))

        def turn_over(t):
            h_mark[t] = to_columns(xn[t], [m_xn[t]], scaled_columns(t, mod_a, ada[layer][:, shift:shift + DC]))

        def begin():
            V.need(A.last(), G.last())
            normalised(0)
            V.need(*ensure(layer, range(shift // 4, shift // 4 + 4)))
            m_mod = V.did(ve.scalar_tensor_tensor(out=mod_a[:], in0=ada[layer][:, scale:scale + DC], scalar=1.0,
                                                  in1=norm, op0=ALU.add, op1=ALU.mult))
            V.need(m_mod)
            A.need(m_mod)

        def finish():
            h_mark[:] = [None] * NT
            turn_over(0)
            normalised(1)
            later.append(lambda: turn_over(1))

        return begin, finish

    def project(src, width, use, tile=None):
        w, m_w, slot = tile or stream(src, DC, width)
        for t in range(NT):
            b = proj_bank()
            T.need(b.free, m_w, *h_mark[t])
            for c in range(DC):
                last = pe.matmul(b.t[:, 0:width], hT[:, c, t * P:(t + 1) * P], w[:, c, :], start=c == 0,
                                 stop=c == DC - 1)
            slot_free[slot] = m = T.did(last)
            run_later()
            b.free = use(t, b.t[:, 0:width], m)
            trickle(4 if width == WT else 2)

    def project_cols(src, width, use, tile=None):
        if h_mark[NT - 1] is None:
            run_later()
        w, m_w, slot = tile or stream(src, DC, width)
        for i in range(width // P):
            b = proj_bank()
            T.need(b.free, m_w, *[m for ms in h_mark for m in ms])
            for c in range(DC):
                last = pe.matmul(b.t[:, 0:S], w[:, c, i * P:(i + 1) * P], hT[:, c, :], start=c == 0, stop=c == DC - 1)
            slot_free[slot] = m = T.did(last)
            run_later()
            b.free = use(i, b.t[:, 0:S], m)
            trickle(3)

    hn = sb("head_ms", [P, NH])

    def head_norm(src, dst, n, g, tab, post, tmp, marks, g_heads=None):
        s3, d3, t3 = (v.rearrange("p (h d) -> p h d", d=HD) for v in (src, dst, tmp))
        np_ = src.shape[0]
        A.need(*marks)
        m = A.did(ac.activation(tmp, src, ACT.Square))
        V.need(m, *marks)
        m = V.did(ve.tensor_reduce(hn[0:np_, 0:n], t3, AX, ALU.add))
        V.need(m)
        m = V.did(ve.tensor_scalar(hn[0:np_, 0:n], hn[0:np_, 0:n], 1.0 / HD, EPS, ALU.mult, ALU.add))
        G.need(m, m_pow)
        m = G.did(po.tensor_tensor(hn[0:np_, 0:n], hn[0:np_, 0:n], pow_half[0:np_, 0:n], ALU.pow))
        V.need(m)
        m_src = V.did(ve.tensor_tensor(d3, s3, hn[0:np_, 0:n].unsqueeze(2).broadcast_to([np_, n, HD]), ALU.mult))
        V.need(m_src, m_rows)
        m = V.did(ve.scalar_tensor_tensor(out=d3, in0=d3, scalar=post, in1=g[0:np_, :].unsqueeze(1).broadcast_to([np_, n, HD]),
                                          op0=ALU.mult, op1=ALU.mult))
        cc = cosd[0:np_, tab, :].unsqueeze(1).broadcast_to([np_, n, ROT])
        G.need(m, m_rope)
        s_lo = sind[0:np_, tab, 0:HALF].unsqueeze(1).broadcast_to([np_, n, HALF])
        s_hi = sind[0:np_, tab, HALF:ROT].unsqueeze(1).broadcast_to([np_, n, HALF])
        G.did(po.tensor_tensor(t3[:, :, ROT:ROT + HALF], d3[:, :, HALF:ROT], s_lo, ALU.mult))
        G.did(po.tensor_tensor(t3[:, :, ROT + HALF:2 * ROT], d3[:, :, 0:HALF], s_hi, ALU.mult))
        m = G.did(po.tensor_tensor(t3[:, :, 0:ROT], d3[:, :, 0:ROT], cc, ALU.mult))
        G.need(m)
        return m_src, G.did(po.tensor_tensor(d3[:, :, 0:ROT], t3[:, :, 0:ROT], t3[:, :, ROT:2 * ROT], ALU.add))

    def q_tile_use(qT, j, tab_g, bufs):
        def use(t, ps, m):
            qn, tmp = bufs[t]
            m_src, mq = head_norm(ps, qn[:], 8, tab_g, t, HD ** -0.5, tmp[:], [m])

            def turn_over():
                b = spare_bank()
                T.need(b.free, mq, m_ident)
                for i in range(4):
                    last = pe.transpose(b.t[:, i * P:(i + 1) * P], qn[:, i * P:(i + 1) * P], ident[:])
                A.need(T.did(last))
                b.free = A.did(ac.activation(qT[:, 4 * j:4 * j + 4, t * P:(t + 1) * P],
                                             b.t[:].rearrange("p (i n) -> p i n", i=4), ACT.Copy))

            later.append(turn_over)
            return m_src
        return use

    def kv_tile_use(kT, v_sb, g, bufs):
        def use(t, ps, m):
            kn, tmp = bufs[t]
            dup = kn[:, 2 * P:4 * P + 2 * P]
            m_src, mk = head_norm(ps[:, 0:NKV * HD], kn[:, 0:NKV * HD], NKV, g, t, 1.0, tmp[:, 0:NKV * HD], [m])
            A.need(m_src)
            m_v = A.did(ac.activation(v_sb[:, t, :], ps[:, NKV * HD:2 * NKV * HD], ACT.Copy))
            G.need(mk)
            mk = G.did(po.tensor_copy(dup.rearrange("p (g u d) -> p g u d", g=NKV, u=2),
                                      kn[:, 0:NKV * HD].rearrange("p (g d) -> p g d", g=NKV).unsqueeze(2).broadcast_to(
                                          [P, NKV, 2, HD])))

            def turn_over():
                b = spare_bank()
                T.need(b.free, mk, m_ident)
                for i in range(NKV):
                    last = pe.transpose(b.t[:, i * P:(i + 1) * P], dup[:, i * P:(i + 1) * P], ident[:])
                A.need(T.did(last))
                b.free = A.did(ac.activation(kT[:, :, t * P:(t + 1) * P], b.t[:].rearrange("p (i n) -> p i n", i=NKV),
                                             ACT.Copy))

            later.append(turn_over)
            return m_v
        return use

    nmax = sb("nmax", [P, NT, NH])
    rsum = sb("rsum", [P, NT, NH])
    esink = sb("esink", [P, NT, HA])
    prob_scale = sb("prob_scale", [P, 2, 4])
    soft_read = {"scores": [None, None], "probs": [None] * 3, "probsT": [None, None]}
    opened = set()

    def add_outputs(head, n, v_dims, probs):
        c, half = head // 2, slice(HD * (head % 2), HD * (head % 2) + HD)
        key = (6 + c // 4, head % 2)
        out = banks[key[0]].t[half, (c % 4) * P:(c % 4 + n) * P].rearrange("p (h q) -> p h q", q=P)
        inst = pe.matmul(out, v_dims, probs, start=key not in opened, stop=True, skip_group_check=True)
        opened.add(key)
        return inst

    def attend(heads, branches, q_of, bias_of, first_of, causal_keys, marks, begin, done, sink=None):
        run_later()
        spare_pair[0] = 0
        units = []
        for t in range(NT):
            w = P if causal_keys and t == 0 else S
            per = 512 // w
            by = [[h for h in heads if h % 2 == par] for par in (0, 1)]
            cut = [[hs[i:i + per] for i in range(0, len(hs), per)] for hs in by]
            for br in branches:
                for i in range(len(cut[0])):
                    for par in (0, 1):
                        units.append((t, w, cut[par][i], br))
        n = len(units)
        m_sc, m_ex, m_nm, m_tr, m_cp = {}, {}, {}, {}, {}

        def of_heads(x, hs):
            return x[:, hs[0]:hs[-1] + 1:2]

        def scores(u):
            t, w, hs, (k_of, _, _, _) = units[u]
            b = banks[2 + u % 2]
            T.need(b.free, *marks)
            for j, h in enumerate(hs):
                last = pe.matmul(b.t[:, j * w:(j + 1) * w], q_of(h, t), k_of(h, w), start=True, stop=True)
            m_sc[u] = T.did(last)
            V.need(m_sc[u], soft_read["scores"][u % 2])
            for j, h in enumerate(hs):
                m = V.did(ve.tensor_tensor_reduce(
                    out=soft["scores"][u % 2][:, j * w:(j + 1) * w], in0=b.t[:, j * w:(j + 1) * w],
                    in1=bias_of(h, t, w), scale=-1.0, scalar=first_of(h), op0=ALU.add, op1=ALU.min,
                    accum_out=nmax[:, t, h:h + 1]))
            b.free = m
            sunk = sink is not None and hs[-1] < sink.shape[1]
            if sunk:
                V.need(m)
                m = V.did(ve.tensor_tensor(of_heads(esink[:, t, :], hs), of_heads(sink, hs), of_heads(nmax[:, t, :], hs),
                                           ALU.add))
            A.need(m, soft_read["probs"][u % 3])
            for j, h in enumerate(hs):
                m = A.did(ac.activation(soft["probs"][u % 3][:, j * w:(j + 1) * w],
                                        soft["scores"][u % 2][:, j * w:(j + 1) * w], ACT.Exp, scale=-1.0,
                                        bias=nmax[:, t, h:h + 1], accum_out=rsum[:, t, h:h + 1]))
            soft_read["scores"][u % 2] = m
            if sunk:
                m = A.did(ac.activation(of_heads(esink[:, t, :], hs), of_heads(esink[:, t, :], hs), ACT.Exp))
            m_ex[u] = m

        def normalise(u):
            t, w, hs, (_, _, _, gate) = units[u]
            sc, rs = prob_scale[:, u % 2, 0:len(hs)], of_heads(rsum[:, t, :], hs)
            V.need(m_ex[u])
            if sink is not None and hs[-1] < sink.shape[1]:
                V.need(V.did(ve.tensor_tensor(rs, rs, of_heads(esink[:, t, :], hs), ALU.add)))
            if gate is None:
                V.need(V.did(ve.tensor_scalar(sc, rs, 1e-30, None, ALU.max)))
                V.need(V.did(ve.reciprocal(sc, sc)))
            else:
                V.need(V.did(ve.reciprocal(sc, rs)))
                V.need(V.did(ve.scalar_tensor_tensor(out=sc, in0=sc, scalar=1e30, in1=of_heads(gate[:, t, :], hs),
                                                     op0=ALU.min, op1=ALU.mult)))
            for j in range(len(hs)):
                part = soft["probs"][u % 3][:, j * w:(j + 1) * w]
                m_nm[u] = V.did(ve.tensor_scalar(part, part, sc[:, j:j + 1], None, ALU.mult))

        def turned(u):
            t, w, hs, _ = units[u]
            b = banks[4 + u % 2]
            T.need(b.free, m_nm[u])
            for i in range(len(hs) * w // P):
                last = pe.transpose(b.t[:, i * P:(i + 1) * P], soft["probs"][u % 3][:, i * P:(i + 1) * P], ident[:])
            m_tr[u] = T.did(last)
            soft_read["probs"][u % 3] = m_tr[u]
            A.need(m_tr[u], soft_read["probsT"][u % 2])
            b.free = m_cp[u] = A.did(ac.activation(soft["probsT"][u % 2][:], b.t[:], ACT.Copy))

        def outputs(u):
            t, w, hs, (_, v_of, v_group, _) = units[u]
            if u == 0 or units[u - 1][0] != t:
                T.need(banks[6].free, banks[7].free)
                opened.clear()
                begin(t)
            T.need(m_cp[u])
            probs = soft["probsT"][u % 2][:].rearrange("p (j k q) -> p k j q", k=w // P, q=P)
            for k in range(w // P):
                j = 0
                while j < len(hs):
                    run = [h for h in hs[j:] if v_group(h) == v_group(hs[j])]
                    last = add_outputs(hs[j], len(run), v_of(hs[j], k), probs[:, k, j:j + len(run), :])
                    j += len(run)
            m = T.did(last)
            soft_read["probsT"][u % 2] = m
            if u + 1 == n or units[u + 1][0] != t:
                banks[6].free, banks[7].free = done(t, m)

        for u in range(n + 3):
            if u < n:
                scores(u)
            if 0 <= u - 1 < n:
                normalise(u - 1)
            run_later()
            if 0 <= u - 3 < n:
                outputs(u - 3)
            if 0 <= u - 2 < n:
                turned(u - 2)
            if u % 2:
                trickle(1)
        spare_pair[0] = 2

    oz_mark = [None] * NT

    def times_z(zT):
        def done(t, m):
            V.need(m)
            out = []
            for half in range(2):
                cs, ts = slice(4 * half, 4 * half + 4), slice(t * P, (t + 1) * P)
                out.append(V.did(ve.tensor_tensor(hT[:, cs, ts], banks[6 + half].t[:].rearrange("p (c q) -> p c q", c=4),
                                                  zT[:, cs, ts], ALU.mult)))
            oz_mark[t] = out
            return out
        return done

    def gated_out(w_src, layer, stack, begin_next, rstd=None):
        gate = 1 if layer == 1 else 0
        tmp = [carve([P, 512], stack) for _ in range(2)]
        m_g = ensure(layer, (4, 5))
        halves = [range(DC)] if rstd is None else [range(DC // 2), range(DC // 2, DC)]
        for j in range(2):
            w, m_w, slot = stream(w_src[:, j * WT:(j + 1) * WT], DC, WT)
            for t in range(NT):
                row_of_gate, dst = gate_row[gate][:, j * 512:(j + 1) * 512], x[:, t, j * 512:(j + 1) * 512]
                for n, cs in enumerate(halves):
                    b = proj_bank()
                    T.need(b.free, m_w, *oz_mark[t])
                    for c in cs:
                        last = pe.matmul(b.t[:], hT[:, c, t * P:(t + 1) * P], w[:, c, :], start=c == cs[0],
                                         stop=c == cs[-1])
                    slot_free[slot] = m = T.did(last)
                    V.need(m, *m_g, x_mark[t])
                    if rstd is None:
                        m = V.did(ve.tensor_tensor(tmp[t], b.t[:], row_of_gate, ALU.mult))
                    else:
                        m = V.did(ve.scalar_tensor_tensor(out=tmp[t], in0=b.t[:], scalar=rstd(t, n), in1=row_of_gate,
                                                          op0=ALU.mult, op1=ALU.mult))
                    b.free = gate_read[gate] = m
                    V.need(m)
                    x_mark[t] = V.did(ve.tensor_tensor(dst, dst, tmp[t], ALU.add))
                if j == 0:
                    trickle(4)
                elif t == 0:
                    begin_next()
        if f"layer {layer}" in fillers:
            fillers.remove(f"layer {layer}")

    def z_cols(zT, j):
        def use(i, ps, m):
            A.need(m)
            return A.did(ac.activation(zT[:, 4 * j + i, :], ps, ACT.Silu))
        return use

    def causal_bias(h, t, w):
        return causal[:, P:S] if w == P else causal[:]

    with ExitStack() as s0:
        w_in = a["nsa_w_in"]
        begin, finish = modulated(0, col("norm_g", 0, 8), 0, 8)
        trickle(DC + 1)
        run_later()
        begin()
        finish()
        ask_chunks()
        qT = carve([P, NH // 2, S], s0)
        kTs = [carve([P, NKV, S], s0) for i in range(2)]
        vs = [carve([P, NT, NKV * HD], s0) for i in range(2)]
        bufs = [(carve([P, 6 * P], s0), carve([P, 512], s0)) for t in range(NT)]
        qbufs = [(b[0][:, 0:512], b[1]) for b in bufs]
        zT = carve([P, DC, S], s0)
        gates = carve([P, 3, NT, NH], s0)
        gtmp = carve([P, 3 * NH], s0)
        x2 = carve([P, NKV, P], s0)
        xpe = carve([P, NPAIR, NKV, NCMP], s0)
        hid = carve([P, 2, NKV, CPAD], s0)
        pe_sb = carve([P, 2, NPAIR], s0)
        w2 = carve([P, 2, 2, HD], s0)
        kc_n = carve([P, 2 * HD], s0)
        kc_t = carve([P, HD], s0)
        kcT = carve([P, P], s0)
        vbd = carve([P, NKV, HD], s0)
        m_pe = load(pe_sb[:], a["cmp_pe"], "ld_pe", ac)
        m_w2 = load(w2[:], a["nsa_cmp_w2"].rearrange("i (c p) d -> p i c d", p=P), "ld_w2", ac)
        mz1 = G.did(po.memset(hid[:], 0.0))
        mz2 = G.did(po.memset(vbd[:], 0.0))

        def x2_use(i2):
            def use(blk, ps, m):
                V.need(m)
                for g2 in range(2):
                    src = ps[g2 * HD:(g2 + 1) * HD, :].rearrange("p (m u) -> p u m", u=2)
                    for par in range(2):
                        mm = V.did(ve.tensor_copy(x2[par * HD:(par + 1) * HD, 2 * blk + g2, :], src[:, par, :]))
                return mm
            return use

        xpe_mark, xpe_read, hid_mark = [None], [None], [None]

        def cmp_inputs(i):
            lo = NH * HD + i * NKV * HD
            project_cols(w_in[:, lo:lo + NKV * HD], NKV * HD, x2_use(i))
            V.need(V.last(), m_pe, xpe_read[0])
            for g in range(NKV):
                flat = x2[:, g, :]
                for c0 in (0, 8):
                    src = x2[:, g, c0:c0 + 8 * NCMP].rearrange("p (n c) -> p c n", c=8)
                    m = V.did(ve.tensor_tensor(xpe[:, c0:c0 + 8, g, :], src,
                                               pe_sb[:, i, c0:c0 + 8].unsqueeze(2).broadcast_to([P, 8, NCMP]), ALU.add))
            xpe_mark[0] = m

        def cmp_hidden(i):
            w1, m_w, slot = stream(a["nsa_cmp_w1"][i], NPAIR, CMP_HID)
            b = proj_bank()
            T.need(b.free, m_w, xpe_mark[0])
            for hb in range(2):
                for c in range(NPAIR):
                    last = pe.matmul(b.t[:, hb * 64:hb * 64 + NKV * NCMP], w1[:, c, hb * P:(hb + 1) * P],
                                     xpe[:, c, :, :].rearrange("p g n -> p (g n)"), start=c == 0, stop=c == NPAIR - 1)
            slot_free[slot] = xpe_read[0] = m = T.did(last)
            A.need(m, mz1, m_cols)
            for hb in range(2):
                m = A.did(ac.activation(hid[:, hb, :, 0:NCMP],
                                        b.t[:, hb * 64:hb * 64 + NKV * NCMP].rearrange("p (g n) -> p g n", g=NKV),
                                        ACT.Gelu_apprx_tanh, bias=col("nsa_cmp_b1", 2 * i + hb, 2 * i + hb + 1)))
            b.free = hid_mark[0] = m

        cmp_mark = {}

        def cmp_outputs(i):
            b = proj_bank()
            T.need(b.free, hid_mark[0], m_w2)
            for hb in range(2):
                last = pe.matmul(b.t[:, 0:HD], hid[:, hb, :, :].rearrange("p g n -> p (g n)"), w2[:, i, hb, :],
                                 start=hb == 0, stop=hb == 1)
            m = T.did(last)
            if i == 0:
                _, mk = head_norm(b.t[:, 0:HD], kc_n[:, 0:HD], 1, row("nsa_k_norm", 0, HD), NT, 1.0, kc_t[:], [m])
                b.free = mk
                G.need(mk)
                mk = G.did(po.tensor_copy(kc_n[:, HD:2 * HD], kc_n[:, 0:HD]))

                def turn_over():
                    b2 = spare_bank()
                    T.need(b2.free, mk, m_ident)
                    V.need(T.did(pe.transpose(b2.t[:, 0:P], kc_n[:], ident[:])))
                    b2.free = cmp_mark["k"] = V.did(ve.tensor_copy(kcT[:], b2.t[:, 0:P]))

                later.append(turn_over)
            else:
                V.need(m, mz2)
                for g in range(NKV):
                    m = V.did(ve.tensor_copy(vbd[g * CPAD:(g + 1) * CPAD, g, :], b.t[g * CPAD:(g + 1) * CPAD, 0:HD]))
                b.free = cmp_mark["v"] = m

        def keys_values(i):
            lo = NH * HD + (2 + 2 * i) * NKV * HD
            project(w_in[:, lo:lo + WT], WT,
                    kv_tile_use(kTs[i], vs[i], row("nsa_k_norm", (i + 1) * HD, (i + 2) * HD), bufs))

        def queries(j):
            project(w_in[:, j * WT:(j + 1) * WT], WT, q_tile_use(qT, j, row("nsa_q_norm"), qbufs))

        lo = NH * HD + 6 * NKV * HD

        def gate_use(t, ps, m):
            V.need(m, m_rows, A.last())
            m_s = V.did(ve.tensor_tensor(gtmp[:], ps, row("nsa_gate_b"), ALU.add))
            A.need(m_s)
            A.did(ac.activation(gates[:, :, t, :], gtmp[:].rearrange("p (h b) -> p b h", b=3), ACT.Sigmoid))
            return m_s

        keys_values(0)
        cmp_inputs(0)
        queries(0)
        cmp_hidden(0)
        keys_values(1)
        cmp_outputs(0)
        cmp_inputs(1)
        queries(1)
        cmp_hidden(1)
        project(w_in[:, lo:lo + 3 * NH], 3 * NH, gate_use)
        cmp_outputs(1)
        run_later()
        m_ready = [V.last(), A.last(), G.last()]

        smc = carve([P, 2, 2 * NKV, CPAD], s0)
        red = carve([P, 3, NH], s0)
        cmp_probs = [None, None]
        cmp_pT = carve([P, NT, GQA, P], s0)
        cmp_copied = [None] * NT

        def cmp_scores(t):
            T.need(banks[2].free, banks[3].free, cmp_mark["k"], *m_ready)
            for par in range(2):
                for g in range(NKV):
                    for r2 in range(2):
                        h = GQA * g + 2 * r2 + par
                        half = slice(HD * par, HD * par + HD)
                        last = pe.matmul(banks[2 + par].t[:, (NKV * r2 + g) * CPAD:(NKV * r2 + g + 1) * CPAD],
                                         qT[half, h // 2, t * P:(t + 1) * P], kcT[half, g * CPAD:(g + 1) * CPAD],
                                         start=True, stop=True)
                m = T.did(last)
            V.need(m, m_cmask)
            for par in range(2):
                m = V.did(ve.tensor_tensor(smc[:, par], banks[2 + par].t[:, 0:2 * NKV * CPAD].rearrange("p (h n) -> p h n", n=CPAD),
                                           cmp_mask[:, t, :].unsqueeze(1).broadcast_to([P, 2 * NKV, CPAD]), ALU.add))
                banks[2 + par].free = m
            sm3 = smc[:].rearrange("p a h n -> p (a h) n")
            V.need(m)
            m = V.did(ve.tensor_reduce(red[:, 0, :], sm3, AX, ALU.max))
            V.need(m)
            m = V.did(ve.tensor_scalar(red[:, 0, :], red[:, 0, :], FLOOR, None, ALU.max))
            V.need(m)
            m = V.did(ve.tensor_tensor(sm3, sm3, red[:, 0, :].unsqueeze(2).broadcast_to([P, NH, CPAD]), ALU.subtract))
            A.need(m)
            m = A.did(ac.activation(sm3, sm3, ACT.Exp))
            V.need(m)
            V.need(V.did(ve.tensor_reduce(red[:, 1, :], sm3, AX, ALU.add)))
            V.need(V.did(ve.tensor_scalar(red[:, 1, :], red[:, 1, :], 1e-30, None, ALU.max)))
            m = V.did(ve.reciprocal(red[:, 2, :], red[:, 1, :]))
            V.need(m)
            for par in range(2):
                r4 = red[:, 2, :].rearrange("p (a r g) -> p a r g", a=2, r=2)[:, par]
                g4 = gates[:, 0, t, :].rearrange("p (g r a) -> p a r g", a=2, r=2)[:, par]
                m = V.did(ve.tensor_tensor(r4, r4, g4, ALU.mult))
            V.need(m)
            cmp_probs[0] = V.did(ve.tensor_tensor(sm3, sm3, red[:, 2, :].unsqueeze(2).broadcast_to([P, NH, CPAD]), ALU.mult))

        def cmp_turned(t):
            T.need(cmp_probs[0], banks[4].free)
            for r in range(GQA):
                last = pe.transpose(banks[4].t[:, r * P:(r + 1) * P],
                                    smc[:, r % 2, NKV * (r // 2):NKV * (r // 2 + 1)].rearrange("p g n -> p (g n)"), ident[:])
            V.need(T.did(last))
            banks[4].free = cmp_copied[t] = V.did(ve.tensor_copy(cmp_pT[:, t], banks[4].t[:].rearrange("p (r q) -> p r q", r=GQA)))

        def cmp_values(t):
            T.need(cmp_copied[t], cmp_mark["v"])
            for par in range(2):
                for g in range(NKV):
                    add_outputs(GQA * g + par, 2, vbd[:, g, :], cmp_pT[:, t, par:GQA:2, :])

        stages = [(cmp_scores, 0), (cmp_turned, 0), (cmp_scores, 1), (cmp_turned, 1)]

        def run_stage(n):
            f, t = stages[n]
            f(t)
            if n + 1 < len(stages):
                later.append(lambda: run_stage(n + 1))

        run_stage(0)
        for j in range(2):
            at = lo + 3 * NH + j * WT
            project_cols(w_in[:, at:at + WT], WT, z_cols(zT, j))
        run_later()

        half_of = lambda h: slice(HD * (h % 2), HD * (h % 2) + HD)

        def branch(i):
            return (lambda h, w: kTs[i][half_of(h), h // GQA, 0:w],
                    lambda h, k: vs[i][:, k, (h // GQA) * HD:(h // GQA + 1) * HD], lambda h: h // GQA, gates[:, i + 1])

        attend(list(range(NH)), [branch(0), branch(1)], lambda h, t: qT[half_of(h), h // 2, t * P:(t + 1) * P],
               causal_bias, lambda h: 3e38, True, [*m_ready, m_causal], cmp_values, times_z(zT))
        begin, finish = modulated(1, col("norm_g", 8, 16), 0, 8)
        gated_out(a["nsa_w_out"], 0, s0, begin)
        if "x1" in dbg:
            Y.need(*x_mark)
            stores.append(load(dbg["x1"].rearrange("(t p) d -> p t d", p=P), x[:], "st_x1"))
        finish()
        meet()

    with ExitStack() as s1:
        w_in = a["moba_w_in"]
        qT = carve([P, NH // 2, S], s1)
        kT = carve([P, NKV, S], s1)
        v1 = carve([P, NT, NKV * HD], s1)
        bufs = [(carve([P, 6 * P], s1), carve([P, 512], s1)) for t in range(NT)]
        qbufs = [(b[0][:, 0:512], b[1]) for b in bufs]
        zT = carve([P, DC, S], s1)
        project(w_in[:, D:D + WT], WT, kv_tile_use(kT, v1, row("moba_k_norm"), bufs))
        for j in range(2):
            project(w_in[:, j * WT:(j + 1) * WT], WT, q_tile_use(qT, j, row("moba_q_norm"), qbufs))

        for j in range(2):
            project_cols(w_in[:, D + WT + j * WT:D + 2 * WT + j * WT], WT, z_cols(zT, j))
            if j == 0:
                m_ready = [V.last(), A.last(), G.last()]
        attend(list(range(NH)),
               [(lambda h, w: kT[half_of(h), h // GQA, 0:w],
                 lambda h, k: v1[:, k, (h // GQA) * HD:(h // GQA + 1) * HD], lambda h: h // GQA, None)],
               lambda h, t: qT[half_of(h), h // 2, t * P:(t + 1) * P],
               causal_bias, lambda h: 3e38, True, m_ready, lambda t: None, times_z(zT))
        begin, finish = modulated(2, col("norm1_g_2"), 0, 8)
        gated_out(a["moba_w_out"], 1, s1, begin)
        if "x2" in dbg:
            Y.need(*x_mark)
            stores.append(load(dbg["x2"].rearrange("(t p) d -> p t d", p=P), x[:], "st_x2"))
        finish()
        meet()

    with ExitStack() as s2:
        w_in = a["w_in_2"]
        bias_a = carve([P, HA, 3 * P], s2)
        bias_b = carve([P, NT, HB, S], s2)
        qT = carve([P, NH // 2, S], s2)
        kaT = carve([P, KVA, S], s2)
        kbT = carve([P, HB // 2, S], s2)
        va = carve([P, NT, KVA * HD], s2)
        vb = carve([P, NT, HB * HD], s2)
        squares = carve([P, DC, P], s2)
        nsink = carve([P, HA], s2)
        wa, wk = HA * HD, KVA * HD

        def q_use(first):
            def use(i, ps, m):
                A.need(m)
                return A.did(ac.activation(qT[:, first + i, :], ps, ACT.Copy, scale=HD ** -0.5))
            return use

        project_cols(w_in[:, 0:wa], wa, q_use(0))
        m_ba = load(bias_a[:], a["bias_a"], "ld_ba", ac)

        def ka_use(i, ps, m):
            V.need(m)
            for g in range(KVA):
                for dup in range(2):
                    mm = V.did(ve.tensor_copy(kaT[dup * HD:(dup + 1) * HD, g, :], ps[g * HD:(g + 1) * HD, :]))
            return mm

        kv_w, *kv_rest = stream(w_in[:, wa:wa + 2 * wk], DC, 2 * wk)
        project_cols(None, wk, ka_use, (kv_w[:, :, 0:wk], *kv_rest))

        def v_use(dst):
            def use(t, ps, m):
                V.need(m)
                return V.did(ve.tensor_copy(dst[:, t, :], ps))
            return use

        project(None, wk, v_use(va), (kv_w[:, :, wk:2 * wk], *kv_rest))
        at = wa + 2 * wk
        project_cols(w_in[:, at:at + WT], WT, q_use(HA // 2))
        m_bb = load(bias_b[:], a["bias_b"], "ld_bb", ac)

        def kb_use(i, ps, m):
            V.need(m)
            return V.did(ve.tensor_copy(kbT[:, i, :], ps))

        project_cols(w_in[:, at + WT:at + 2 * WT], WT, kb_use)
        project(w_in[:, at + 2 * WT:at + 3 * WT], WT, v_use(vb))
        V.need(m_rows)
        m_ns = V.did(ve.tensor_scalar(nsink[:], row("sink_a_2"), -1.0, None, ALU.mult))
        V.need(m_ns)
        m_ready = [V.last(), A.last(), G.last()]

        def bias_of(h, t, w):
            return bias_a[:, h, P * (1 - t):P * (3 - t)] if h < HA else bias_b[:, t, h - HA, :]

        norm_cols = cols[:, COL_AT["out_norm_a_2"][0]:COL_AT["out_norm_b_2"][1]]
        rstds = carve([P, NT, 2], s2)
        squares_read = [None]

        def normed(t, m):
            A.need(m, squares_read[0])
            V.need(m)
            for half in range(2):
                bank, cs = banks[6 + half].t[:].rearrange("p (c q) -> p c q", c=4), slice(4 * half, 4 * half + 4)
                m_s = A.did(ac.activation(squares[:, cs, :], bank, ACT.Square))
                V.need(m_s)
                for c in range(4):
                    mv = V.did(ve.tensor_scalar(hT[:, 4 * half + c, t * P:(t + 1) * P], bank[:, c, :],
                                                norm_cols[:, 4 * half + c:4 * half + c + 1], None, ALU.mult))
                banks[6 + half].free = mv
            oz_mark[t] = [banks[6].free, banks[7].free]

            def sum_squares():
                b = spare_bank()
                T.need(b.free, m_s, m_ones)
                for half in range(2):
                    for c in range(4):
                        last = pe.matmul(b.t[:, half:half + 1], squares[:, 4 * half + c, :], ones[:, 0:1], start=c == 0,
                                         stop=c == 3)
                squares_read[0] = T.did(last)
                V.need(squares_read[0])
                b.free = V.did(ve.tensor_scalar(rstds[:, t, :], b.t[:, 0:2], 1.0 / (HA * HD), EPS, ALU.mult, ALU.add))
                G.need(b.free, m_pow)
                V.need(G.did(po.tensor_tensor(rstds[:, t, :], rstds[:, t, :], pow_half[:, 0:2], ALU.pow)))

            later.append(sum_squares)
            return oz_mark[t]

        attend(list(range(NH)),
               [(lambda h, w: kaT[half_of(h), h // (HA // KVA), 0:w] if h < HA else kbT[half_of(h), (h - HA) // 2, 0:w],
                 lambda h, k: va[:, k, (h // 4) * HD:(h // 4 + 1) * HD] if h < HA else vb[:, k, (h - HA) * HD:(h - HA + 1) * HD],
                 lambda h: h // 4 if h < HA else h, None)],
               lambda h, t: qT[half_of(h), h // 2, t * P:(t + 1) * P],
               bias_of, lambda h: nsink[:, h:h + 1] if h < HA else 3e38, False, [*m_ready, m_ba, m_bb], lambda t: None,
               normed, sink=row("sink_a_2"))
        run_later()
        begin, finish = modulated(2, col("norm2_g_2"), 24, 32)
        gated_out(a["w_out_2"], 2, s2, begin, lambda t, half: rstds[:, t, half:half + 1])
        assert not fillers
        if "x3" in dbg:
            Y.need(*x_mark)
            stores.append(load(dbg["x3"].rearrange("(t p) d -> p t d", p=P), x[:], "st_x3"))
        finish()
        run_later()
        meet()

    split = {}
    for name in ("u", "v"):
        split[name] = [[sb(f"{name}_{part}{k}", [P, D], F32R) for k in range(2)] for part in ("hi", "lo")]
    raw = {name: [raw_all[:, 2 * n + k, :] for k in range(2)] for n, name in enumerate(("u", "v"))}
    h_hi, h_lo = sb("h_hi", [P, DC, S], F32R), sb("h_lo", [P, DC, S], F32R)
    a_hi, a_lo = ([sb(f"a_{part}{k}", [P, S], F32R) for k in range(2)] for part in ("hi", "lo"))

    def new_sem(name):
        return st.enter_context(nc.semaphore(name))

    s_load = {(n, k): new_sem(f"s_load_{n}{k}") for n in ("u", "v") for k in range(2)}
    s_uhi, s_ulo, s_vhi, s_vlo, s_z, s_gelu, s_a, s_out = (
        new_sem(n) for n in ("s_uhi", "s_ulo", "s_vhi", "s_vlo", "s_z", "s_gelu", "s_a", "s_out"))
    for e, s in ((ac, s_uhi), (po, s_ulo), (ac, s_vhi), (ve, s_vlo), (pe, s_z), (ac, s_gelu), (ve, s_a), (pe, s_out)):
        e.sem_inc(s, 2)
    mat = arena[:, 0:PK * S].rearrange("p (e t) -> p e t", e=PK)
    zbank, outb = banks[0:2], banks[4:8]

    def at(i, k):
        return i * 2 + k

    def load_block(name, i, k, s_split):
        sy.wait_ge(s_split, at(i, k) + 1)
        sy.dma_start(raw[name][k], a[name][bass.ds(at(i, k), 1)].rearrange("o p n -> (o p) n")).then_inc(s_load[name, k], 16)

    def split_hi(name, i, k, s_hi, s_used, first):
        ac.wait_ge(s_load[name, k], (i - first) * 16 + 16)
        ac.wait_ge(s_used, at(i, k) + 1)
        ac.activation(split[name][0][k][:], raw[name][k], ACT.Copy).then_inc(s_hi, 1)

    def split_lo(eng, name, i, k, s_hi, s_lo):
        eng.wait_ge(s_hi, at(i, k) + 3)
        eng.tensor_tensor(split[name][1][k][:], raw[name][k], split[name][0][k][:].bitcast(F32), ALU.subtract).then_inc(s_lo, 1)

    def z_product(b, slot):
        pe.wait_ge(s_ulo, b + 3)
        pe.wait_ge(s_gelu, b + 1)
        k = slot % 2
        u_hi, u_lo = (quad[slot][x].rearrange("p (c e) -> p c e", c=DC) for x in range(2))
        n = 0
        for c in range(DC):
            for u, h in ((u_hi, h_hi), (u_hi, h_lo), (u_lo, h_hi)):
                last = pe.matmul(zbank[k].t[:, 0:S], u[:, c, :], h[:, c, :], start=n == 0, stop=n == 3 * DC - 1)
                n += 1
        last.then_inc(s_z, 1)

    def out_product(i, k, start=False, stop=False, kept=False):
        pe.wait_ge(s_vlo, at(i, k) + 3)
        if kept:
            pe.wait_ge(s_vlo_g, at(i, k) + 3)
        pe.wait_ge(s_a, at(i, k) + 3)
        for t in range(NT):
            for n, (x, y) in enumerate(((a_hi, 0), (a_hi, 1), (a_lo, 0))):
                for h in range(2):
                    last = pe.matmul(outb[2 * t + h].t[:], x[k][:, t * P:(t + 1) * P],
                                     split["v"][y][k][:, h * 512:(h + 1) * 512], start=start and n == 0,
                                     stop=stop and n == 2, skip_group_check=True)
        last.then_inc(s_out, 1)

    def split_a(i, k, src, link):
        ve.wait_ge(s_out, at(i, k) + 1)
        ve.tensor_copy(a_hi[k][:], src).then_inc(link, 1)
        return lambda n: (ve.wait_ge(link, n), ve.tensor_tensor(a_lo[k][:], src, a_hi[k][:].bitcast(F32), ALU.subtract).then_inc(s_a, 1))

    def block_of(i, k):
        return mat[:, bass.ds(at(i, k), 1), :].rearrange("p o t -> p (o t)")

    quad = [(split[n][0][k][:], split[n][1][k][:]) for n in ("u", "v") for k in range(2)]
    s_quad = [new_sem(f"s_load_quad{k}") for k in range(4)]

    def quad_load(b, slot):
        if not isinstance(b, int):
            sy.wait_ge(s_ulo, b - 1)
        sy.dma_start(raw_all[:, slot, :], a["u"][bass.ds(b, 1)].rearrange("o p n -> (o p) n")).then_inc(s_quad[slot], 16)

    def quad_split(b, turn, slot):
        ac.wait_ge(s_quad[slot], turn * 16 + 16)
        if not isinstance(b, int):
            ac.wait_ge(s_z, b - 1)
        ac.activation(quad[slot][0], raw_all[:, slot, :], ACT.Copy).then_inc(s_uhi, 1)
        po.wait_ge(s_uhi, b + 3)
        po.tensor_tensor(quad[slot][1], raw_all[:, slot, :], quad[slot][0].bitcast(F32), ALU.subtract).then_inc(s_ulo, 1)

    def u_load(i, k):
        load_block("u", i, k, s_ulo)

    def u_split(i, k):
        split_hi("u", i, k, s_uhi, s_z, KEEP // 2 + 1)
        split_lo(po, "u", i, k, s_uhi, s_ulo)

    def v_split(i, k):
        load_block("v", i, k, s_vlo)
        split_hi("v", i, k, s_vhi, s_out, KEEP // 2)
        split_lo(ve, "v", i, k, s_vhi, s_vlo)

    s_vhalf, s_vlo_g = new_sem("s_vhalf"), new_sem("s_vlo_g")
    s_load_kept = [new_sem(f"s_load_vkept{k}") for k in range(2)]
    po.sem_inc(s_vlo_g, 2)

    def kept_v(i, k):
        sy.wait_ge(s_vlo, at(i, k) + 1)
        sy.wait_ge(s_vlo_g, at(i, k) + 1)
        sy.dma_start(raw["v"][k], a["v"][bass.ds(at(i, k), 1)].rearrange("o p n -> (o p) n")).then_inc(s_load_kept[k], 16)
        ac.wait_ge(s_load_kept[k], i * 16 + 16)
        ac.wait_ge(s_out, at(i, k) + 1)
        for h in range(2):
            cs = slice(512 * h, 512 * h + 512)
            ac.activation(split["v"][0][k][:, cs], raw["v"][k][:, cs], ACT.Copy).then_inc(s_vhalf, 1)
        for h, (e, done) in enumerate(((po, s_vlo_g), (ve, s_vlo))):
            cs = slice(512 * h, 512 * h + 512)
            e.wait_ge(s_vhalf, at(i, k) * 2 + 1 + h)
            e.tensor_tensor(split["v"][1][k][:, cs], raw["v"][k][:, cs], split["v"][0][k][:, cs].bitcast(F32),
                            ALU.subtract).then_inc(done, 1)

    def after(i, k):
        return (i, 1) if k == 0 else (i + 1, 0)

    with ExitStack() as s3:
        V.need(*[m for ms in h_mark for m in ms])
        m_hh = V.did(ve.tensor_copy(h_hi[:], hT[:]))
        V.need(m_hh)
        m_hl = V.did(ve.tensor_tensor(h_lo[:], hT[:], h_hi[:].bitcast(F32), ALU.subtract))
        top[0] = max(top[0], KEEP * S)
        qsT = carve([P, 2 * PH, S], s3)
        keysT = carve([P, 2 * PH, PK], s3)
        for j in range(4):
            def use(i, ps, m, j=j):
                A.need(m)
                return A.did(ac.activation(qsT[:, 4 * j + i, :], ps, ACT.Copy))
            project_cols(a["w_query_2"][:, j * WT:(j + 1) * WT], WT, use)
            if j == 0:
                m_keys = load(keysT, a["keysT"], "ld_keys", ac)
        m_q = A.last()
        sc = carve([P, NT, 2 * PH, PK], s3)
        sc2 = carve([P, 2, PK], s3)
        top_v = carve([P, PH, 2, PTOP], s3)
        top_i = carve([P, PH, 2, PTOP], s3, U32)
        top_f = carve([P, PH, 2, PTOP], s3)
        cand, eq = (qsT[:, 8 * x:8 * x + 8, :].rearrange("p (h) (i j) -> p h i j", j=PTOP) for x in range(2))
        cand2 = carve([P, 2, PTOP * PTOP], s3)
        best = carve([P, PH, PTOP], s3)
        best_i = carve([P, PH, PTOP], s3, U32)
        rank_u = carve([P, 2, PH, PTOP], s3, U32)
        rank = carve([P, 2, PH, PTOP], s3)
        hk = carve([P, NT, 3, PH, PTOP], s3)
        weight = carve([P, NT, PH, PTOP], s3)
        gsum = carve([P, PH], s3)

        def top16(src, work, vals, idx, marks):
            V.need(V.last(), *marks)
            m = V.did(ve.max(vals[:, 0:8], src))
            V.need(m)
            V.did(ve.max_index(idx[:, 0:8], vals[:, 0:8], src))
            m = V.did(ve.match_replace(work, vals[:, 0:8], src, -3.4e38))
            V.need(m)
            m = V.did(ve.max(vals[:, 8:16], work))
            V.need(m)
            return V.did(ve.max_index(idx[:, 8:16], vals[:, 8:16], work))

        Y.need(slot_free[0])
        for k in range(4):
            quad_load(k, k)
            quad_split(k, 0, k)

        m_sc = {}
        for t in range(NT):
            for q in range(4):
                b = banks[2 + q % 2]
                T.need(b.free, m_q, m_keys)
                for i in range(4):
                    hh = 4 * q + i
                    last = pe.matmul(b.t[:, i * PK:(i + 1) * PK], qsT[:, hh, t * P:(t + 1) * P], keysT[:, hh, :],
                                     start=True, stop=True)
                m = m_scored = T.did(last)
                A.need(m, V.last())
                b.free = m_sc[t, q] = A.did(ac.activation(sc[:, t, 4 * q:4 * q + 4, :],
                                                          b.t[:].rearrange("p (i n) -> p i n", i=4), ACT.Copy))

        for e in (T, Y, A, G):
            e.need(m_hl, T.last(), A.last())
        def kept_block(i, k, ahead):
            b = i * 4 + k
            z_product(b, k)
            ac.wait_ge(s_z, b + 3)
            ac.activation(mat[:, bass.ds(b, 1), :].rearrange("p o t -> p (o t)"), zbank[k % 2].t[:, 0:S],
                          ACT.Gelu_apprx_tanh).then_inc(s_gelu, 1)
            if ahead:
                if isinstance(b, int):
                    sy.wait_ge(s_ulo, b + 3)
                    ac.wait_ge(s_z, b + 3)
                quad_load(b + 4, k)
                quad_split(b + 4, i + 1, k)

        with nc.Fori(0, KEEP // 4 - 1, engines=(mybir.EngineType.SP, mybir.EngineType.Activation, mybir.EngineType.Pool,
                                                mybir.EngineType.PE)) as i:
            for k in range(4):
                kept_block(i, k, True)
        for k in range(4):
            kept_block(KEEP // 4 - 1, k, k < 2)

        for t in range(NT):
            for hh in range(2 * PH):
                m = top16(sc[:, t, hh, :], sc2[:, hh % 2, :], top_v[:, hh // 2, hh % 2, :], top_i[:, hh // 2, hh % 2, :],
                          [m_sc[t, hh // 4]])
            V.need(m)
            m = V.did(ve.tensor_copy(top_f, top_i))
            V.need(m, m_scored)
            m = V.did(ve.tensor_tensor(cand, top_v[:, :, 0, :].unsqueeze(3).broadcast_to([P, PH, PTOP, PTOP]),
                                       top_v[:, :, 1, :].unsqueeze(2).broadcast_to([P, PH, PTOP, PTOP]), ALU.add))
            for h in range(PH):
                m = top16(cand[:, h].rearrange("p i j -> p (i j)"), cand2[:, h % 2, :], best[:, h, :], best_i[:, h, :], [m])
            V.need(m)
            V.did(ve.tensor_scalar(rank_u[:, 0], best_i, 4, None, ALU.logical_shift_right))
            m = V.did(ve.tensor_scalar(rank_u[:, 1], best_i, 15, None, ALU.bitwise_and))
            V.need(m)
            m = V.did(ve.tensor_copy(rank, rank_u))
            for side in range(2):
                V.need(m, m_iota)
                m = V.did(ve.tensor_tensor(eq, rank[:, side].unsqueeze(3).broadcast_to([P, PH, PTOP, PTOP]),
                                           iota_k[:, 0:PTOP].unsqueeze(1).unsqueeze(1).broadcast_to([P, PH, PTOP, PTOP]),
                                           ALU.is_equal))
                V.need(m)
                m = V.did(ve.tensor_tensor(eq, eq, top_f[:, :, side, :].unsqueeze(2).broadcast_to([P, PH, PTOP, PTOP]),
                                           ALU.mult))
                V.need(m)
                m = V.did(ve.tensor_reduce(hk[:, t, side], eq, AX, ALU.add))
            V.need(m)
            m = V.did(ve.tensor_tensor(weight[:, t], best, best[:, :, 0:1].broadcast_to([P, PH, PTOP]), ALU.subtract))
        A.need(m)
        m = A.did(ac.activation(weight, weight, ACT.Exp))
        for t in range(NT):
            V.need(m, V.last())
            mm = V.did(ve.tensor_reduce(gsum, weight[:, t], AX, ALU.add))
            V.need(mm)
            mm = V.did(ve.reciprocal(gsum, gsum))
            V.need(mm)
            mm = V.did(ve.tensor_tensor(hk[:, t, 2], weight[:, t], gsum.unsqueeze(2).broadcast_to([P, PH, PTOP]), ALU.mult))
            b = banks[2 + t]
            T.need(mm, b.free)
            for i in range(3):
                last = pe.transpose(b.t[:, i * P:(i + 1) * P], hk[:, t, i].rearrange("p h k -> p (h k)"), ident[:])
            mm = T.did(last)
            V.need(mm)
            b.free = V.did(ve.tensor_copy(hkT[:, :, t * P:(t + 1) * P], b.t[:, 0:3 * P].rearrange("p (i n) -> p i n", i=3)))
        if "hk" in dbg:
            Y.need(V.last())
            stores.append(load(dbg["hk"], hkT[:], "st_hk"))
        meet()
    meet(with_loads=True)
    layers.close()

    n_quad = S // TOK // 4
    s_oh, s_ohg, s_gm, s_gc, s_gx = (new_sem(n) for n in ("s_onehot", "s_onehot_g", "s_gatemm", "s_gatecopy", "s_gatemul"))
    raw_oh = raw_all[:].rearrange("p (k x) (j n) -> p k x j n", k=2, n=P)
    nq = TOK // 4
    for e, s, n in ((ve, s_oh, 8), (po, s_ohg, 4), (pe, s_gm, 4 * nq), (ac, s_gc, 4 * nq), (ve, s_gx, 4 * nq)):
        e.sem_inc(s, n)
    iota_w = iota_k[:].unsqueeze(1).broadcast_to([P, TOK, P])
    for e in (ve, ac, po):
        e.wait_ge(s_gelu, KEEP + 2)
        e.wait_ge(s_ulo, KEEP + 4)

    def one_hots(i, k):
        g = i * 4 + k

        def tokens(side):
            return hkT[:, side, bass.ds(g * TOK, TOK)].unsqueeze(2).broadcast_to([P, TOK, P])

        ve.wait_ge(s_gm, (g + 3) * nq)
        ve.tensor_tensor(raw_oh[:, k % 2, 1], iota_w, tokens(1), ALU.is_equal).then_inc(s_oh, 1)
        po.wait_ge(s_oh, g * 2 + 9)
        po.tensor_tensor(raw_oh[:, k % 2, 1], raw_oh[:, k % 2, 1], tokens(2), ALU.mult).then_inc(s_ohg, 1)
        ve.tensor_tensor(raw_oh[:, k % 2, 0], iota_w, tokens(0), ALU.is_equal).then_inc(s_oh, 1)

    def gate_group(i, k):
        g = i * 4 + k
        one_hots(i, k)
        pe.wait_ge(s_oh, g * 2 + 10)
        pe.wait_ge(s_ohg, g + 5)
        pe.wait_ge(s_gx, (g + 1) * nq)
        for q in range(nq):
            for j in range(4):
                last = pe.matmul(banks[nq * k + q].t[:, j * P:(j + 1) * P], raw_oh[:, k % 2, 0, 4 * q + j, :],
                                 raw_oh[:, k % 2, 1, 4 * q + j, :], start=True, stop=True)
            last.then_inc(s_gm, 1)
        for q in range(nq):
            ac.wait_ge(s_gm, (g + 4) * nq + q + 1)
            ac.activation(mat[:, KEEP:PK, bass.ds(g * TOK + 4 * q, 4)],
                          banks[nq * k + q].t[:].rearrange("p (k e) -> p e k", k=4)[:, KEEP:PK, :],
                          ACT.Copy).then_inc(s_gc, 1)

    def multiply(i, k):
        g = i * 4 + k
        for q in range(nq):
            ve.wait_ge(s_gc, (g + 4) * nq + q + 1)
            dst = mat[:, 0:KEEP, bass.ds(g * TOK + 4 * q, 4)]
            ve.tensor_tensor(dst, banks[nq * k + q].t[:].rearrange("p (k e) -> p e k", k=4)[:, 0:KEEP, :], dst,
                             ALU.mult).then_inc(s_gx, 1)

    gate_group(0, 0)
    gate_group(0, 1)
    for k in (2, 3):
        gate_group(0, k)
        multiply(0, k - 2)
    with nc.Fori(1, n_quad) as i:
        for k in range(4):
            gate_group(i, k)
            multiply(i if k >= 2 else i - 1, (k - 2) % 4)
    multiply(n_quad - 1, 2)
    multiply(n_quad - 1, 3)
    total = (S // TOK + 4) * nq
    for e in (ve, ac, pe, po, sy):
        e.wait_ge(s_gx, total)

    s_link = new_sem("s_link")
    ve.sem_inc(s_link, 2)

    def kept_a(i, k):
        split_a(i, k, block_of(i, k), s_link)(at(i, k) + 3)

    kept_v(0, 0)
    kept_a(0, 0)
    kept_a(0, 1)
    kept_v(0, 1)
    out_product(0, 0, start=True, kept=True)
    with nc.Fori(0, KEEP // 2 - 1) as i:
        kept_a(i + 1, 0)
        kept_v(i + 1, 0)
        out_product(i, 1, kept=True)
        kept_a(i + 1, 1)
        kept_v(i + 1, 1)
        out_product(i + 1, 0, kept=True)
    last_kept = (KEEP // 2 - 1, 1)
    ac.sem_inc(s_vhi, KEEP)
    sy.wait_ge(s_vlo_g, KEEP + 2)
    v_split(KEEP // 2, 0)
    z_product(KEEP, 0)
    out_product(*last_kept, kept=True)

    zg = [hkT[:, k, :] for k in range(2)]
    s_mul = new_sem("s_mul")
    ve.sem_inc(s_mul, 2)

    def rest_block(i, k, ahead=2, stop=False):
        ac.wait_ge(s_z, at(i, k) + 3)
        ac.wait_ge(s_a, at(i, k) + 1)
        ac.activation(zg[k], zbank[k].t[:, 0:S], ACT.Gelu_apprx_tanh).then_inc(s_gelu, 1)
        ve.wait_ge(s_gelu, at(i, k) + 3)
        ve.tensor_tensor(zg[k], zg[k], block_of(i, k), ALU.mult).then_inc(s_mul, 1)
        if ahead >= 2:
            u_load(i + 1, k)
            u_split(i + 1, k)
        ve.wait_ge(s_mul, at(i, k) - KEEP + 3)
        split_a(i, k, zg[k], s_link)(at(i, k) + 3)
        if ahead >= 1:
            v_split(*after(i, k))
            z_product(at(i, k) + 1, 1 - k)
        out_product(i, k, stop=stop)

    with nc.Fori(KEEP // 2, PK // 2 - 1) as i:
        rest_block(i, 0)
        rest_block(i, 1)
    rest_block(PK // 2 - 1, 0, ahead=1)
    rest_block(PK // 2 - 1, 1, ahead=0, stop=True)

    for e in (ve, ac, pe):
        e.wait_ge(s_out, PK + 2)
    tmp = arena[:, 0:D]
    sy.wait_ge(s_ulo, PK + 2)
    final_g = raw_all[:, 0, :]
    m_fg = load(final_g, a["final_g"].broadcast_to([P, D]), "ld_final_g")
    V.need(*[m for m in (A.last(),) if m])
    for t in range(NT):
        V.need(V.last())
        for h in range(2):
            m = V.did(ve.tensor_tensor(tmp[:, h * 512:(h + 1) * 512], outb[2 * t + h].t[:],
                                       gate_row[1][:, h * 512:(h + 1) * 512], ALU.mult))
        V.need(m)
        m = V.did(ve.tensor_tensor(x[:, t, :], x[:, t, :], tmp, ALU.add))
        m = row_rstd(stat[:, t:t + 1], x[:, t, :], D, [m], tmp)
        V.need(m, m_fg)
        m = V.did(ve.scalar_tensor_tensor(out=x[:, t, :], in0=x[:, t, :], scalar=stat[:, t:t + 1],
                                          in1=final_g, op0=ALU.mult, op1=ALU.mult))
        Y.need(m)
        stores.append(load(a["out"].rearrange("(t p) d -> t p d", p=P)[t], x[:, t, :], f"st_out{t}"))
    for m in stores:
        sy.wait_ge(*m)


def t5_buckets(rel):
    half, exact = 16, 8
    n = np.abs(rel)
    nf = np.maximum(n, 1).astype(np.float32)
    large = exact + (np.log(nf / np.float32(exact)) / np.float32(np.log(128 / exact)) * np.float32(half - exact)).astype(np.int32)
    return np.where(rel > 0, half, 0) + np.where(n < exact, n, np.minimum(large, half - 1))


DEBUG = {}


def kernel(**inputs):
    import numpy as _np
    import concourse.bacc as _bacc
    from concourse import mybir as _mybir
    from concourse.bass_utils import run_bass_kernel_spmd as _run

    f = {k: _np.asarray(v) for k, v in inputs.items()}
    arrays = {}
    arrays["cols"] = _np.concatenate([f[n].reshape(-1, P) for n, _ in COLS]).T
    arrays["rows"] = _np.concatenate([f[n].reshape(-1) for n, _ in ROWS])[None, :]
    pos = f["positions"][0]
    cpos = pos[_np.minimum(_np.arange(CPAD) * CMP_STRIDE + CMP_LEN - 1, S - 1)]
    arrays["pos"] = _np.stack([pos[:P], pos[P:], _np.tile(cpos, NKV)], axis=1)
    arrays["x"] = f["x"][0]
    arrays["ada_w"] = f["ada_w"]
    arrays["w_ada_2"] = f["w_ada_2"][0]
    for n in ("nsa_w_in", "nsa_w_out", "moba_w_in", "moba_w_out", "w_in_2", "w_out_2", "w_query_2", "nsa_cmp_w1", "nsa_cmp_w2"):
        arrays[n] = f[n][0]
    arrays["cmp_pe"] = f["nsa_cmp_pe"][0].reshape(2, NPAIR, P).transpose(2, 0, 1)
    rel = _np.arange(3 * P)[None, :] - P - _np.arange(P)[:, None]
    seen = _np.abs(rel) <= P
    table = f["t5_table_2"][t5_buckets(rel)]
    arrays["bias_a"] = _np.where(seen[:, :, None], table, _np.float32(NEG)).transpose(0, 2, 1)
    tok = _np.arange(S)
    rr, cc = tok // 64, tok % 64
    start = _np.clip(cc - 8, 0, 64 - 16)
    row_off = rr[None, :] - rr[:, None] + 7
    col_off = cc[None, :] - cc[:, None] + 15
    inside = (cc[None, :] >= start[:, None]) & (cc[None, :] < start[:, None] + 16)
    rpb = f["rpb_b_2"][0][:, row_off, _np.clip(col_off, 0, 30)]
    bb = _np.where(inside[None], rpb, _np.float32(NEG))
    arrays["bias_b"] = bb.reshape(HB, NT, P, S).transpose(2, 1, 0, 3)
    arrays["keysT"] = f["sub_keys_2"][0].reshape(2 * PH, PK, P).transpose(2, 0, 1)
    arrays["u"] = f["u_experts_2"][0].reshape(PK, PK, DC, P).transpose(1, 3, 2, 0).reshape(PK, P, D)
    arrays["v"] = f["v_experts_2"][0].reshape(PK, PK, D).transpose(1, 0, 2)
    arrays["final_g"] = f["final_g_2"][None, :]
    arrays["ada_b"] = f["ada_b"]
    arrays["b_ada_2"] = f["b_ada_2"]
    arrays = {k: _np.ascontiguousarray(v) for k, v in arrays.items()}

    nc = _bacc.Bacc("TRN2", target_bir_lowering=False, num_devices=1, dynamic_dma_scratch_size=1024)
    aps = {k: nc.dram_tensor(f"in_{k}", v.shape, _mybir.dt.from_np(v.dtype), kind="ExternalInput").ap()
           for k, v in arrays.items()}
    aps["out"] = nc.dram_tensor("out", (S, D), F32, kind="ExternalOutput").ap()
    dbg = {k: nc.dram_tensor(f"dbg_{k}", s, F32, kind="ExternalOutput").ap() for k, s in DEBUG.items()}
    program(nc, aps, dbg)
    r = _run(nc, [{f"in_{k}": v for k, v in arrays.items()}], core_ids=[0])
    return r.results[0]["out"][None]
```
